# Optimizing a Trainium2 kernel written in Bass

```python
import functools
import jax, jax.numpy as jnp
from jax import lax
import numpy as np

D_MODEL = 1024
BATCH = 1
SEQ = 1024
DEPTH = 1
DEC_BATCH = 8
DEC_SEQ = 16
PAST_LEN = 256

CHUNK = 64
MIX_W = D_MODEL // 2
HEAD_DIM = 64
LRU_BLOCKS = MIX_W // HEAD_DIM
LRU_BD = MIX_W // LRU_BLOCKS
LRU_CONV = 4
LRU_C = 8.0
SWA_HEADS = MIX_W // HEAD_DIM
SWA_KV = max(1, SWA_HEADS // 4)
WINDOW = 128
WINDOW_CHUNKS = WINDOW // CHUNK
RWKV_HEADS = MIX_W // HEAD_DIM
RWKV_HD = HEAD_DIM
W_LORA = 64
A_LORA = 64
G_LORA = 128
RWKV_COLS = 3 * MIX_W + W_LORA + A_LORA + G_LORA
RWKV_SPLITS = [MIX_W, 2 * MIX_W, 3 * MIX_W, 3 * MIX_W + W_LORA, 3 * MIX_W + W_LORA + A_LORA]
N_BRANCH = 3
SWA_COLS = (SWA_HEADS + 2 * SWA_KV) * HEAD_DIM
IN_COLS = 2 * MIX_W + SWA_COLS + RWKV_COLS + N_BRANCH * D_MODEL
IN_SPLITS = [MIX_W, 2 * MIX_W, 2 * MIX_W + SWA_COLS, 2 * MIX_W + SWA_COLS + RWKV_COLS]
N_MEM = 256
X_HEADS = 4
X_HD = D_MODEL // X_HEADS
D_FF = 11 * D_MODEL // 4
FFN_CONV = 3
RMS_EPS = 1e-6
GN_EPS = 64e-5
NEG = -1e30

kernel_name = 'hybrid_lru_swa_rwkv7_stream_step'

def rmsnorm(x, g):
    xf = x.astype(jnp.float32)
    y = xf * lax.rsqrt(jnp.mean(xf * xf, axis=-1, keepdims=True) + RMS_EPS)
    return (y * g.astype(jnp.float32)).astype(x.dtype)

def causal_dwconv(x, buf, w):
    T = x.shape[1]
    K = w.shape[0]
    xp = jnp.concatenate([buf.astype(x.dtype), x], axis=1)
    y = sum(xp[:, k:k + T] * w[k] for k in range(K))
    return y, xp[:, T:]

def linear_recurrence(a, b, h0):
    def comb(l, r):
        return l[0] * r[0], r[0] * l[1] + r[1]
    a_c, b_c = lax.associative_scan(comb, (a, b), axis=1)
    h = a_c * h0[:, None] + b_c
    return h, h[:, -1]

def rg_lru(xc, h0, gate_w, gate_b, lam):
    B, T, _ = xc.shape
    f32 = jnp.float32
    xb = xc.reshape(B, T, LRU_BLOCKS, LRU_BD)
    gates = jnp.einsum('btnd,gnde->gbtne', xb, gate_w).reshape(2, B, T, MIX_W) + gate_b[:, None, None]
    r = jax.nn.sigmoid(gates[0].astype(f32))
    i = jax.nn.sigmoid(gates[1].astype(f32))
    log_a = LRU_C * r * jax.nn.log_sigmoid(lam.astype(f32))
    a = jnp.exp(log_a)
    mult = jnp.sqrt(-jnp.expm1(2.0 * log_a))
    h, h_last = linear_recurrence(a, mult * i * xc.astype(f32), h0.astype(f32))
    return h.astype(xc.dtype), h_last.astype(h0.dtype)

def rwkv_scan(r, decay, k, v, a_in, b_in, S0):
    def step(S, inp):
        r_t, w_t, k_t, v_t, a_t, b_t = inp
        Sa = jnp.einsum('bhvk,bhk->bhv', S, a_t)
        S = S * w_t[:, :, None, :] + Sa[..., None] * b_t[:, :, None, :] + v_t[..., None] * k_t[:, :, None, :]
        return S, jnp.einsum('bhvk,bhk->bhv', S, r_t)
    xs = tuple(jnp.moveaxis(t, 1, 0) for t in (r, decay, k, v, a_in, b_in))
    S, o = lax.scan(step, S0, xs)
    return jnp.moveaxis(o, 0, 1), S

def rwkv_mix(z, shift, S0, mu, w0, w2, a0, a2, g2, k_k, k_a, r_k, ln_w, ln_b):
    B, T, _ = z.shape
    f32 = jnp.float32
    z_prev = jnp.concatenate([shift.astype(z.dtype), z[:, :-1]], axis=1)
    zs = z + (z_prev - z) * mu
    r, k, v, wl, al, gl = jnp.split(zs, RWKV_SPLITS, axis=-1)
    w_log = -jax.nn.softplus(-(w0 + jnp.tanh(wl) @ w2).astype(f32)) - 0.5
    decay = jnp.exp(-jnp.exp(w_log))
    a = jax.nn.sigmoid((a0 + al @ a2).astype(f32))
    g = jax.nn.sigmoid(gl) @ g2
    hs = lambda t: t.reshape(B, T, RWKV_HEADS, RWKV_HD)
    kf = k.astype(f32)
    kk = hs(kf * k_k)
    kk = kk / jnp.maximum(jnp.sqrt(jnp.sum(kk * kk, axis=-1, keepdims=True)), 1e-12)
    kh = hs(kf * (1.0 + (a - 1.0) * k_a))
    rf = hs(r.astype(f32))
    vh = hs(v.astype(f32))
    o, S = rwkv_scan(rf, hs(decay), kh, vh, -kk, kk * hs(a), S0.astype(f32))
    mean = jnp.mean(o, axis=-1, keepdims=True)
    var = jnp.mean(jnp.square(o - mean), axis=-1, keepdims=True)
    o = ((o - mean) * lax.rsqrt(var + GN_EPS)).reshape(B, T, MIX_W) * ln_w + ln_b
    bonus = jnp.sum(rf * kh * r_k, axis=-1, keepdims=True) * vh
    o = (o + bonus.reshape(B, T, MIX_W)) * g
    return o.astype(z.dtype), z[:, -1:], S.astype(S0.dtype)

def sink_softmax(s, sink):
    sink_col = jnp.broadcast_to(sink.astype(jnp.float32), s.shape[:-1] + (1,))
    return jax.nn.softmax(jnp.concatenate([s, sink_col], axis=-1), axis=-1)[..., :-1]

def swa_prompt(q, k, v, sink):
    B, T, H, hd = q.shape
    G = H // SWA_KV
    nC = T // CHUNK
    qc = q.reshape(B, nC, CHUNK, SWA_KV, G, hd)
    kc = k.reshape(B, nC, CHUNK, SWA_KV, hd)
    vc = v.reshape(B, nC, CHUNK, SWA_KV, hd)
    shifts = list(range(WINDOW_CHUNKS - 1, -1, -1))
    def band(t):
        return jnp.concatenate([jnp.pad(t, ((0, 0), (j, 0), (0, 0), (0, 0), (0, 0)))[:, :nC] for j in shifts], axis=2)
    kb, vb = band(kc), band(vc)
    src = jnp.arange(nC)[:, None] - jnp.array(shifts)[None, :]
    valid = jnp.repeat(src >= 0, CHUNK, axis=1)
    s = jnp.einsum('bnqkgd,bnskd->bnkgqs', qc, kb).astype(jnp.float32) * (hd ** -0.5)
    s = jnp.where(valid[None, :, None, None, None, :], s, NEG)
    p = sink_softmax(s, sink.reshape(SWA_KV, G)[None, None, :, :, None, None])
    o = jnp.einsum('bnkgqs,bnskd->bnqkgd', p.astype(v.dtype), vb)
    return o.reshape(B, T, H * hd)

def swa_prompt_attend(q, k, v, sink):
    return swa_prompt(q, k, v, sink), k[:, -WINDOW:], v[:, -WINDOW:]

def swa_step(q, k, v, sink, k_cache, v_cache):
    B, S, H, hd = q.shape
    G = H // SWA_KV
    W = k_cache.shape[1]
    kf = jnp.concatenate([k_cache.astype(k.dtype), k], axis=1)
    vf = jnp.concatenate([v_cache.astype(v.dtype), v], axis=1)
    q_pos = PAST_LEN + jnp.arange(S)
    k_pos = jnp.concatenate([PAST_LEN - W + jnp.arange(W), q_pos])
    qch = q_pos // CHUNK
    kch = k_pos // CHUNK
    valid = (kch[None, :] <= qch[:, None]) & (kch[None, :] > qch[:, None] - WINDOW_CHUNKS)
    s = jnp.einsum('bqkgd,bskd->bkgqs', q.reshape(B, S, SWA_KV, G, hd), kf).astype(jnp.float32) * (hd ** -0.5)
    s = jnp.where(valid, s, NEG)
    p = sink_softmax(s, sink.reshape(SWA_KV, G)[None, :, :, None, None])
    o = jnp.einsum('bkgqs,bskd->bqkgd', p.astype(v.dtype), vf).reshape(B, S, H * hd)
    return o, kf[:, -W:], vf[:, -W:]

def mem_kv(mem, g, w_mem_kv):
    B, M, _ = mem.shape
    k, v = jnp.split(rmsnorm(mem, g) @ w_mem_kv, 2, axis=-1)
    return k.reshape(B, M, X_HEADS, X_HD), v.reshape(B, M, X_HEADS, X_HD)

def cross_attn(xn, mk, mv, w_xq, w_xo):
    B, T, _ = xn.shape
    q = (xn @ w_xq).reshape(B, T, X_HEADS, X_HD)
    s = jnp.einsum('bthd,bmhd->bhtm', q, mk.astype(q.dtype)).astype(jnp.float32) * (X_HD ** -0.5)
    p = jax.nn.softmax(s, axis=-1).astype(q.dtype)
    o = jnp.einsum('bhtm,bmhd->bthd', p, mv.astype(q.dtype)).reshape(B, T, D_MODEL)
    return o @ w_xo

def conv_ffn(xn, w_up, conv_w, w_down, buf):
    u, buf_new = causal_dwconv(xn @ w_up, buf, conv_w)
    gate, val = jnp.split(u, 2, axis=-1)
    return (jax.nn.gelu(gate) * val) @ w_down, buf_new

def setup_inputs(seed: int = 0) -> dict:
    key = jax.random.key(seed)
    ks = iter(jax.random.split(key, 64))
    f32 = jnp.float32
    def nrm(shape, scale=1.0):
        return jax.random.normal(next(ks), shape, f32) * scale
    def unif(shape, lo, hi):
        return jax.random.uniform(next(ks), shape, f32, lo, hi)
    W = min(WINDOW, PAST_LEN)
    u = unif((DEPTH, MIX_W), 0.9, 0.999)
    return {
        'x_prompt': nrm((BATCH, SEQ, D_MODEL)),
        'x_sample': nrm((DEC_BATCH, DEC_SEQ, D_MODEL)),
        'mem_prompt': nrm((BATCH, N_MEM, D_MODEL)),
        'state_lru_conv': nrm((DEPTH, DEC_BATCH, LRU_CONV - 1, MIX_W)),
        'state_lru_h': nrm((DEPTH, DEC_BATCH, MIX_W), 0.5),
        'cache_swa_k': nrm((DEPTH, DEC_BATCH, W, SWA_KV, HEAD_DIM)),
        'cache_swa_v': nrm((DEPTH, DEC_BATCH, W, SWA_KV, HEAD_DIM)),
        'state_rwkv_shift': nrm((DEPTH, DEC_BATCH, 1, RWKV_COLS)),
        'state_rwkv': nrm((DEPTH, DEC_BATCH, RWKV_HEADS, RWKV_HD, RWKV_HD), 0.2),
        'cache_mem_k': nrm((DEPTH, DEC_BATCH, N_MEM, X_HEADS, X_HD)),
        'cache_mem_v': nrm((DEPTH, DEC_BATCH, N_MEM, X_HEADS, X_HD)),
        'state_ffn_conv': nrm((DEPTH, DEC_BATCH, FFN_CONV - 1, 2 * D_FF)),
        'norm_mix': 1.0 + nrm((DEPTH, D_MODEL), 0.02),
        'w_in': nrm((DEPTH, D_MODEL, IN_COLS), D_MODEL ** -0.5),
        'b_gate': nrm((DEPTH, N_BRANCH, D_MODEL), 0.02),
        'lru_conv_w': nrm((DEPTH, LRU_CONV, MIX_W), LRU_CONV ** -0.5),
        'lru_conv_b': nrm((DEPTH, MIX_W), 0.02),
        'lru_gate_w': nrm((DEPTH, 2, LRU_BLOCKS, LRU_BD, LRU_BD), LRU_BD ** -0.5),
        'lru_gate_b': nrm((DEPTH, 2, MIX_W), 0.02),
        'lru_lambda': jnp.log(u) - jnp.log1p(-u),
        'swa_sink': nrm((DEPTH, SWA_HEADS), 0.5),
        'rwkv_mu': unif((DEPTH, RWKV_COLS), 0.0, 1.0),
        'rwkv_w0': unif((DEPTH, MIX_W), -6.0, 1.0),
        'rwkv_w2': nrm((DEPTH, W_LORA, MIX_W), 0.5 * W_LORA ** -0.5),
        'rwkv_a0': nrm((DEPTH, MIX_W), 0.1),
        'rwkv_a2': nrm((DEPTH, A_LORA, MIX_W), 0.5 * A_LORA ** -0.5),
        'rwkv_g2': nrm((DEPTH, G_LORA, MIX_W), G_LORA ** -0.5),
        'rwkv_k_k': 0.85 + nrm((DEPTH, MIX_W), 0.05),
        'rwkv_k_a': 1.0 + nrm((DEPTH, MIX_W), 0.05),
        'rwkv_r_k': nrm((DEPTH, RWKV_HEADS, RWKV_HD), 0.1),
        'rwkv_ln_w': 1.0 + nrm((DEPTH, MIX_W), 0.02),
        'rwkv_ln_b': nrm((DEPTH, MIX_W), 0.02),
        'w_branch': nrm((DEPTH, N_BRANCH, MIX_W, D_MODEL), MIX_W ** -0.5),
        'w_out': nrm((DEPTH, D_MODEL, D_MODEL), 0.5 * D_MODEL ** -0.5),
        'norm_x': 1.0 + nrm((DEPTH, D_MODEL), 0.02),
        'norm_mem': 1.0 + nrm((DEPTH, D_MODEL), 0.02),
        'w_xq': nrm((DEPTH, D_MODEL, D_MODEL), D_MODEL ** -0.5),
        'w_mem_kv': nrm((DEPTH, D_MODEL, 2 * D_MODEL), D_MODEL ** -0.5),
        'w_xo': nrm((DEPTH, D_MODEL, D_MODEL), 0.5 * D_MODEL ** -0.5),
        'norm_ffn': 1.0 + nrm((DEPTH, D_MODEL), 0.02),
        'w_up': nrm((DEPTH, D_MODEL, 2 * D_FF), D_MODEL ** -0.5),
        'ffn_conv_w': nrm((DEPTH, FFN_CONV, 2 * D_FF), FFN_CONV ** -0.5),
        'w_down': nrm((DEPTH, D_FF, D_MODEL), 0.5 * D_FF ** -0.5),
        'norm_final': 1.0 + nrm((D_MODEL,), 0.02),
    }

def reference(x_prompt, x_sample, mem_prompt,
              state_lru_conv, state_lru_h, cache_swa_k, cache_swa_v, state_rwkv_shift, state_rwkv,
              cache_mem_k, cache_mem_v, state_ffn_conv,
              norm_mix, w_in, b_gate, lru_conv_w, lru_conv_b, lru_gate_w, lru_gate_b, lru_lambda,
              swa_sink, rwkv_mu, rwkv_w0, rwkv_w2, rwkv_a0, rwkv_a2, rwkv_g2, rwkv_k_k, rwkv_k_a, rwkv_r_k,
              rwkv_ln_w, rwkv_ln_b, w_branch, w_out, norm_x, norm_mem, w_xq, w_mem_kv, w_xo,
              norm_ffn, w_up, ffn_conv_w, w_down, norm_final):
    f32 = jnp.float32
    Bp = x_prompt.shape[0]
    dt = x_prompt.dtype
    hp, hs = x_prompt, x_sample
    P = [[] for _ in range(9)]
    Q = [[] for _ in range(7)]
    for l in range(DEPTH):
        def run(x, lru_buf, lru_h, shift, S, ffn_buf, attend, mk, mv):
            Bx, T, _ = x.shape
            xn = rmsnorm(x, norm_mix[l])
            lru_x, lru_y, swa_p, rw, gl = jnp.split(xn @ w_in[l], IN_SPLITS, axis=-1)
            xc, lru_buf = causal_dwconv(lru_x, lru_buf, lru_conv_w[l])
            hA, lru_h = rg_lru(xc + lru_conv_b[l], lru_h, lru_gate_w[l], lru_gate_b[l], lru_lambda[l])
            oA = hA * jax.nn.gelu(lru_y)
            q, k, v = jnp.split(swa_p, [SWA_HEADS * HEAD_DIM, (SWA_HEADS + SWA_KV) * HEAD_DIM], axis=-1)
            oB, kb, vb = attend(q.reshape(Bx, T, SWA_HEADS, HEAD_DIM), k.reshape(Bx, T, SWA_KV, HEAD_DIM),
                                v.reshape(Bx, T, SWA_KV, HEAD_DIM), swa_sink[l])
            oC, shift, S = rwkv_mix(rw, shift, S, rwkv_mu[l], rwkv_w0[l], rwkv_w2[l], rwkv_a0[l], rwkv_a2[l],
                                    rwkv_g2[l], rwkv_k_k[l], rwkv_k_a[l], rwkv_r_k[l], rwkv_ln_w[l], rwkv_ln_b[l])
            gates = jax.nn.sigmoid(gl.reshape(Bx, T, N_BRANCH, D_MODEL) + b_gate[l])
            merged = sum(gates[:, :, n] * (o @ w_branch[l, n]) for n, o in enumerate((oA, oB, oC)))
            x = x + merged @ w_out[l]
            x = x + cross_attn(rmsnorm(x, norm_x[l]), mk, mv, w_xq[l], w_xo[l])
            f, ffn_buf = conv_ffn(rmsnorm(x, norm_ffn[l]), w_up[l], ffn_conv_w[l], w_down[l], ffn_buf)
            return x + f, (lru_buf, lru_h, kb, vb, shift, S, ffn_buf)

        mk_p, mv_p = mem_kv(mem_prompt, norm_mem[l], w_mem_kv[l])
        hp, st_p = run(hp, jnp.zeros((Bp, LRU_CONV - 1, MIX_W), dt), jnp.zeros((Bp, MIX_W), dt),
                       jnp.zeros((Bp, 1, RWKV_COLS), dt), jnp.zeros((Bp, RWKV_HEADS, RWKV_HD, RWKV_HD), f32),
                       jnp.zeros((Bp, FFN_CONV - 1, 2 * D_FF), dt), swa_prompt_attend, mk_p, mv_p)
        step_attend = functools.partial(swa_step, k_cache=cache_swa_k[l], v_cache=cache_swa_v[l])
        hs, st_s = run(hs, state_lru_conv[l], state_lru_h[l], state_rwkv_shift[l], state_rwkv[l],
                       state_ffn_conv[l], step_attend, cache_mem_k[l], cache_mem_v[l])
        for i, a in enumerate(st_p + (mk_p, mv_p)):
            P[i].append(a)
        for i, a in enumerate(st_s):
            Q[i].append(a)

    y_prompt = rmsnorm(hp, norm_final)
    y_sample = rmsnorm(hs, norm_final)
    p_lru_conv, p_lru_h, p_swa_k, p_swa_v, p_rwkv_shift, p_rwkv, p_ffn_conv, p_mem_k, p_mem_v = [jnp.stack(a) for a in P]
    s_lru_conv, s_lru_h, s_swa_k, s_swa_v, s_rwkv_shift, s_rwkv, s_ffn_conv = [jnp.stack(a) for a in Q]
    return (y_prompt, y_sample,
            p_lru_conv, p_lru_h, p_swa_k, p_swa_v, p_rwkv_shift, p_rwkv, p_ffn_conv, p_mem_k, p_mem_v,
            s_lru_conv, s_lru_h, s_swa_k, s_swa_v, s_rwkv_shift, s_rwkv, s_ffn_conv)


_drawn_inputs = setup_inputs


def setup_inputs(seed=0):
    import zlib

    import numpy as np

    out = dict(_drawn_inputs(seed))
    spreads = {}
    factors = {'b_gate': 8.0,
     'lru_gate_b': 6.006,
     'swa_sink': 8.0,
     'rwkv_ln_w': 8.0,
     'rwkv_ln_b': 8.0,
     'norm_x': 8.0,
     'norm_mem': 2.96,
     'norm_ffn': 2.754,
     'norm_final': 2.825}
    for name, (base, spread) in spreads.items():
        noise = np.random.default_rng([zlib.crc32(name.encode()), seed]).standard_normal(out[name].shape)
        drawn = base * np.exp(spread * noise) if base else spread * noise
        out[name] = __import__('jax').numpy.asarray(drawn.astype(out[name].dtype))
    for name, factor in factors.items():
        out[name] = (out[name] * factor).astype(out[name].dtype)
    return out
```

```python
from contextlib import ExitStack

import numpy as np

import concourse.bass as bass
from concourse import mybir

F32 = mybir.dt.float32
F32R = mybir.dt.float32r
ALU = mybir.AluOpType
ACT = mybir.ActivationFunctionType
AX = mybir.AxisListType

P = 128
D = 1024
KD = D // P
SEQ = 1024
NB, NS = 8, 16
T = SEQ + NB * NS
TC = 384
NTC = T // TC
TT = T // P
MIX = 512
KM = MIX // P
NH, HD = 8, 64
CH = 64
NCH = SEQ // CH
FF = 2816
KF = FF // P
NMEM = 256
XH, XHD = 4, 256
EPS = 1e-6
GN_EPS = 64e-5
DEC = float(np.exp(-0.5))

Z_LX, Z_LY, Z_Q, Z_K, Z_V, Z_RW, Z_G, Z_N = 0, 4, 8, 12, 13, 14, 28, 52
NRW = Z_G - Z_RW

VEC = [("norm_mix", 8), ("b_gate", 24), ("lru_conv_w", 16), ("lru_conv_b", 4), ("lru_gate_b", 8),
       ("lru_lambda", 4), ("rwkv_mu", 14), ("rwkv_w0", 4), ("rwkv_a0", 4), ("rwkv_k_k", 4),
       ("rwkv_k_a", 4), ("rwkv_r_k", 4), ("rwkv_ln_w", 4), ("rwkv_ln_b", 4), ("norm_x", 8),
       ("norm_mem", 8), ("norm_ffn", 8), ("ffn_conv_w", 132), ("norm_final", 8)]
VAT = {}
for _n, _c in VEC:
    VAT[_n] = sum(c for _, c in VEC[:len(VAT)])
NVEC = sum(c for _, c in VEC)

MASKS = ["ident", "ones", "head", "off2", "off2T", "off4", "off8", "off16", "off32", "off64",
         "upS64", "upI64", "upS16", "upI16"]


def shape_masks():
    t = np.arange(P)[:, None]
    j = np.arange(P)[None, :]
    same = lambda n: t // n == j // n
    off = lambda n: same(n) & (t % n >= n // 2) & (j % n < n // 2)
    m = {"ident": t == j, "ones": (t >= 0) & (j >= 0), "head": same(HD), "off2": off(2), "off2T": off(2).T}
    for n in (4, 8, 16, 32, 64):
        m[f"off{n}"] = off(n)
    for n in (64, 16):
        m[f"upS{n}"] = same(n) & (t < j)
        m[f"upI{n}"] = same(n) & (t <= j)
    blocks = [m[n].astype(np.float32) for n in MASKS]
    col = np.arange(KM * P)[None, :] + np.zeros((P, 1), int)
    resets = [(col % n != 0).astype(np.float32) for n in (CH, NS)]
    rows = (t // NS == np.arange(NB)[None, :]).astype(np.float32)
    return np.ascontiguousarray(np.concatenate(blocks + resets + [rows], axis=1))


MW = len(MASKS) * P + 2 * KM * P + NB


class Stage:

    def __init__(self, nc, name):
        self.nc, self.name, self.ctx, self.sems = nc, name, ExitStack(), {}

    def __enter__(self):
        self.ctx.__enter__()
        return self

    def __exit__(self, *e):
        self.nc.clear_and_free_semaphores(list(self.sems.values()))
        self.nc.all_engine_barrier()
        return self.ctx.__exit__(*e)

    def sb(self, name, shape, dt=F32):
        return self.ctx.enter_context(self.nc.sbuf_tensor(f"{self.name}_{name}", shape, dt))

    def banks(self, n=8):
        return [self.ctx.enter_context(self.nc.psum_tensor(f"{self.name}_bank{i}", [P, 512], F32)) for i in range(n)]

    def sem(self, name):
        if name not in self.sems:
            self.sems[name] = self.nc.alloc_semaphore(f"{self.name}_{name}")
        return self.sems[name]


class Product:

    def __init__(self, st, tag, kt, pairs, weights, xh, xl, banks, tc=TC, ntc=NTC, bufs=None):
        self.st, self.kt, self.pairs, self.w = st, kt, pairs, weights
        self.xh, self.xl, self.tc, self.ntc = xh, xl, tc, ntc
        self.bank = [banks[:ntc], banks[ntc:2 * ntc]]
        self.raw, self.hi, self.lo = bufs or Product.buffers(st, kt, tag)
        self.arrived = [st.sem(f"{tag}_w_arrived{s}") for s in range(2)]
        self.rounded = st.sem(f"{tag}_w_rounded")
        self.rest = st.sem(f"{tag}_w_rest")
        self.ready = st.sem(f"{tag}_product_ready")
        self.used = st.sem(f"{tag}_product_used")

    @staticmethod
    def buffers(st, kt, tag):
        return tuple([st.sb(f"{tag}_{n}{s}", [P, kt, P], dt) for s in range(2)]
                     for n, dt in (("raw", F32), ("hi", F32R), ("lo", F32R)))

    def load(self, eng):
        for s in range(2):
            eng.dma_start(self.raw[s][:, 0:self.kt], self.w(0, s)).then_inc(self.arrived[s], 16)
        with eng.Fori(1, self.pairs) as p:
            for s in range(2):
                eng.wait_ge(self.rest, p * 2 + (s - 1))
                eng.dma_start(self.raw[s][:, 0:self.kt], self.w(p, s)).then_inc(self.arrived[s], 16)

    def split_hi(self, act, p, s):
        act.wait_ge(self.arrived[s], p * 16 + 16)
        if not (isinstance(p, int) and p == 0):
            act.wait_ge(self.ready, (p * 2 + (s - 1)) * self.ntc)
        act.copy(self.hi[s][:, 0:self.kt], self.raw[s][:, 0:self.kt]).then_inc(self.rounded, 1)

    def split_lo(self, dve, p, s):
        dve.wait_ge(self.rounded, p * 2 + (s + 1))
        dve.tensor_tensor(self.lo[s][:, 0:self.kt], self.raw[s][:, 0:self.kt],
                          self.hi[s][:, 0:self.kt].bitcast(F32), ALU.subtract).then_inc(self.rest, 1)

    def pipeline(self, eng, split, evac):
        def pair(p):
            if split:
                split(eng, p, 0)
            evac(p - 1, 1)
            if split:
                split(eng, p, 1)
            evac(p, 0)
        if split:
            split(eng, 0, 0)
            split(eng, 0, 1)
        evac(0, 0)
        pair(1)
        with eng.Fori(2, self.pairs) as p:
            pair(p)
        evac(self.pairs - 1, 1)

    def products(self, pe):
        def tile(p, s, wait):
            pe.wait_ge(self.rest, p * 2 + (s + 1))
            if wait:
                pe.wait_ge(self.used, (p * 2 + (s - 1)) * self.ntc)
            passes = ((self.hi, self.xh), (self.lo, self.xh), (self.hi, self.xl))
            for k in range(self.kt):
                for n, (w, x) in enumerate(passes):
                    for c in range(self.ntc):
                        last = k == self.kt - 1 and n == 2
                        mm = pe.matmul(self.bank[s][c][:, 0:self.tc], w[s][:, k, :],
                                       x[:, k, c * self.tc:(c + 1) * self.tc], start=(k == 0 and n == 0), stop=last)
                        if last:
                            mm.then_inc(self.ready, 1)
        tile(0, 0, False)
        tile(0, 1, False)
        with pe.Fori(1, self.pairs) as p:
            tile(p, 0, True)
            tile(p, 1, True)


class Norm:

    def __init__(self, st, tag, xt, gain, xh, xl, ones, banks, tc=TC, ntc=NTC, kd=KD, bufs=None):
        self.xt, self.gain, self.xh, self.xl, self.ones, self.banks = xt, gain, xh, xl, ones, banks
        self.tc, self.ntc, self.kd = tc, ntc, kd
        self.sq, self.rs, self.xn = bufs or Norm.buffers(st, tag)
        (self.squared, self.summed, self.rooted, self.inverse, self.normed, self.rounded, self.rest) = (
            st.sem(f"{tag}_{n}") for n in ("squared", "summed", "rooted", "inverse", "normed", "rounded", "rest"))

    @staticmethod
    def buffers(st, tag):
        return st.sb(f"{tag}_sq", [P, 4, TC]), st.sb(f"{tag}_rs", [P, T]), st.sb(f"{tag}_xn", [P, 2, TC])

    def cols(self, c):
        return slice(c * self.tc, (c + 1) * self.tc)

    def scalar(self, act):
        n = 0
        for c in range(self.ntc):
            for k in range(self.kd):
                if n >= 4:
                    act.wait_ge(self.summed, n - 3)
                act.activation(self.sq[:, n % 4, 0:self.tc], self.xt[:, k, self.cols(c)], ACT.Square).then_inc(self.squared, 1)
                n += 1
        for c in range(self.ntc):
            act.wait_ge(self.summed, self.kd * (c + 1))
            act.activation(self.rs[:, self.cols(c)], self.banks[c][:, 0:self.tc], ACT.Sqrt,
                           scale=1.0 / D, bias=self.eps[:, 0:1]).then_inc(self.rooted, 1)
        if self.xh is not None:
            for i in range(self.ntc * self.kd):
                c, k = divmod(i, self.kd)
                act.wait_ge(self.normed, i + 1)
                act.copy(self.xh[:, k, self.cols(c)], self.xn[:, i % 2, 0:self.tc]).then_inc(self.rounded, 1)

    def tensor(self, pe):
        n = 0
        for c in range(self.ntc):
            for k in range(self.kd):
                pe.wait_ge(self.squared, n + 1)
                pe.matmul(self.banks[c][:, 0:self.tc], self.ones, self.sq[:, n % 4, 0:self.tc],
                          start=(k == 0), stop=(k == self.kd - 1)).then_inc(self.summed, 1)
                n += 1

    def vector(self, dve):
        for c in range(self.ntc):
            dve.wait_ge(self.rooted, c + 1)
            dve.reciprocal(self.rs[:, self.cols(c)], self.rs[:, self.cols(c)]).then_inc(self.inverse, 1)
            dve.wait_ge(self.inverse, c + 1)
            for k in range(self.kd):
                i = c * self.kd + k
                out = self.xn[:, i % 2, 0:self.tc] if self.xh is not None else self.xl[:, k, self.cols(c)]
                if self.xh is not None and i >= 2:
                    dve.wait_ge(self.rest, i - 1)
                dve.scalar_tensor_tensor(out=out, in0=self.xt[:, k, self.cols(c)], scalar=self.gain[:, k:k + 1],
                                         in1=self.rs[:, self.cols(c)], op0=ALU.mult, op1=ALU.mult).then_inc(self.normed, 1)
                if self.xh is not None and i:
                    self.remainder(dve, i - 1)
        if self.xh is not None:
            self.remainder(dve, self.ntc * self.kd - 1)

    def remainder(self, dve, i):
        c, k = divmod(i, self.kd)
        dve.wait_ge(self.rounded, i + 1)
        dve.tensor_tensor(self.xl[:, k, self.cols(c)], self.xn[:, i % 2, 0:self.tc],
                          self.xh[:, k, self.cols(c)].bitcast(F32), ALU.subtract).then_inc(self.rest, 1)


def wtile(w, kt, m0=0, k0=0):
    def at(p, s):
        return w[bass.ds(p * 2 + (m0 + s), 1), :, k0:k0 + kt, :].rearrange("o p k m -> (o p) k m")
    return at


def stage_in_projection(nc, env, io):
    with Stage(nc, "inproj") as st:
        banks = st.banks()
        xt = st.sb("xt", [P, KD, T])
        xh, xl = st.sb("xh", [P, KD, T], F32R), st.sb("xl", [P, KD, T], F32R)
        out = [st.sb(f"z{s}", [P, T]) for s in range(2)]
        x_in = [st.sem(f"x_arrived{c}") for c in range(NTC)]
        vec_in = st.sem("constants_arrived")
        eps_set = st.sem("eps_set")
        stored = [st.sem(f"z_stored{s}") for s in range(2)]
        vec, masks = env["vec"], env["masks"]
        norm = Norm(st, "norm", xt, vec[:, VAT["norm_mix"]:], xh, xl, env["mask"]("ones"), banks)
        norm.eps = env["eps"]
        prod = Product(st, "win", KD, Z_N // 2, wtile(io["w_in"], KD), xh, xl, banks)
        with nc.Block() as block:
            @block.sync
            def _(sp):
                for c in range(NTC):
                    sp.dma_start(xt[:, :, c * TC:(c + 1) * TC], io["xt"][:, :, c * TC:(c + 1) * TC]).then_inc(x_in[c], 16)
                sp.dma_start(vec[:], io["vec"]).then_inc(vec_in, 16)
                sp.dma_start(masks[:], io["masks"]).then_inc(vec_in, 16)
                prod.load(sp)

            @block.gpsimd
            def _(pool):
                pool.memset(env["eps"][:, 0:1], EPS).then_inc(eps_set, 1)
                pool.memset(env["eps"][:, 1:2], GN_EPS).then_inc(eps_set, 1)

            @block.scalar
            def _(act):
                for c in range(NTC):
                    act.wait_ge(x_in[c], 16)
                act.wait_ge(eps_set, 2)
                norm.scalar(act)

                def evac(p, s):
                    if not (isinstance(p, int) and p == 0):
                        act.wait_ge(stored[s], p * 16)
                    for c in range(NTC):
                        act.wait_ge(prod.ready, (p * 2 + s) * NTC + (c + 1))
                        act.copy(out[s][:, c * TC:(c + 1) * TC], prod.bank[s][c][:, 0:TC]).then_inc(prod.used, 1)
                    act.wait_ge(prod.used, (p * 2 + (s + 1)) * NTC)
                    act.dma_start(io["z"][bass.ds(p * 2 + s, 1)].rearrange("o p t -> (o p) t"), out[s][:]).then_inc(stored[s], 16)
                prod.pipeline(act, prod.split_hi, evac)
                for s in range(2):
                    act.wait_ge(stored[s], 16 * prod.pairs)

            @block.vector
            def _(dve):
                dve.wait_ge(vec_in, 32)
                norm.vector(dve)
                prod.pipeline(dve, prod.split_lo, lambda p, s: None)

            @block.tensor
            def _(pe):
                pe.wait_ge(vec_in, 32)
                norm.tensor(pe)
                pe.wait_ge(norm.rest, KD * NTC)
                prod.products(pe)


def stage_lru(nc, env, io):
    with Stage(nc, "lru") as st:
        banks = st.banks()
        PAD = 3 + SEQ + NB * (3 + NS)
        xp = st.sb("x_padded", [P, KM, PAD])
        ly = st.sb("gate_branch", [P, KM, T])
        xc, r, i_, a, m = (st.sb(n, [P, KM, T]) for n in ("conv", "r", "i", "a", "m"))
        gw = st.sb("gate_w", [P, 2, KM, P])
        h0, hl = st.sb("h0", [P, KM, NB]), st.sb("h_last", [P, KM, NB + 1])
        sp = st.sb("softplus", [P, 8, KM])
        S = st.sem
        V = lambda n, c: env["vec"][:, VAT[n] + c:VAT[n] + c + 1]
        prompt = lambda x, ct, k=0: x[:, ct, k:k + SEQ]
        samples = lambda x, ct: x[:, ct, SEQ:T].rearrange("p (b s) -> p b s", b=NB)
        padded = lambda ct: xp[:, ct, 3 + SEQ:PAD].rearrange("p (b s) -> p b s", b=NB)
        zt = io["z"]
        with nc.Block() as block:
            @block.sync
            def _(eng):
                for ct in range(KM):
                    eng.dma_start(xp[:, ct, 3:3 + SEQ], zt[Z_LX + ct, :, 0:SEQ]).then_inc(S(f"x_in{ct}"), 16)
                    eng.dma_start(padded(ct)[:, :, 3:], zt[Z_LX + ct, :, SEQ:T].rearrange("p (b s) -> p b s", b=NB)).then_inc(S(f"x_in{ct}"), 16)
                    eng.dma_start(padded(ct)[:, :, 0:3], io["lru_conv"][ct]).then_inc(S(f"x_in{ct}"), 16)
                eng.dma_start(gw[:], io["lru_gate_w"]).then_inc(S("gate_w_in"), 16)
                eng.dma_start(h0[:], io["lru_h"]).then_inc(S("h0_in"), 16)
                for ct in range(KM):
                    eng.dma_start(ly[:, ct], zt[Z_LY + ct]).then_inc(S(f"y_in{ct}"), 16)
                for ct in range(KM):
                    eng.wait_ge(S(f"x_in{ct}"), 48)
                    eng.dma_start(io["o_conv_p"][ct], xp[:, ct, SEQ:SEQ + 3]).then_inc(S("stored"), 16)
                    eng.dma_start(io["o_conv_s"][ct], padded(ct)[:, :, NS:NS + 3]).then_inc(S("stored"), 16)
                for ct in range(KM):
                    eng.wait_ge(S("branch_out"), ct + 1)
                    eng.dma_start(io["branch"][0, :, ct], ly[:, ct]).then_inc(S("stored"), 16)
                eng.wait_ge(S("h_last"), 2 * KM)
                eng.dma_start(io["o_h"], hl[:]).then_inc(S("stored"), 16)
                eng.wait_ge(S("stored"), 16 * (3 * KM + 1))

            @block.gpsimd
            def _(pool):
                pool.memset(xp[:, :, 0:3], 0.0).then_inc(S("padding_zero"), 1)
                for ct in range(KM):
                    pool.wait_ge(S("scanned"), ct + 1)
                    pool.tensor_copy(hl[:, ct, 0:1], m[:, ct, SEQ - 1:SEQ]).then_inc(S("h_last"), 1)
                    pool.tensor_copy(hl[:, ct, 1:], samples(m, ct)[:, :, NS - 1]).then_inc(S("h_last"), 1)

            @block.scalar
            def _(act):
                lam = env["vec"][:, VAT["lru_lambda"]:VAT["lru_lambda"] + KM]
                act.activation(sp[:, 0], lam, ACT.Abs).then_inc(S("abs"), 1)
                act.wait_ge(S("abs"), 1)
                act.activation(sp[:, 1], sp[:, 0], ACT.Exp, scale=-1.0).then_inc(S("e"), 1)
                act.wait_ge(S("w"), 1)
                act.activation(sp[:, 3], sp[:, 2], ACT.Ln).then_inc(S("ln"), 1)
                for ct in range(KM):
                    for g, dst in ((0, r), (1, i_)):
                        for c in range(NTC):
                            n = (ct * 2 + g) * NTC + c
                            act.wait_ge(S("gated"), n + 1)
                            act.activation(dst[:, ct, c * TC:(c + 1) * TC], banks[n % 6][:, 0:TC], ACT.Sigmoid,
                                           bias=V("lru_gate_b", g * KM + ct)).then_inc(S("gate"), 1)
                act.wait_ge(S("rate"), 1)
                act.wait_ge(S("gate"), 6 * KM)
                for ct in range(KM):
                    act.activation(a[:, ct], r[:, ct], ACT.Exp, scale=sp[:, 6, ct:ct + 1]).then_inc(S("a"), 1)
                    act.activation(m[:, ct], r[:, ct], ACT.Tanh, scale=sp[:, 5, ct:ct + 1]).then_inc(S("tanh"), 1)
                for ct in range(KM):
                    act.wait_ge(S("square"), ct + 1)
                    act.activation(r[:, ct], m[:, ct], ACT.Sqrt).then_inc(S("mult"), 1)
                for ct in range(KM):
                    act.wait_ge(S(f"y_in{ct}"), 16)
                    act.activation(ly[:, ct], ly[:, ct], ACT.Gelu_apprx_tanh).then_inc(S("gelu"), 1)

            @block.tensor
            def _(pe):
                pe.wait_ge(S("gate_w_in"), 16)
                for ct in range(KM):
                    pe.wait_ge(S("conv"), 2 * (ct + 1))
                    for g in range(2):
                        for c in range(NTC):
                            n = (ct * 2 + g) * NTC + c
                            if n >= 6:
                                pe.wait_ge(S("gate"), n - 5)
                            pe.matmul(banks[n % 6][:, 0:TC], gw[:, g, ct], xc[:, ct, c * TC:(c + 1) * TC],
                                      start=True, stop=True).then_inc(S("gated"), 1)

            @block.vector
            def _(dve):
                steps = [0]

                def link(ins):
                    steps[0] += 1
                    ins.then_inc(S("dve_step"), 1)
                    dve.wait_ge(S("dve_step"), steps[0])
                lam = env["vec"][:, VAT["lru_lambda"]:VAT["lru_lambda"] + KM]
                dve.wait_ge(S("e"), 1)
                dve.tensor_scalar(sp[:, 2], sp[:, 1], 1.0, None, ALU.add).then_inc(S("w"), 1)
                dve.wait_ge(S("w"), 1)
                link(dve.tensor_scalar(sp[:, 4], sp[:, 2], -1.0, None, ALU.add))
                link(dve.tensor_tensor(sp[:, 4], sp[:, 1], sp[:, 4], ALU.subtract))
                link(dve.reciprocal(sp[:, 5], sp[:, 2]))
                link(dve.tensor_tensor(sp[:, 4], sp[:, 4], sp[:, 5], ALU.mult))
                dve.wait_ge(S("ln"), 1)
                link(dve.tensor_tensor(sp[:, 4], sp[:, 4], sp[:, 3], ALU.add))
                link(dve.tensor_scalar(sp[:, 5], lam, -1.0, 0.0, ALU.mult, ALU.max))
                link(dve.tensor_tensor(sp[:, 4], sp[:, 4], sp[:, 5], ALU.add))
                link(dve.tensor_scalar(sp[:, 5], sp[:, 4], 8.0, None, ALU.mult))
                dve.tensor_scalar(sp[:, 6], sp[:, 4], -8.0, None, ALU.mult).then_inc(S("rate"), 1)
                dve.wait_ge(S("padding_zero"), 1)
                for ct in range(KM):
                    dve.wait_ge(S(f"x_in{ct}"), 48)
                    w = lambda k: V("lru_conv_w", k * KM + ct)
                    srcs = (lambda k: xp[:, ct, k:k + SEQ], lambda k: padded(ct)[:, :, k:k + NS])
                    for src, dst in zip(srcs, (prompt(xc, ct), samples(xc, ct))):
                        link(dve.tensor_scalar(dst, src(0), w(0), V("lru_conv_b", ct), ALU.mult, ALU.add))
                        link(dve.scalar_tensor_tensor(out=dst, in0=src(1), scalar=w(1), in1=dst, op0=ALU.mult, op1=ALU.add))
                        link(dve.scalar_tensor_tensor(out=dst, in0=src(2), scalar=w(2), in1=dst, op0=ALU.mult, op1=ALU.add))
                        dve.scalar_tensor_tensor(out=dst, in0=src(3), scalar=w(3), in1=dst, op0=ALU.mult, op1=ALU.add).then_inc(S("conv"), 1)
                for ct in range(KM):
                    dve.wait_ge(S("tanh"), ct + 1)
                    link(dve.tensor_scalar(r[:, ct], m[:, ct], 1.0, None, ALU.add))
                    link(dve.reciprocal(r[:, ct], r[:, ct]))
                    dve.scalar_tensor_tensor(out=m[:, ct], in0=m[:, ct], scalar=2.0, in1=r[:, ct],
                                             op0=ALU.mult, op1=ALU.mult).then_inc(S("square"), 1)
                dve.wait_ge(S("h0_in"), 16)
                for ct in range(KM):
                    link(dve.tensor_tensor(xc[:, ct], xc[:, ct], i_[:, ct], ALU.mult))
                    dve.wait_ge(S("mult"), ct + 1)
                    link(dve.tensor_tensor(xc[:, ct], xc[:, ct], r[:, ct], ALU.mult))
                    dve.wait_ge(S("a"), ct + 1)
                    link(dve.tensor_tensor(h0[:, ct], h0[:, ct], samples(a, ct)[:, :, 0], ALU.mult))
                    link(dve.tensor_tensor(samples(xc, ct)[:, :, 0], samples(xc, ct)[:, :, 0], h0[:, ct], ALU.add))
                    link(dve.memset(samples(a, ct)[:, :, 0], 0.0))
                    dve.tensor_tensor_scan(m[:, ct], a[:, ct], xc[:, ct], 0.0, ALU.mult, ALU.add).then_inc(S("scanned"), 1)
                    dve.wait_ge(S("scanned"), ct + 1)
                    dve.wait_ge(S("gelu"), ct + 1)
                    dve.tensor_tensor(ly[:, ct], ly[:, ct], m[:, ct], ALU.mult).then_inc(S("branch_out"), 1)


def stage_swa(nc, env, io):
    with Stage(nc, "swa") as st:
        banks = st.banks()
        q = st.sb("q", [P, 2, T // CH, 2, CH])
        k2 = st.sb("k", [P, 2, T])
        v = st.sb("v", [P, T])
        sink, sinkq = st.sb("sink", [P, NH]), st.sb("sink_of_row", [P, 4])
        s_ = [st.sb(f"scores{i}", [P, 4, P + 1]) for i in range(2)]
        stat = [st.sb(f"stat{i}", [P, 3, 4]) for i in range(2)]
        pt = [st.sb(f"probs_t{i}", [P, 4, P]) for i in range(2)]
        vt = [st.sb(f"v_t{i}", [P, P]) for i in range(2)]
        ob = st.sb("out", [P, 4, T])
        NK = NS + CH
        kc = st.sb("k_sample", [P, 2, NB, NK])
        vc = st.sb("v_sample", [NK, NB, P])
        qm = st.sb("q_masked", [P, 4, NB, P])
        ss = st.sb("scores_sample", [P, NH, NK + 1])
        sst = st.sb("stat_sample", [P, 3, NH])
        pts = st.sb("probs_t_sample", [NK, NH, P])
        S = st.sem
        ident = env["mask"]("ident")
        SC = HD ** -0.5
        zt = io["z"]
        units = [(g, b) for g in range(2) for b in range(2)]
        with nc.Block() as block:
            @block.sync
            def _(eng):
                for ct in range(4):
                    eng.dma_start(q[:, ct // 2, :, ct % 2], zt[Z_Q + ct].rearrange("p (c t) -> p c t", t=CH)).then_inc(S("qkv_in"), 16)
                eng.dma_start(k2[:, 0], zt[Z_K]).then_inc(S("qkv_in"), 16)
                for b in range(2):
                    eng.dma_start(k2[64 * b:64 * b + 64, 1], zt[Z_K, 64 - 64 * b:128 - 64 * b]).then_inc(S("qkv_in"), 16)
                eng.dma_start(v[:], zt[Z_V]).then_inc(S("qkv_in"), 16)
                eng.dma_start(sink[:], io["sink"].broadcast_to([P, NH])).then_inc(S("qkv_in"), 16)
                eng.dma_start(kc[:, :, :, NS:NK], io["swa_k"]).then_inc(S("cache_in"), 16)
                eng.dma_start(vc[NS:NK], io["swa_v"]).then_inc(S("cache_in"), 16)
                eng.dma_start(io["o_swa_kept"], io["swa_cache"]).then_inc(S("stored"), 16)
                eng.wait_ge(S("qkv_in"), 16 * 9)
                eng.dma_start(io["o_swa_new"][0], k2[:, 0, SEQ - P:T]).then_inc(S("stored"), 16)
                eng.dma_start(io["o_swa_new"][1], v[:, SEQ - P:T]).then_inc(S("stored"), 16)
                eng.wait_ge(S("attended"), NCH)
                eng.wait_ge(S("sample_out"), 2)
                eng.dma_start(io["branch"][1], ob[:]).then_inc(S("stored"), 16)
                eng.wait_ge(S("stored"), 16 * 4)

            @block.gpsimd
            def _(pool):
                pool.memset(qm[:], 0.0).then_inc(S("q_zero"), 1)
                pool.wait_ge(S("q_zero"), 1)
                pool.wait_ge(S("qkv_in"), 16 * 9)
                for b in range(NB):
                    at = b * NS % CH
                    pool.tensor_copy(qm[:, :, b, b * NS:(b + 1) * NS].rearrange("p (g n) t -> p g n t", g=2),
                                     q[:, :, NCH + b * NS // CH, :, at:at + NS]).then_inc(S("q_masked"), 1)
                for n in range(2):
                    pool.tensor_copy(kc[:, n, :, 0:NS], k2[:, n, SEQ:T].rearrange("p (b s) -> p b s", b=NB)).then_inc(S("k_new"), 1)

            @block.tensor
            def _(pe):
                pe.wait_ge(S("qkv_in"), 16 * 9)
                for c in range(NCH):
                    lo, nk = max(c - 1, 0) * CH, CH * min(c + 1, 2)
                    bs = banks[0:2]
                    if c:
                        pe.wait_ge(S("scored"), 2 * c)
                    for g, b in units:
                        kk = k2[64 * b:64 * b + 64, 0 if b == g else 1, lo:lo + nk]
                        qq = q[64 * b:64 * b + 64, g, c].rearrange("p n t -> p (n t)")
                        mm = pe.matmul(bs[b][:, g * P:g * P + nk], qq, kk, start=True, stop=True, skip_group_check=True)
                    mm.then_inc(S("scores"), 1)
                    if c >= 1:
                        pe.wait_ge(S("v_turned_copied"), c)
                    pe.transpose(banks[2][0:nk, 0:P], v[:, lo:lo + nk], ident).then_inc(S("v_turned"), 1)
                    pe.wait_ge(S("probs"), c + 1)
                    if c:
                        pe.wait_ge(S("probs_t"), c)
                    for n in range(4):
                        mm = pe.transpose(banks[3][0:nk, n * P:(n + 1) * P], s_[c % 2][:, n, 0:nk], ident)
                    mm.then_inc(S("probs_turned"), 1)
                    pe.wait_ge(S("probs_t"), c + 1)
                    pe.wait_ge(S("v_turned_copied"), c + 1)
                    if c:
                        pe.wait_ge(S("attended"), c)
                    for n, (g, b) in enumerate(units):
                        mm = pe.matmul(banks[4 + g][64 * b:64 * b + 64, 0:P], vt[c % 2][0:nk, g * HD:(g + 1) * HD],
                                       pt[c % 2][0:nk, n, :], start=True, stop=True, skip_group_check=True)
                    mm.then_inc(S("weighted"), 1)
                pe.wait_ge(S("q_masked"), NB)
                pe.wait_ge(S("k_new"), 2)
                pe.wait_ge(S("cache_in"), 32)
                for h in range(NH):
                    g, b = h // 4, h % 2
                    for s in range(NB):
                        mm = pe.matmul(banks[6 + b][:, (h // 2) * NK:(h // 2 + 1) * NK], qm[64 * b:64 * b + 64, h // 2, s, :],
                                       kc[64 * b:64 * b + 64, 0 if b == g else 1, s, :], start=(s == 0), stop=(s == NB - 1),
                                       skip_group_check=True)
                mm.then_inc(S("scores_sample"), 1)
                pe.wait_ge(S("v_turned_copied"), NCH)
                for s in range(NB):
                    if s:
                        pe.wait_ge(S("v_sample_copied"), s)
                    pe.transpose(banks[2][0:NS, 0:P], v[:, SEQ + s * NS:SEQ + (s + 1) * NS], ident).then_inc(S("v_sample_turned"), 1)
                pe.wait_ge(S("probs_sample"), 1)
                for n in range(2):
                    pe.wait_ge(S("probs_t_sample") if n else S("probs_t"), n or NCH)
                    for h in range(4 * n, 4 * n + 4):
                        mm = pe.transpose(banks[3][0:NK, (h % 4) * P:(h % 4 + 1) * P], ss[:, h, 0:NK], ident)
                    mm.then_inc(S("probs_turned_sample"), 1)
                pe.wait_ge(S("probs_t_sample"), 2)
                pe.wait_ge(S("v_sample_copied"), NB)
                pe.wait_ge(S("attended"), NCH)
                for g in range(2):
                    for b in range(2):
                        for s in range(NB):
                            mm = pe.matmul(banks[4 + g][64 * b:64 * b + 64, s * 2 * NS:(s + 1) * 2 * NS], vc[:, s, g * HD:(g + 1) * HD],
                                           pts[:, 4 * g + b:4 * g + b + 3:2, s * NS:(s + 1) * NS],
                                           start=True, stop=True, skip_group_check=True)
                mm.then_inc(S("weighted_sample"), 1)

            @block.scalar
            def _(act):
                for c in range(NCH):
                    nk = CH * min(c + 1, 2)
                    act.wait_ge(S("centred"), c + 1)
                    n = nk if c == 0 else P + 1
                    act.activation(s_[c % 2][:, :, 0:n], s_[c % 2][:, :, 0:n], ACT.Exp).then_inc(S("exp"), 1)
                    if c == 0:
                        act.activation(s_[0][:, :, P:P + 1], s_[0][:, :, P:P + 1], ACT.Exp).then_inc(S("exp_sink0"), 1)
                    act.wait_ge(S("v_turned"), c + 1)
                    if c >= 2:
                        act.wait_ge(S("weighted"), c - 1)
                    act.copy(vt[c % 2][0:nk, :], banks[2][0:nk, 0:P]).then_inc(S("v_turned_copied"), 1)
                    act.wait_ge(S("probs_turned"), c + 1)
                    act.copy(pt[c % 2][0:nk], banks[3][0:nk, :].rearrange("p (n t) -> p n t", n=4)).then_inc(S("probs_t"), 1)
                act.wait_ge(S("cache_in"), 32)
                for s in range(NB):
                    act.wait_ge(S("v_sample_turned"), s + 1)
                    act.copy(vc[0:NS, s, :], banks[2][0:NS, 0:P]).then_inc(S("v_sample_copied"), 1)
                act.wait_ge(S("centred_sample"), 1)
                act.activation(ss[:], ss[:], ACT.Exp).then_inc(S("exp_sample"), 1)
                for n in range(2):
                    act.wait_ge(S("probs_turned_sample"), n + 1)
                    act.copy(pts[:, 4 * n:4 * n + 4], banks[3][0:NK, :].rearrange("p (n t) -> p n t", n=4)).then_inc(S("probs_t_sample"), 1)

            @block.vector
            def _(dve):
                steps = [0]

                def link(ins):
                    steps[0] += 1
                    ins.then_inc(S("dve_step"), 1)
                    dve.wait_ge(S("dve_step"), steps[0])
                dve.wait_ge(S("qkv_in"), 16 * 9)
                for n, (g, b) in enumerate(units):
                    for half in range(2):
                        h = 4 * g + 2 * half + b
                        link(dve.tensor_copy(sinkq[64 * half:64 * half + 64, n:n + 1], sink[64 * half:64 * half + 64, h:h + 1]))
                for c in range(NCH):
                    nk = CH * min(c + 1, 2)
                    x, z = s_[c % 2], stat[c % 2]
                    dve.wait_ge(S("scores"), c + 1)
                    if c >= 2:
                        dve.wait_ge(S("probs_turned"), c - 1)
                    for b in range(2):
                        dve.tensor_scalar(x[:, b::2, 0:nk], banks[b][:, 0:2 * P].rearrange("p (g k) -> p g k", g=2)[:, :, 0:nk],
                                          SC, None, ALU.mult).then_inc(S("scored"), 1)
                    dve.tensor_copy(x[:, :, P], sinkq[:]).then_inc(S("sink_put"), 1)
                    dve.wait_ge(S("scored"), 2 * c + 2)
                    dve.wait_ge(S("sink_put"), c + 1)
                    link(dve.tensor_reduce(z[:, 0], x[:, :, 0:nk], AX.X, ALU.max))
                    link(dve.tensor_tensor(z[:, 0], z[:, 0], sinkq[:], ALU.max))
                    m = z[:, 0].rearrange("p (n o) -> p n o", o=1)
                    if c == 0:
                        link(dve.tensor_tensor(x[:, :, P:P + 1], x[:, :, P:P + 1], m, ALU.subtract))
                        dve.tensor_tensor(x[:, :, 0:nk], x[:, :, 0:nk], m.broadcast_to([P, 4, nk]), ALU.subtract).then_inc(S("centred"), 1)
                        dve.wait_ge(S("exp_sink0"), 1)
                    else:
                        dve.tensor_tensor(x[:], x[:], m.broadcast_to([P, 4, P + 1]), ALU.subtract).then_inc(S("centred"), 1)
                    dve.wait_ge(S("exp"), c + 1)
                    link(dve.tensor_reduce(z[:, 1], x[:, :, 0:nk], AX.X, ALU.add))
                    link(dve.tensor_tensor(z[:, 1], z[:, 1], x[:, :, P], ALU.add))
                    link(dve.reciprocal(z[:, 2], z[:, 1]))
                    dve.tensor_tensor(x[:, :, 0:nk], x[:, :, 0:nk], z[:, 2].rearrange("p (n o) -> p n o", o=1).broadcast_to([P, 4, nk]),
                                      ALU.mult).then_inc(S("probs"), 1)
                    dve.wait_ge(S("weighted"), c + 1)
                    for g in range(2):
                        o = dve.tensor_copy(ob[:, 2 * g:2 * g + 2, c * CH:(c + 1) * CH],
                                            banks[4 + g][:, 0:P].rearrange("p (n t) -> p n t", n=2))
                    o.then_inc(S("attended"), 1)
                dve.wait_ge(S("scores_sample"), 1)
                for b in range(2):
                    link(dve.tensor_scalar(ss[:, b::2, 0:NK], banks[6 + b][:, 0:4 * NK].rearrange("p (n k) -> p n k", n=4), SC, None, ALU.mult))
                link(dve.tensor_copy(ss[:, :, NK], sink[:]))
                link(dve.tensor_reduce(sst[:, 0], ss[:], AX.X, ALU.max))
                up = lambda x, n: x.rearrange("p (n o) -> p n o", o=1).broadcast_to([P, NH, n])
                dve.tensor_tensor(ss[:], ss[:], up(sst[:, 0], NK + 1), ALU.subtract).then_inc(S("centred_sample"), 1)
                dve.wait_ge(S("exp_sample"), 1)
                link(dve.tensor_reduce(sst[:, 1], ss[:], AX.X, ALU.add))
                link(dve.reciprocal(sst[:, 2], sst[:, 1]))
                dve.tensor_tensor(ss[:, :, 0:NK], ss[:, :, 0:NK], up(sst[:, 2], NK), ALU.mult).then_inc(S("probs_sample"), 1)
                dve.wait_ge(S("weighted_sample"), 1)
                for g in range(2):
                    dve.tensor_copy(ob[:, 2 * g:2 * g + 2, SEQ:T].rearrange("p n (s t) -> p s n t", s=NB),
                                    banks[4 + g][:, 0:NB * 2 * NS].rearrange("p (s n t) -> p s n t", s=NB, n=2)).then_inc(S("sample_out"), 1)


def stage_rwkv(nc, env, io):
    with Stage(nc, "rwkv") as st:
        banks = st.banks()
        W4 = KM * P
        t4 = [P, KM, P]
        z = st.sb("z", [P, NRW, P + 1])
        zs = st.sb("shifted", [P, NRW, P])
        shift = st.sb("shift_state", [P, NRW, NB])
        zlast = st.sb("z_last", [P, NRW, NB + 1])
        w2a2, g2 = st.sb("w2_a2", [P, MIX]), st.sb("g2", [P, MIX])
        wl, gl = st.sb("tanh_w", [P, P]), st.sb("sig_g", [P, P])
        names = ["sw", "asig", "c", "cprev", "Pi", "kk", "sq", "B", "K", "kh", "rk"]
        (sw, asig, c_, cprev, Pi, kk, sq, B, K, kh, rk) = (st.sb(n, t4) for n in names)
        Pp, Pv, nrm = c_, cprev, sq
        AR = st.sb("AR", [P, KM, 2, P])
        Bt, Kt, Vt, Z1, X, U = (st.sb(n, [P, W4]) for n in ("B_tok", "K_tok", "V_tok", "LakV", "X", "U"))
        L, Ti, TiT, O_, Zm, MrbT, LakT, MrkT = ([st.sb(f"{n}{s}", t4) for s in range(2)]
                                               for n in ("L", "T", "TT", "O", "Z", "MrbT", "LakT", "MrkT"))
        Sbd, Stmp, Pcm = (st.sb(n, t4) for n in ("state", "state_sum", "decay_end"))
        S0bd, S0c = st.sb("state0_diag", [P, NB, KM, P]), st.sb("state0", [P, KM, NB, HD])
        X0T = Zm[0]
        Um = S0bd[:].rearrange("p b k v -> p b (k v)")
        GO, OT, BO = st.sb("gate", [P, KM, T]), st.sb("o", [P, KM, T]), st.sb("bonus", [P, KM, T])
        S = st.sem
        mask, vec = env["mask"], env["vec"]
        ident, ones, head = mask("ident"), mask("ones"), mask("head")
        vb = lambda n, k, cols=P: vec[:, VAT[n]:VAT[n] + k].rearrange("p (k o) -> p k o", o=1).broadcast_to([P, k, cols])
        mb = lambda n: mask(n).rearrange("p (o t) -> p o t", o=1).broadcast_to(t4)
        bank4 = lambda i: banks[i][:].rearrange("p (n t) -> p n t", n=KM)
        flat = lambda x: x.rearrange("p n t -> p (n t)")
        zt = io["z"]
        rows = lambda s: slice(64 * s, 64 * s + 64)

        def levels(t):
            return [n for n in (4, 8, 16, 32, 64) if n <= (CH if t < TT - 1 else NS)]
        sq_post, rs_post = ([flat(x[s][:]) for s in range(2)] for x in (Ti, TiT))
        merges = [sum(len(levels(u)) for u in range(t)) for t in range(TT + 1)]

        with nc.Block() as block:
            @block.sync
            def _(eng):
                eng.dma_start(w2a2[:], io["w2a2"]).then_inc(S("weights_in"), 16)
                eng.dma_start(g2[:], io["g2"]).then_inc(S("weights_in"), 16)
                eng.dma_start(shift[:], io["shift"]).then_inc(S("weights_in"), 16)
                eng.dma_start(S0bd[:], io["s0_diag"]).then_inc(S("weights_in"), 16)
                eng.dma_start(S0c[:], io["s0"]).then_inc(S("weights_in"), 16)
                for t in range(TT):
                    lo = t * P
                    first = 1 if t in (0, TT - 1) else 0
                    if t:
                        eng.wait_ge(S("zs"), t)
                        eng.wait_ge(S("z_last"), max(0, t - TT + 2)) if t == TT - 1 else None
                    eng.dma_start(z[:, :, first:P + 1], zt[Z_RW:Z_G, :, lo - 1 + first:lo + P].rearrange("n p t -> p n t")).then_inc(S("z_in"), 16)
                eng.wait_ge(S("z_last"), 2)
                eng.dma_start(io["o_shift"], zlast[:]).then_inc(S("stored"), 16)
                eng.wait_ge(S("state"), NCH)
                eng.dma_start(io["o_state_p"], Sbd[:]).then_inc(S("stored"), 16)
                eng.wait_ge(S("state_sample"), KM)
                eng.dma_start(io["o_state_s"], S0c[:]).then_inc(S("stored"), 16)
                for ct in range(KM):
                    eng.wait_ge(S("branch_out"), ct + 1)
                    eng.dma_start(io["branch"][2, :, ct], OT[:, ct]).then_inc(S("stored"), 16)
                eng.wait_ge(S("stored"), 16 * (3 + KM))

            @block.gpsimd
            def _(pool):
                pool.memset(z[:, :, 0:1], 0.0).then_inc(S("z_start"), 1)
                pool.memset(Sbd[:], 0.0).then_inc(S("state_zero"), 1)
                for t in range(TT):
                    pool.wait_ge(S("z_in"), 16 * (t + 1))
                    if t == TT - 2:
                        pool.tensor_copy(zlast[:, :, 0:1], z[:, :, P:P + 1]).then_inc(S("z_last"), 1)
                    if t == TT - 1:
                        pool.tensor_copy(zlast[:, :, 1:], z[:, :, NS:P + 1:NS]).then_inc(S("z_last"), 1)
                    lv = levels(t)
                    for i, n in enumerate(lv):
                        for s in range(2):
                            at = merges[t] + i
                            pool.wait_ge(S("L"), 2 * t + s + 1)
                            if at:
                                pool.wait_ge(S("Z"), 2 * (at - 1) + s + 1)
                            pool.tensor_tensor(O_[s][:], L[s][:], mb(f"off{n}"), ALU.mult).then_inc(S("O"), 1)

            @block.scalar
            def _(act):
                for t in range(TT):
                    act.wait_ge(S("zs"), t + 1)
                    if t:
                        act.wait_ge(S("lora"), t)
                    act.activation(wl[0:64, :], zs[0:64, 12, :], ACT.Tanh).then_inc(S("lora_in"), 1)
                    act.activation(gl[:], zs[:, 13, :], ACT.Sigmoid).then_inc(S("lora_in"), 1)
                    act.wait_ge(S("lora"), t + 1)
                    act.copy(GO[:, :, t * P:(t + 1) * P], bank4(2)).then_inc(S("g"), 1)
                    act.wait_ge(S("wa"), 2 * t + 2)
                    act.activation(sw[:], sw[:], ACT.Sigmoid).then_inc(S("sw"), 1)
                    act.activation(asig[:], asig[:], ACT.Sigmoid).then_inc(S("asig"), 1)
                    act.wait_ge(S("kk"), t + 1)
                    act.activation(sq[:], kk[:], ACT.Square).then_inc(S("sq"), 1)
                    act.wait_ge(S("cprev"), t + 1)
                    act.activation(Pi[:], c_[:], ACT.Exp, scale=DEC).then_inc(S("P"), 1)
                    act.activation(Pp[:], c_[:], ACT.Exp, scale=-DEC).then_inc(S("P"), 1)
                    act.activation(Pv[:], cprev[:], ACT.Exp, scale=-DEC).then_inc(S("P"), 1)
                    act.wait_ge(S("norm2"), t + 1)
                    act.activation(flat(nrm[:]), banks[3][:], ACT.Sqrt).then_inc(S("norm"), 1)
                    act.wait_ge(S("tok"), 3 * t + 1)
                    act.copy(Vt[:], banks[5][:]).then_inc(S("tok_copied"), 1)
                    act.wait_ge(S("tok"), 3 * t + 2)
                    act.copy(Bt[:], banks[6][:]).then_inc(S("tok_copied"), 1)
                    act.wait_ge(S("tok"), 3 * t + 3)
                    act.copy(Kt[:], banks[7][:]).then_inc(S("tok_copied"), 1)
                    for s in range(2):
                        act.wait_ge(S("grams"), 2 * t + s + 1)
                        act.copy(flat(L[s][:]), banks[0][:]).then_inc(S("L"), 1)
                    for i, n in enumerate(levels(t)):
                        for s in range(2):
                            act.wait_ge(S("Z"), 2 * (merges[t] + i) + s + 1)
                            act.copy(flat(Zm[s][:]), banks[s][:]).then_inc(S("Z_copied"), 1)
                    if t < TT - 1:
                        for c in range(2):
                            n = 2 * t + c
                            act.wait_ge(S("U"), n + 1)
                            act.copy(U[rows(c), :], banks[1][rows(c), :]).then_inc(S("U_copied"), 1)
                    else:
                        act.wait_ge(S("X0T"), 1)
                        act.copy(flat(X0T[:]), banks[3][:]).then_inc(S("X0T_copied"), 1)
                        act.wait_ge(S("U"), NCH + 1)
                        act.copy(U[:], banks[1][:]).then_inc(S("U_copied"), 1)
                for ct in range(KM):
                    for c in range(NTC):
                        n = ct * NTC + c
                        act.wait_ge(S("centred"), n + 1)
                        if n >= 2:
                            act.wait_ge(S("var"), n - 1)
                        act.activation(sq_post[n % 2][:, 0:TC], OT[:, ct, c * TC:(c + 1) * TC], ACT.Square).then_inc(S("dev2"), 1)
                        act.wait_ge(S("var"), n + 1)
                        act.activation(rs_post[n % 2][:, 0:TC], banks[4 + n % 2][:, 0:TC], ACT.Sqrt, scale=1.0 / HD,
                                       bias=env["eps"][:, 1:2]).then_inc(S("dev"), 1)

            @block.vector
            def _(dve):
                steps = [0]

                def link(ins):
                    steps[0] += 1
                    ins.then_inc(S("dve_step"), 1)
                    dve.wait_ge(S("dve_step"), steps[0])
                tt, stt = dve.tensor_tensor, dve.scalar_tensor_tensor
                dve.wait_ge(S("weights_in"), 80)
                dve.wait_ge(S("z_start"), 1)
                for t in range(TT):
                    sample = t == TT - 1
                    dve.wait_ge(S("z_in"), 16 * (t + 1))
                    link(tt(zs[:], z[:, :, 0:P], z[:, :, 1:P + 1], ALU.subtract))
                    if sample:
                        link(tt(zs[:, :, 0:P:NS], shift[:], z[:, :, 1:P + 1:NS], ALU.subtract))
                    link(tt(zs[:], zs[:], vb("rwkv_mu", NRW), ALU.mult))
                    tt(zs[:], zs[:], z[:, :, 1:P + 1], ALU.add).then_inc(S("zs"), 1)
                    dve.wait_ge(S("zs"), t + 1)
                    r, k, v = (zs[:, 4 * i:4 * i + 4] for i in range(3))
                    tt(kk[:], k, vb("rwkv_k_k", KM), ALU.mult).then_inc(S("kk"), 1)
                    link(tt(rk[:], r, vb("rwkv_r_k", KM), ALU.mult))
                    dve.wait_ge(S("lora"), t + 1)
                    tt(sw[:], bank4(0), vb("rwkv_w0", KM), ALU.add).then_inc(S("wa"), 1)
                    tt(asig[:], bank4(1), vb("rwkv_a0", KM), ALU.add).then_inc(S("wa"), 1)
                    dve.wait_ge(S("sw"), t + 1)
                    link(dve.tensor_tensor_scan(flat(c_[:]), env["resets"][1 if sample else 0], flat(sw[:]), 0.0, ALU.mult, ALU.add))
                    tt(cprev[:], c_[:], sw[:], ALU.subtract).then_inc(S("cprev"), 1)
                    dve.wait_ge(S("asig"), t + 1)
                    link(stt(out=kh[:], in0=asig[:], scalar=-1.0, in1=vb("rwkv_k_a", KM), op0=ALU.add, op1=ALU.mult))
                    link(stt(out=kh[:], in0=kh[:], scalar=1.0, in1=k, op0=ALU.add, op1=ALU.mult))
                    tt(rk[:], rk[:], kh[:], ALU.mult).then_inc(S("rk"), 1)
                    dve.wait_ge(S("norm"), t + 1)
                    link(dve.tensor_scalar(nrm[:], nrm[:], 1e-12, None, ALU.max))
                    link(dve.reciprocal(nrm[:], nrm[:]))
                    link(tt(kk[:], kk[:], nrm[:], ALU.mult))
                    dve.wait_ge(S("P"), 3 * t + 3)
                    tt(K[:], kh[:], Pi[:], ALU.mult).then_inc(S("K"), 1)
                    tt(AR[:, :, 1, :], r, Pp[:], ALU.mult).then_inc(S("AR"), 1)
                    stt(out=AR[:, :, 0, :], in0=kk[:], scalar=-1.0, in1=Pv[:], op0=ALU.mult, op1=ALU.mult).then_inc(S("AR"), 1)
                    link(tt(kk[:], kk[:], asig[:], ALU.mult))
                    tt(B[:], kk[:], Pi[:], ALU.mult).then_inc(S("B"), 1)
                    dve.wait_ge(S("bonus"), t + 1)
                    tt(BO[:, :, t * P:(t + 1) * P], bank4(4), v, ALU.mult).then_inc(S("bonus_out"), 1)
                    up = "16" if sample else "64"
                    for s in range(2):
                        dve.wait_ge(S("grams"), 2 * t + s + 1)
                        bj = lambda i: [banks[i + n // 2][:].rearrange("p (n w t) -> p n w t", n=2, w=2) for n in (0, 2)]
                        for half, (b1, b2) in enumerate(zip(bj(1), bj(3))):
                            two = slice(2 * half, 2 * half + 2)
                            m2 = lambda n: mask(n).rearrange("p (o t) -> p o t", o=1).broadcast_to([P, 2, P])
                            tt(TiT[s][:, two], b1[:, :, 0], m2("off2T"), ALU.mult).then_inc(S("masked"), 1)
                            tt(MrbT[s][:, two], b1[:, :, 1], m2("upI" + up), ALU.mult).then_inc(S("masked"), 1)
                            tt(LakT[s][:, two], b2[:, :, 0], m2("upS" + up), ALU.mult).then_inc(S("masked"), 1)
                            tt(MrkT[s][:, two], b2[:, :, 1], m2("upI" + up), ALU.mult).then_inc(S("masked"), 1)
                        dve.wait_ge(S("L"), 2 * t + s + 1)
                        link(tt(Ti[s][:], L[s][:], mb("off2"), ALU.mult))
                        tt(Ti[s][:], Ti[s][:], mb("ident"), ALU.add).then_inc(S("T"), 1)
                        dve.wait_ge(S("masked"), 16 * t + 8 * s + 8)
                        tt(TiT[s][:], TiT[s][:], mb("ident"), ALU.add).then_inc(S("T"), 1)
                    nl = len(levels(t))
                    for i in range(nl):
                        for s in range(2):
                            at = 2 * (merges[t] + i) + s
                            dve.wait_ge(S("merged"), at + 1)
                            tt(flat(TiT[s][:]), banks[2 + s][:], flat(TiT[s][:]), ALU.add).then_inc(S("T"), 1)
                            if i < nl - 1:
                                tt(flat(Ti[s][:]), banks[4 + s][:], flat(Ti[s][:]), ALU.add).then_inc(S("T"), 1)
                    dve.wait_ge(S("Z1"), t + 1)
                    link(dve.tensor_copy(Z1[:], banks[6][:]))
                    if not sample:
                        for c in range(2):
                            n = 2 * t + c
                            dve.wait_ge(S("X"), n + 1)
                            tt(X[rows(c), :], banks[0][rows(c), :], Z1[rows(c), :], ALU.add).then_inc(S("X_added"), 1)
                            end = Pp[:, :, c * CH + CH - 1:c * CH + CH]
                            tt(Pcm[:], mb("head"), end.broadcast_to(t4), ALU.mult).then_inc(S("decay_end"), 1)
                            dve.wait_ge(S("S_update"), n + 1)
                            dve.wait_ge(S("decay_end"), n + 1)
                            if n == 0:
                                dve.wait_ge(S("state_zero"), 1)
                            link(tt(flat(Stmp[:]), banks[2][:], flat(Sbd[:]), ALU.add))
                            tt(Sbd[:], Stmp[:], Pcm[:], ALU.mult).then_inc(S("state"), 1)
                    else:
                        dve.wait_ge(S("X"), NCH + 1)
                        tt(X[:], banks[4][:], Z1[:], ALU.add).then_inc(S("X_added"), 1)
                        dve.wait_ge(S("U_copied"), NCH + 1)
                        for part, src in enumerate((U, Vt)):
                            if part:
                                dve.wait_ge(S("S_update"), NCH + 1)
                            for s in range(NB):
                                dve.tensor_scalar(Um[:, s, :], src[:], env["sample_rows"][:, s:s + 1], None, ALU.mult).then_inc(S("row_masked"), 1)
                        dve.wait_ge(S("S_update"), NCH + 2)
                        for ct in range(KM):
                            bk = banks[(0, 2, 4, 5)[ct]][:].rearrange("p (b v) -> p b v", b=NB)
                            link(tt(S0c[:, ct], S0c[:, ct], bk, ALU.add))
                            tt(S0c[:, ct], S0c[:, ct], Pp[:, ct, NS - 1:P:NS].rearrange("p (b o) -> p b o", o=1).broadcast_to([P, NB, HD]),
                               ALU.mult).then_inc(S("state_sample"), 1)
                    dve.wait_ge(S("O_sum"), t + 1)
                    dve.tensor_copy(OT[:, :, t * P:(t + 1) * P], bank4(7)).then_inc(S("o"), 1)
                dve.wait_ge(S("o"), TT)
                for ct in range(KM):
                    for c in range(NTC):
                        n = ct * NTC + c
                        cc = slice(c * TC, (c + 1) * TC)
                        o = OT[:, ct, cc]
                        V = lambda name: vec[:, VAT[name] + ct:VAT[name] + ct + 1]
                        dve.wait_ge(S("mean"), n + 1)
                        stt(out=o, in0=banks[6 + n % 2][:, 0:TC], scalar=-1.0 / HD, in1=o, op0=ALU.mult, op1=ALU.add).then_inc(S("centred"), 1)
                        dve.wait_ge(S("dev"), n + 1)
                        rs = rs_post[n % 2][:, 0:TC]
                        link(dve.reciprocal(rs, rs))
                        link(tt(o, o, rs, ALU.mult))
                        link(dve.tensor_scalar(o, o, V("rwkv_ln_w"), V("rwkv_ln_b"), ALU.mult, ALU.add))
                        link(tt(o, o, BO[:, ct, cc], ALU.add))
                        f = tt(o, o, GO[:, ct, cc], ALU.mult)
                        if c == NTC - 1:
                            f.then_inc(S("branch_out"), 1)
                        else:
                            link(f)

            @block.tensor
            def _(pe):
                pe.wait_ge(S("weights_in"), 80)
                mm_ = lambda *a, **k: pe.matmul(*a, skip_group_check=True, **k)
                for t in range(TT):
                    sample = t == TT - 1
                    zv = zs[:, 8:12]
                    pe.wait_ge(S("lora_in"), 2 * t + 2)
                    if t:
                        pe.wait_ge(S("o"), t)
                    for ct in range(KM):
                        cs = slice(ct * P, (ct + 1) * P)
                        mm_(banks[0][:, cs], w2a2[0:64, cs], wl[0:64, :], start=True, stop=True)
                        mm_(banks[1][:, cs], w2a2[64:128, cs], zs[64:128, 12, :], start=True, stop=True)
                        mm = mm_(banks[2][:, cs], g2[:, cs], gl[:], start=True, stop=True)
                    mm.then_inc(S("lora"), 1)
                    pe.wait_ge(S("sq"), t + 1)
                    mm_(banks[3][:], head, flat(sq[:]), start=True, stop=True).then_inc(S("norm2"), 1)
                    pe.wait_ge(S("rk"), t + 1)
                    mm_(banks[4][:], head, flat(rk[:]), start=True, stop=True).then_inc(S("bonus"), 1)
                    for dst, src, sig, need in ((5, zv, "tok", None), (6, B[:], "tok", "B"), (7, K[:], "tok", "K")):
                        if need:
                            pe.wait_ge(S(need), t + 1)
                        for ct in range(KM):
                            mm = pe.transpose(banks[dst][:, ct * P:(ct + 1) * P], src[:, ct, :], ident)
                        mm.then_inc(S("tok"), 1)
                    pe.wait_ge(S("AR"), 2 * t + 2)
                    pe.wait_ge(S("bonus_out"), t + 1)
                    pe.wait_ge(S("g"), t + 1)
                    pe.wait_ge(S("norm"), t + 1)
                    pe.wait_ge(S("wa"), 2 * t + 2)
                    for s in range(2):
                        if s:
                            pe.wait_ge(S("masked"), 16 * t + 8)
                            pe.wait_ge(S("L"), 2 * t + 1)
                        for p in range(KM):
                            mm_(banks[0][:, p * P:(p + 1) * P], AR[rows(s), p, 0, :], B[rows(s), p, :], start=True, stop=True)
                            w = slice((p % 2) * 2 * P, (p % 2 + 1) * 2 * P)
                            ar = AR[rows(s), p].rearrange("p w t -> p (w t)")
                            mm_(banks[1 + p // 2][:, w], B[rows(s), p, :], ar, start=True, stop=True)
                            mm = mm_(banks[3 + p // 2][:, w], K[rows(s), p, :], ar, start=True, stop=True)
                        mm.then_inc(S("grams"), 1)
                    lv = levels(t)
                    for i in range(len(lv)):
                        for s in range(2):
                            at = 2 * (merges[t] + i) + s
                            if i == 0:
                                if s == 0:
                                    pe.wait_ge(S("masked"), 16 * t + 16)
                                    pe.wait_ge(S("L"), 2 * t + 2)
                            pe.wait_ge(S("T"), tbase(levels, t) + 4 * i + 2 * s + 2)
                            pe.wait_ge(S("O"), at + 1)
                            for p in range(KM):
                                mm = mm_(banks[s][:, p * P:(p + 1) * P], O_[s][:, p, :], TiT[s][:, p, :], start=True, stop=True)
                            mm.then_inc(S("Z"), 1)
                        for s in range(2):
                            at = 2 * (merges[t] + i) + s
                            pe.wait_ge(S("Z_copied"), at + 1)
                            for p in range(KM):
                                mm = mm_(banks[2 + s][:, p * P:(p + 1) * P], Ti[s][:, p, :], Zm[s][:, p, :], start=True, stop=True)
                                if i < len(lv) - 1:
                                    mm = mm_(banks[4 + s][:, p * P:(p + 1) * P], Zm[s][:, p, :], Ti[s][:, p, :], start=True, stop=True)
                            mm.then_inc(S("merged"), 1)
                    pe.wait_ge(S("tok_copied"), 3 * t + 3)
                    for p in range(KM):
                        for s in range(2):
                            h = 2 * p + s
                            mm = mm_(banks[6][:, h * HD:(h + 1) * HD], LakT[s][:, p, :], Vt[:, h * HD:(h + 1) * HD], start=True, stop=True)
                    mm.then_inc(S("Z1"), 1)
                    pe.wait_ge(S("T"), tbase(levels, t + 1))
                    if not sample:
                        for c in range(2):
                            n = 2 * t + c
                            cc, rc = slice(c * CH, (c + 1) * CH), rows(c)
                            if n:
                                pe.wait_ge(S("state"), n)
                            else:
                                pe.wait_ge(S("state_zero"), 1)
                            for p in range(KM):
                                mm = mm_(banks[0][rc, p * P:(p + 1) * P], AR[:, p, 0, cc], Sbd[:, p, :], start=True, stop=True)
                            mm.then_inc(S("X"), 1)
                            for p in range(KM):
                                mm_(banks[7][:, p * P + c * CH:p * P + (c + 1) * CH], Sbd[:, p, :], AR[:, p, 1, cc],
                                    start=(c == 0 and p == 0), stop=False)
                            pe.wait_ge(S("X_added"), n + 1)
                            for p in range(KM):
                                for s in range(2):
                                    h = 2 * p + s
                                    hs = slice(h * HD, (h + 1) * HD)
                                    mm = mm_(banks[1][rc, hs], TiT[s][rc, p, cc], X[rc, hs], start=True, stop=True)
                            mm.then_inc(S("U"), 1)
                            pe.wait_ge(S("U_copied"), n + 1)
                            for p in range(KM):
                                ps = slice(p * P, (p + 1) * P)
                                mm_(banks[2][:, ps], Bt[rc, ps], U[rc, ps], start=True, stop=False)
                                mm = mm_(banks[2][:, ps], Kt[rc, ps], Vt[rc, ps], start=False, stop=True)
                            mm.then_inc(S("S_update"), 1)
                    else:
                        for p in range(KM):
                            for b in range(NB):
                                bc = slice(b * NS, (b + 1) * NS)
                                pc = slice(p * P + b * NS, p * P + (b + 1) * NS)
                                mm_(banks[7][:, pc], S0bd[:, b, p, :], AR[:, p, 1, bc], start=(p == 0 and b == 0), stop=False)
                                mm = mm_(banks[3][:, pc], S0bd[:, b, p, :], AR[:, p, 0, bc], start=(p == 0 and b == 0), stop=True)
                        mm.then_inc(S("X0T"), 1)
                        pe.wait_ge(S("X0T_copied"), 1)
                        for p in range(KM):
                            mm = pe.transpose(banks[4][:, p * P:(p + 1) * P], X0T[:, p, :], ident)
                        mm.then_inc(S("X"), 1)
                        pe.wait_ge(S("X_added"), NCH + 1)
                        for p in range(KM):
                            for s in range(2):
                                hs = slice((2 * p + s) * HD, (2 * p + s + 1) * HD)
                                mm = mm_(banks[1][:, hs], TiT[s][:, p, :], X[:, hs], start=True, stop=True)
                        mm.then_inc(S("U"), 1)
                        for part, tok in enumerate((Bt, Kt)):
                            pe.wait_ge(S("row_masked"), NB * (part + 1))
                            for p in range(KM):
                                for s in range(2):
                                    hs = slice((2 * p + s) * HD, (2 * p + s + 1) * HD)
                                    mm = mm_(banks[(0, 2, 4, 5)[p]][rows(s), :], tok[:, hs], Um[:, :, hs], start=(part == 0), stop=(part == 1))
                            mm.then_inc(S("S_update"), 1)
                    for p in range(KM):
                        for s in range(2):
                            hs = slice((2 * p + s) * HD, (2 * p + s + 1) * HD)
                            ps = slice(p * P, (p + 1) * P)
                            mm_(banks[7][rows(s), ps], U[:, hs], MrbT[s][:, p, :], start=False, stop=False)
                            mm = mm_(banks[7][rows(s), ps], Vt[:, hs], MrkT[s][:, p, :], start=False, stop=True)
                    mm.then_inc(S("O_sum"), 1)
                pe.wait_ge(S("o"), TT)
                pe.wait_ge(S("state_sample"), KM)
                for ct in range(KM):
                    for c in range(NTC):
                        n = ct * NTC + c
                        if n == 0:
                            mm_(banks[6][:, 0:TC], head, OT[:, 0, 0:TC], start=True, stop=True).then_inc(S("mean"), 1)
                        if n + 1 < KM * NTC:
                            m_ct, m_c = divmod(n + 1, NTC)
                            if n >= 1:
                                pe.wait_ge(S("centred"), n)
                            mm_(banks[6 + (n + 1) % 2][:, 0:TC], head, OT[:, m_ct, m_c * TC:(m_c + 1) * TC], start=True, stop=True).then_inc(S("mean"), 1)
                        pe.wait_ge(S("dev2"), n + 1)
                        if n >= 2:
                            pe.wait_ge(S("dev"), n - 1)
                        mm_(banks[4 + n % 2][:, 0:TC], head, sq_post[n % 2][:, 0:TC], start=True, stop=True).then_inc(S("var"), 1)


def tbase(levels, t):
    return sum(4 + 4 * (len(levels(u)) - 1) + 2 for u in range(t))


class StreamSplit:

    SLOTS = 3

    def __init__(self, st, tag, src, xh, xl, n, ring):
        self.src, self.xh, self.xl, self.n, self.ring = src, xh, xl, n, ring
        self.arrived = [st.sem(f"{tag}_x_arrived{s}") for s in range(self.SLOTS)]
        self.rounded, self.rest = st.sem(f"{tag}_x_rounded"), st.sem(f"{tag}_x_rest")

    def load(self, eng):
        for k in range(self.n):
            if k >= self.SLOTS:
                eng.wait_ge(self.rest, k - self.SLOTS + 1)
            eng.dma_start(self.ring[:, k % self.SLOTS], self.src(k)).then_inc(self.arrived[k % self.SLOTS], 16)

    def scalar(self, act):
        for k in range(self.n):
            act.wait_ge(self.arrived[k % self.SLOTS], 16 * (k // self.SLOTS + 1))
            act.copy(self.xh[:, k], self.ring[:, k % self.SLOTS]).then_inc(self.rounded, 1)

    def vector(self, dve):
        for k in range(self.n):
            dve.wait_ge(self.rounded, k + 1)
            dve.tensor_tensor(self.xl[:, k], self.ring[:, k % self.SLOTS], self.xh[:, k].bitcast(F32), ALU.subtract).then_inc(self.rest, 1)


def add_to_residual(dve, prod, xt, added):
    def evac(p, s):
        for c in range(NTC):
            dve.wait_ge(prod.ready, (p * 2 + s) * NTC + (c + 1))
            row = xt[:, bass.ds(p * 2 + s, 1), c * TC:(c + 1) * TC].rearrange("p o t -> p (o t)")
            dve.tensor_tensor(row, prod.bank[s][c][:, 0:TC], row, ALU.add).then_inc(prod.used, 1)
    return evac


def stage_merge(nc, env, io):
    with Stage(nc, "merge") as st:
        banks = st.banks()
        S = st.sem
        ring = st.sb("branch", [P, 3, T])
        bh, bl = st.sb("branch_hi", [P, KM, T], F32R), st.sb("branch_lo", [P, KM, T], F32R)
        merged = st.sb("merged", [P, KD, T])
        gz = [st.sb(f"gate_z{s}", [P, T]) for s in range(2)]
        gs = [st.sb(f"gate{s}", [P, T]) for s in range(2)]
        tmp = st.sb("gated", [P, NTC, TC])
        bufs = Product.buffers(st, KM, "wb")
        prods = [Product(st, f"wb{n}", KM, KD // 2, wtile(io["w_branch"], KM, m0=KD * n), bh, bl, banks, bufs=bufs) for n in range(3)]
        splits = [StreamSplit(st, f"br{n}", lambda k, n=n: io["branch"][n, :, k], bh, bl, KM, ring) for n in range(3)]
        half = KD // 2
        with nc.Block() as block:
            @block.sync
            def _(sp):
                for n in range(3):
                    if n:
                        sp.wait_ge(splits[n - 1].rest, KM)
                        sp.wait_ge(prods[n - 1].rest, KD)
                    splits[n].load(sp)
                    prods[n].load(sp)
                sp.wait_ge(S("merged_done"), 1)
                sp.dma_start(io["merged"], merged[:]).then_inc(S("stored"), 16)
                sp.wait_ge(S("stored"), 16)

            @block.gpsimd
            def _(pool):
                for n in range(3):
                    def load(p, s, wait=True):
                        if wait:
                            pool.wait_ge(S(f"gate{n}"), p * 2 + (s - 1))
                        pool.dma_start(gz[s][:], io["z"][bass.ds(p * 2 + (Z_G + n * KD + s), 1)].rearrange("o p t -> (o p) t")).then_inc(S(f"gate_in{n}_{s}"), 16)
                    if n:
                        pool.wait_ge(S(f"gate{n - 1}"), KD)
                    load(0, 0, False)
                    load(0, 1, False)
                    with pool.Fori(1, half) as p:
                        load(p, 0)
                        load(p, 1)

            @block.scalar
            def _(act):
                for n in range(3):
                    if n:
                        act.wait_ge(prods[n - 1].ready, KD * NTC)
                    splits[n].scalar(act)

                    def gate(p, s):
                        act.wait_ge(S(f"gate_in{n}_{s}"), p * 16 + 16)
                        if not (isinstance(p, int) and p == 0):
                            act.wait_ge(prods[n].used, (p * 2 + (s - 1)) * NTC)
                        at = VAT["b_gate"] + n * KD
                        act.activation(gs[s][:], gz[s][:], ACT.Sigmoid, bias=env["vec"][:, bass.ds(p * 2 + (at + s), 1)]).then_inc(S(f"gate{n}"), 1)
                    if n:
                        act.wait_ge(prods[n - 1].used, KD * NTC)
                    prods[n].pipeline(act, prods[n].split_hi, gate)

            @block.vector
            def _(dve):
                for n in range(3):
                    splits[n].vector(dve)
                    prod = prods[n]

                    def evac(p, s):
                        dve.wait_ge(S(f"gate{n}"), p * 2 + (s + 1))
                        if n and not (isinstance(p, int) and p == 0 and s == 0):
                            dve.wait_ge(S(f"summed{n}"), (p * 2 + s) * NTC)
                        elif n == 2:
                            dve.wait_ge(S("summed1"), KD * NTC)
                        for c in range(NTC):
                            cs = slice(c * TC, (c + 1) * TC)
                            row = merged[:, bass.ds(p * 2 + s, 1), cs].rearrange("p o t -> p (o t)")
                            dve.wait_ge(prod.ready, (p * 2 + s) * NTC + (c + 1))
                            if n == 0:
                                dve.tensor_tensor(row, prod.bank[s][c][:, 0:TC], gs[s][:, cs], ALU.mult).then_inc(prod.used, 1)
                            else:
                                dve.tensor_tensor(tmp[:, c, :], prod.bank[s][c][:, 0:TC], gs[s][:, cs], ALU.mult).then_inc(prod.used, 1)
                                dve.wait_ge(prod.used, (p * 2 + s) * NTC + (c + 1))
                                dve.tensor_tensor(row, tmp[:, c, :], row, ALU.add).then_inc(S(f"summed{n}"), 1)
                    prod.pipeline(dve, prod.split_lo, evac)
                    if n:
                        dve.wait_ge(S(f"summed{n}"), KD * NTC)
                    else:
                        dve.wait_ge(prod.used, KD * NTC)
                dve.tensor_copy(tmp[:, 0, 0:1], tmp[:, 1, 0:1]).then_inc(S("merged_done"), 1)

            @block.tensor
            def _(pe):
                for n in range(3):
                    pe.wait_ge(splits[n].rest, KM)
                    if n:
                        pe.wait_ge(prods[n - 1].used, KD * NTC)
                    prods[n].products(pe)




def stage_residual(nc, env, io, name, src, w, parts, load_x=False):
    with Stage(nc, name) as st:
        banks = st.banks()
        S = st.sem
        kt = max(n for _, n in parts)
        xt = env["xt"]
        ring = st.sb("x", [P, 3, T])
        xh, xl = st.sb("x_hi", [P, kt, T], F32R), st.sb("x_lo", [P, kt, T], F32R)
        bufs = Product.buffers(st, kt, "w")
        prods = [Product(st, f"w{i}", n, KD // 2, wtile(w, n, k0=k0), xh, xl, banks, bufs=bufs) for i, (k0, n) in enumerate(parts)]
        splits = [StreamSplit(st, f"x{i}", lambda k, k0=k0: src[:, k0 + k], xh, xl, n, ring) for i, (k0, n) in enumerate(parts)]
        whole = lambda eng, i: eng.wait_ge(prods[i].ready, KD * NTC)
        with nc.Block() as block:
            @block.sync
            def _(sp):
                for i, prod in enumerate(prods):
                    if i:
                        sp.wait_ge(splits[i - 1].rest, splits[i - 1].n)
                        sp.wait_ge(prods[i - 1].rest, KD)
                    splits[i].load(sp)
                    if load_x and i == 0:
                        sp.dma_start(xt[:], io["xt"]).then_inc(S("residual_in"), 16)
                    prod.load(sp)

            @block.scalar
            def _(act):
                for i, prod in enumerate(prods):
                    if i:
                        whole(act, i - 1)
                    splits[i].scalar(act)
                    prod.pipeline(act, prod.split_hi, lambda p, s: None)

            @block.vector
            def _(dve):
                for i, prod in enumerate(prods):
                    splits[i].vector(dve)
                    if load_x and i == 0:
                        dve.wait_ge(S("residual_in"), 16)
                    if i:
                        dve.wait_ge(prods[i - 1].used, KD * NTC)
                    prod.pipeline(dve, prod.split_lo, add_to_residual(dve, prod, xt, None))

            @block.tensor
            def _(pe):
                for i, prod in enumerate(prods):
                    pe.wait_ge(splits[i].rest, splits[i].n)
                    if i:
                        pe.wait_ge(prods[i - 1].used, KD * NTC)
                    prod.products(pe)


def stage_queries(nc, env, io):
    with Stage(nc, "xq") as st:
        banks = st.banks()
        S = st.sem
        xt, vec = env["xt"], env["vec"]
        xh, xl = st.sb("xh", [P, KD, T], F32R), st.sb("xl", [P, KD, T], F32R)
        mem = st.sb("mem", [P, KD, NMEM])
        out = [st.sb(f"q{s}", [P, T]) for s in range(2)]
        bufs, nbufs = Product.buffers(st, KD, "w"), Norm.buffers(st, "norm")
        ones = env["mask"]("ones")
        nx = Norm(st, "nx", xt, vec[:, VAT["norm_x"]:], xh, xl, ones, banks, bufs=nbufs)
        nm = Norm(st, "nm", mem, vec[:, VAT["norm_mem"]:], xh, xl, ones, banks, tc=NMEM, ntc=1, bufs=nbufs)
        nx.eps = nm.eps = env["eps"]
        pq = Product(st, "wq", KD, KD // 2, wtile(io["w_xq"], KD), xh, xl, banks, bufs=bufs)
        pm = Product(st, "wm", KD, KD, wtile(io["w_mem_kv"], KD), xh, xl, banks[6:8], tc=NMEM, ntc=1, bufs=bufs)
        kv = env["kv"]
        with nc.Block() as block:
            @block.sync
            def _(sp):
                sp.dma_start(mem[:], io["memt"]).then_inc(S("mem_in"), 16)
                pm.load(sp)
                sp.wait_ge(pm.rest, 2 * KD)
                pq.load(sp)

            @block.scalar
            def _(act):
                act.wait_ge(S("mem_in"), 16)
                nm.scalar(act)
                pm.pipeline(act, pm.split_hi, lambda p, s: None)
                act.wait_ge(pm.ready, 2 * KD)
                nx.scalar(act)

                def evac(p, s):
                    if not (isinstance(p, int) and p == 0):
                        act.wait_ge(S(f"q_stored{s}"), p * 16)
                    for c in range(NTC):
                        act.wait_ge(pq.ready, (p * 2 + s) * NTC + (c + 1))
                        act.copy(out[s][:, c * TC:(c + 1) * TC], pq.bank[s][c][:, 0:TC]).then_inc(pq.used, 1)
                    act.wait_ge(pq.used, (p * 2 + (s + 1)) * NTC)
                    act.dma_start(io["q"][:, bass.ds(p * 2 + s, 1)].rearrange("p o t -> p (o t)"), out[s][:]).then_inc(S(f"q_stored{s}"), 16)
                pq.pipeline(act, pq.split_hi, evac)
                act.dma_start(io["o_mem"], kv[:]).then_inc(S("kv_stored"), 16)
                act.wait_ge(S("kv_stored"), 16)
                for s in range(2):
                    act.wait_ge(S(f"q_stored{s}"), 16 * pq.pairs)

            @block.vector
            def _(dve):
                nm.vector(dve)

                def evac(p, s):
                    dve.wait_ge(pm.ready, p * 2 + (s + 1))
                    dve.tensor_copy(kv[:, bass.ds(p * 2 + s, 1)].rearrange("p o t -> p (o t)"), pm.bank[s][0][:, 0:NMEM]).then_inc(pm.used, 1)
                pm.pipeline(dve, pm.split_lo, evac)
                nx.vector(dve)
                pq.pipeline(dve, pq.split_lo, lambda p, s: None)

            @block.tensor
            def _(pe):
                nm.tensor(pe)
                pe.wait_ge(nm.rest, KD)
                pm.products(pe)
                pe.wait_ge(nm.rooted, 1)
                nx.tensor(pe)
                pe.wait_ge(nx.rest, KD * NTC)
                pq.products(pe)


def stage_cross(nc, env, io):
    with Stage(nc, "cross") as st:
        banks = st.banks()
        S = st.sem
        kv, ident = env["kv"], env["mask"]("ident")
        q = st.sb("q", [P, KD, T])
        v = st.sb("v", [P, 2, D])
        s_ = [st.sb(f"scores{i}", [P, XH, NMEM]) for i in range(2)]
        stat = [st.sb(f"stat{i}", [P, 3, XH]) for i in range(2)]
        pt = st.sb("probs_t", [P, XH, 2, P])
        o = [st.sb(f"out{i}", [P, KD, P]) for i in range(2)]
        qm = st.sb("q_masked", [P, KD, 2, P])
        ks = [st.sb(f"k_sample{i}", [P, KD, NMEM]) for i in range(2)]
        vs = [st.sb(f"v_sample{i}", [P, 2, D]) for i in range(2)]
        SC = XHD ** -0.5
        NT = TT - 1
        b2 = lambda i: banks[i][:].rearrange("p (h m) -> p h m", h=2)
        dt_ = lambda i: banks[i][:].rearrange("p (n t) -> p n t", n=4)
        with nc.Block() as block:
            @block.sync
            def _(sp):
                sp.dma_start(q[:], io["q"]).then_inc(S("q_in"), 16)
                for b in range(NB):
                    if b >= 2:
                        sp.wait_ge(S("k_used"), b - 1)
                    sp.dma_start(ks[b % 2][:], io["mem_k"][b]).then_inc(S(f"k_in{b % 2}"), 16)
                for b in range(NB):
                    if b >= 2:
                        sp.wait_ge(S("v_used"), b - 1)
                    sp.dma_start(vs[b % 2][:], io["mem_v"][b]).then_inc(S(f"v_in{b % 2}"), 16)

            @block.gpsimd
            def _(pool):
                pool.wait_ge(S("q_in"), 16)
                for b in range(NB):
                    if b >= 2:
                        pool.wait_ge(S("k_used"), b - 1)
                    pool.memset(qm[:, :, b % 2], 0.0).then_inc(S("q_zero"), 1)
                    pool.wait_ge(S("q_zero"), b + 1)
                    pool.tensor_copy(qm[:, :, b % 2, b * NS:(b + 1) * NS], q[:, :, SEQ + b * NS:SEQ + (b + 1) * NS]).then_inc(S("q_masked"), 1)

            def softmax_scores(pe, t, keys):
                if t:
                    pe.wait_ge(S("scored"), 2 * t)
                for h in range(XH):
                    for d in range(2):
                        mm = pe.matmul(banks[h // 2][:, (h % 2) * NMEM:(h % 2 + 1) * NMEM], q[:, 2 * h + d, t * P:(t + 1) * P],
                                       keys(h, d), start=(d == 0), stop=(d == 1), skip_group_check=True)
                mm.then_inc(S("scores"), 1)

            def turn_probs(pe, t):
                pe.wait_ge(S("probs"), t + 1)
                if t:
                    pe.wait_ge(S("probs_t"), 2 * t)
                for h in range(XH):
                    for m in range(2):
                        mm = pe.transpose(banks[2 + h // 2][:, ((h % 2) * 2 + m) * P:((h % 2) * 2 + m + 1) * P],
                                          s_[t % 2][:, h, m * P:(m + 1) * P], ident)
                mm.then_inc(S("probs_turned"), 1)
                pe.wait_ge(S("probs_t"), 2 * (t + 1))
                if t:
                    pe.wait_ge(S("out_copied"), 2 * t)

            @block.tensor
            def _(pe):
                for n in range(4):
                    if n >= 2:
                        pe.wait_ge(S("v_copied"), n - 1)
                    for j in range(4):
                        m, f = n // 2, (n % 2) * 4 + j
                        mm = pe.transpose(banks[6 + n % 2][:, j * P:(j + 1) * P], kv[:, KD + f, m * P:(m + 1) * P], ident)
                    mm.then_inc(S("v_turned"), 1)
                pe.wait_ge(S("v_copied"), 4)
                pe.wait_ge(S("q_in"), 16)
                for t in range(NT + 1):
                    if t < NT:
                        softmax_scores(pe, t, lambda h, d: kv[:, 2 * h + d, :])
                    if t == 0:
                        continue
                    turn_probs(pe, t - 1)
                    for f in range(KD):
                        for m in range(2):
                            mm = pe.matmul(banks[4 + f // 4][:, (f % 4) * P:(f % 4 + 1) * P], v[:, m, f * P:(f + 1) * P],
                                           pt[:, f // 2, m, :], start=(m == 0), stop=(m == 1), skip_group_check=True)
                    mm.then_inc(S("weighted"), 1)
                pe.wait_ge(S("scored"), 2 * NT)
                for b in range(NB):
                    pe.wait_ge(S("q_masked"), b + 1)
                    pe.wait_ge(S(f"k_in{b % 2}"), 16 * (b // 2 + 1))
                    for h in range(XH):
                        for d in range(2):
                            first = b == 0 and d == 0
                            mm = pe.matmul(banks[h // 2][:, (h % 2) * NMEM:(h % 2 + 1) * NMEM], qm[:, 2 * h + d, b % 2, :],
                                           ks[b % 2][:, 2 * h + d, :], start=(first and h % 2 == 0), stop=(b == NB - 1 and d == 1),
                                           skip_group_check=True)
                    mm.then_inc(S("k_used"), 1)
                mm_scores = pe.matmul(banks[7][:, 0:2], ident, ident[:, 0:2], start=True, stop=True)
                mm_scores.then_inc(S("scores"), 1)
                turn_probs(pe, NT)
                for b in range(NB):
                    pe.wait_ge(S(f"v_in{b % 2}"), 16 * (b // 2 + 1))
                    for f in range(KD):
                        for m in range(2):
                            mm = pe.matmul(banks[4 + f // 4][:, (f % 4) * P + b * NS:(f % 4) * P + (b + 1) * NS],
                                           vs[b % 2][:, m, f * P:(f + 1) * P], pt[:, f // 2, m, b * NS:(b + 1) * NS],
                                           start=(m == 0), stop=(m == 1), skip_group_check=True)
                    mm.then_inc(S("v_used"), 1)
                pe.matmul(banks[7][:, 0:2], ident, ident[:, 0:2], start=True, stop=True).then_inc(S("weighted"), 1)

            @block.scalar
            def _(act):
                for n in range(4):
                    m, f = n // 2, (n % 2) * 512
                    act.wait_ge(S("v_turned"), n + 1)
                    act.copy(v[:, m, f:f + 512], banks[6 + n % 2][:]).then_inc(S("v_copied"), 1)
                for t in range(TT):
                    act.wait_ge(S("centred"), t + 1)
                    act.activation(s_[t % 2][:], s_[t % 2][:], ACT.Exp, scale=SC).then_inc(S("exp"), 1)
                    act.wait_ge(S("probs_turned"), t + 1)
                    for n in range(2):
                        act.copy(pt[:, 2 * n:2 * n + 2].rearrange("p h m t -> p (h m t)"), banks[2 + n][:]).then_inc(S("probs_t"), 1)
                    act.wait_ge(S("weighted"), t + 1)
                    if t >= 2:
                        act.wait_ge(S(f"out_stored{t % 2}"), 16 * (t // 2))
                    for n in range(2):
                        act.copy(o[t % 2][:, 4 * n:4 * n + 4], dt_(4 + n)).then_inc(S("out_copied"), 1)
                    act.wait_ge(S("out_copied"), 2 * t + 2)
                    act.dma_start(io["xo"][:, :, t * P:(t + 1) * P], o[t % 2][:]).then_inc(S(f"out_stored{t % 2}"), 16)
                act.wait_ge(S("out_stored0"), 16 * 5)
                act.wait_ge(S("out_stored1"), 16 * 4)

            @block.vector
            def _(dve):
                steps = [0]

                def link(ins):
                    steps[0] += 1
                    ins.then_inc(S("dve_step"), 1)
                    dve.wait_ge(S("dve_step"), steps[0])
                up = lambda x: x.rearrange("p (h o) -> p h o", o=1).broadcast_to([P, XH, NMEM])
                for t in range(TT):
                    x, z = s_[t % 2], stat[t % 2]
                    dve.wait_ge(S("scores"), t + 1)
                    if t >= 2:
                        dve.wait_ge(S("probs_turned"), t - 1)
                    for n in range(2):
                        dve.tensor_reduce(z[:, 0, 2 * n:2 * n + 2], b2(n), AX.X, ALU.max).then_inc(S("maxed"), 1)
                    dve.wait_ge(S("maxed"), 2 * t + 2)
                    for n in range(2):
                        m = z[:, 0, 2 * n:2 * n + 2].rearrange("p (h o) -> p h o", o=1).broadcast_to([P, 2, NMEM])
                        dve.tensor_tensor(x[:, 2 * n:2 * n + 2], b2(n), m, ALU.subtract).then_inc(S("scored"), 1)
                    dve.wait_ge(S("scored"), 2 * t + 2)
                    dve.tensor_copy(z[:, 1], z[:, 0]).then_inc(S("centred"), 1)
                    dve.wait_ge(S("exp"), t + 1)
                    link(dve.tensor_reduce(z[:, 1], x[:], AX.X, ALU.add))
                    link(dve.reciprocal(z[:, 2], z[:, 1]))
                    dve.tensor_tensor(x[:], x[:], up(z[:, 2]), ALU.mult).then_inc(S("probs"), 1)


def stage_up(nc, env, io):
    with Stage(nc, "up") as st:
        banks = st.banks()
        S = st.sem
        xt, vec = env["xt"], env["vec"]
        xh, xl = st.sb("xh", [P, KD, T], F32R), st.sb("xl", [P, KD, T], F32R)
        PAD = 2 + SEQ + NB * (2 + NS)
        u = [st.sb(f"u{s}", [P, PAD]) for s in range(2)]
        y = [st.sb(f"y{s}", [P, T]) for s in range(2)]
        last = st.sb("last", [P, 2 * KF, 2 * (NB + 1)])
        state = st.sb("state", [P, 2 * KF, NB, 2])
        norm = Norm(st, "norm", xt, vec[:, VAT["norm_ffn"]:], xh, xl, env["mask"]("ones"), banks)
        norm.eps = env["eps"]
        w = io["w_up"]
        pair = lambda p, s: w[bass.ds(p + s * KF, 1)].rearrange("o p k m -> (o p) k m")
        prod = Product(st, "wup", KD, KF, pair, xh, xl, banks)
        prompt = lambda x: x[:, 0:SEQ]
        samples = lambda x: x[:, SEQ:T].rearrange("p (b s) -> p b s", b=NB)
        padded = lambda x: x[:, 2 + SEQ:PAD].rearrange("p (b s) -> p b s", b=NB)
        with nc.Block() as block:
            @block.sync
            def _(sp):
                sp.dma_start(state[:], io["ffn_state"]).then_inc(S("state_in"), 16)
                for s in range(2):
                    sp.dma_start(prod.raw[s][:], pair(0, s)).then_inc(prod.arrived[s], 16)

                def store(p):
                    sp.wait_ge(S("h"), p + 1)
                    sp.dma_start(io["h"][:, bass.ds(p, 1)].rearrange("p o t -> p (o t)"), y[0][:]).then_inc(S("h_stored"), 16)
                with sp.Fori(1, KF) as p:
                    for s in range(2):
                        sp.wait_ge(prod.rest, p * 2 + (s - 1))
                        sp.dma_start(prod.raw[s][:], pair(p, s)).then_inc(prod.arrived[s], 16)
                    store(p - 1)
                store(KF - 1)
                sp.wait_ge(S("h_stored"), 16 * KF)

            @block.gpsimd
            def _(pool):
                for s in range(2):
                    pool.memset(u[s][:, 0:2], 0.0).then_inc(S("padding_zero"), 1)
                pool.wait_ge(S("state_in"), 16)

                def put(p, s):
                    f = bass.ds(p + s * KF, 1)
                    if not (isinstance(p, int) and p == 0):
                        pool.wait_ge(S(f"conv{s}"), p * 2)
                        pool.wait_ge(S(f"last{s}"), p * 2)
                    pool.tensor_copy(padded(u[s])[:, :, 0:2], state[:, f].rearrange("p o b k -> p (o b) k")).then_inc(S(f"state_put{s}"), 1)
                    pool.wait_ge(S(f"u{s}"), p * 4 + 4)
                    pool.tensor_copy(last[:, f, 0:2].rearrange("p o k -> p (o k)"), u[s][:, SEQ:SEQ + 2]).then_inc(S(f"last{s}"), 1)
                    pool.tensor_copy(last[:, f, 2:].rearrange("p o (b k) -> p (o b) k", k=2), padded(u[s])[:, :, NS:NS + 2]).then_inc(S(f"last{s}"), 1)
                put(0, 0)
                put(0, 1)
                with pool.Fori(1, KF) as p:
                    put(p, 0)
                    put(p, 1)

            @block.scalar
            def _(act):
                norm.scalar(act)

                def evac(p, s):
                    if not (isinstance(p, int) and p == 0):
                        act.wait_ge(S(f"conv{s}"), p * 2)
                        act.wait_ge(S(f"last{s}"), p * 2)
                    for c in range(NTC):
                        act.wait_ge(prod.ready, (p * 2 + s) * NTC + (c + 1))
                        n = TC if c < NTC - 1 else SEQ - c * TC
                        f = act.copy(u[s][:, 2 + c * TC:2 + c * TC + n], prod.bank[s][c][:, 0:n]).then_inc(S(f"u{s}"), 1)
                    act.copy(padded(u[s])[:, :, 2:], prod.bank[s][NTC - 1][:, TC - NB * NS:TC].rearrange("p (b s) -> p b s", b=NB)).then_inc(S(f"u{s}"), 1)
                    act.wait_ge(S(f"u{s}"), p * 4 + 4)
                    act.sem_inc(prod.used, NTC)
                    if s == 1:
                        act.wait_ge(S("conv0"), p * 2 + 2)
                        act.activation(y[0][:], y[0][:], ACT.Gelu_apprx_tanh).then_inc(S("gelu"), 1)
                prod.pipeline(act, prod.split_hi, evac)
                act.wait_ge(S("last0"), 2 * KF)
                act.wait_ge(S("last1"), 2 * KF)
                act.dma_start(io["o_ffn"], last[:]).then_inc(S("last_stored"), 16)
                act.wait_ge(S("last_stored"), 16)

            @block.vector
            def _(dve):
                norm.vector(dve)
                dve.wait_ge(S("padding_zero"), 2)

                def evac(p, s):
                    dve.wait_ge(S(f"u{s}"), p * 4 + 4)
                    dve.wait_ge(S(f"state_put{s}"), p + 1)
                    tap = lambda k: vec[:, bass.ds(p + (VAT["ffn_conv_w"] + k * 2 * KF + s * KF), 1)]
                    if not (isinstance(p, int) and p == 0):
                        dve.wait_ge(S("h"), p)
                        dve.wait_ge(S("h_stored"), p * 16)
                    srcs = (lambda k: u[s][:, k:k + SEQ], lambda k: padded(u[s])[:, :, k:k + NS])
                    dsts = (prompt(y[s]), samples(y[s]))
                    for i, (src, dst) in enumerate(zip(srcs, dsts)):
                        dve.tensor_scalar(dst, src(0), tap(0), None, ALU.mult).then_inc(S(f"tap_a{s}"), 1)
                    dve.wait_ge(S(f"tap_a{s}"), p * 2 + 2)
                    for src, dst in zip(srcs, dsts):
                        dve.scalar_tensor_tensor(out=dst, in0=src(1), scalar=tap(1), in1=dst, op0=ALU.mult, op1=ALU.add).then_inc(S(f"tap_b{s}"), 1)
                    dve.wait_ge(S(f"tap_b{s}"), p * 2 + 2)
                    for src, dst in zip(srcs, dsts):
                        dve.scalar_tensor_tensor(out=dst, in0=src(2), scalar=tap(2), in1=dst, op0=ALU.mult, op1=ALU.add).then_inc(S(f"conv{s}"), 1)
                    if s == 1:
                        dve.wait_ge(S("gelu"), p + 1)
                        dve.wait_ge(S("conv1"), p * 2 + 2)
                        dve.tensor_tensor(y[0][:], y[0][:], y[1][:], ALU.mult).then_inc(S("h"), 1)
                prod.pipeline(dve, prod.split_lo, evac)

            @block.tensor
            def _(pe):
                norm.tensor(pe)
                pe.wait_ge(norm.rest, KD * NTC)
                prod.products(pe)


def stage_final(nc, env, io):
    with Stage(nc, "final") as st:
        banks = st.banks()
        S = st.sem
        y = st.sb("y", [P, KD, T])
        norm = Norm(st, "norm", env["xt"], env["vec"][:, VAT["norm_final"]:], None, y, env["mask"]("ones"), banks)
        norm.eps = env["eps"]
        with nc.Block() as block:
            @block.sync
            def _(sp):
                for c in range(NTC):
                    sp.wait_ge(norm.normed, KD * (c + 1))
                    cs = slice(c * TC, (c + 1) * TC)
                    sp.dma_start(io["y"][:, :, cs], y[:, :, cs]).then_inc(S("stored"), 16)
                sp.wait_ge(S("stored"), 16 * NTC)

            @block.scalar
            def _(act):
                norm.scalar(act)

            @block.vector
            def _(dve):
                norm.vector(dve)

            @block.tensor
            def _(pe):
                norm.tensor(pe)


OUTS = {"y": [P, KD, T], "o_conv_p": [KM, P, 3], "o_conv_s": [KM, P, NB, 3], "o_h": [P, KM, NB + 1],
        "o_swa_new": [2, P, P + NB * NS], "o_swa_kept": [2 * NB, (P - NS) * P], "o_shift": [P, NRW, NB + 1], "o_state_p": [P, KM, P], "o_state_s": [P, KM, NB, HD],
        "o_mem": [P, 2 * KD, NMEM], "o_ffn": [P, 2 * KF, 2 * (NB + 1)]}
SCRATCH = {"z": [Z_N, P, T], "branch": [3, P, KM, T], "merged": [P, KD, T], "q": [P, KD, T], "xo": [P, KD, T], "h": [P, KF, T]}


def hybrid_stream_step(nc, io, stages=99):
    for name, shape in SCRATCH.items():
        io[name] = nc.dram_tensor(f"scratch_{name}", shape, F32, kind="Internal").ap() if name not in io else io[name]
    with ExitStack() as ctx:
        sb = lambda n, s: ctx.enter_context(nc.sbuf_tensor(n, s, F32))
        vec, masks, eps = sb("vec", [P, NVEC]), sb("masks", [P, MW]), sb("eps", [P, 2])
        w = len(MASKS) * P
        env = {"vec": vec, "masks": masks, "eps": eps,
               "mask": lambda n: masks[:, MASKS.index(n) * P:(MASKS.index(n) + 1) * P],
               "resets": [masks[:, w + i * KM * P:w + (i + 1) * KM * P] for i in range(2)],
               "sample_rows": masks[:, w + 2 * KM * P:MW]}
        todo = [stage_in_projection, stage_lru, stage_swa, stage_rwkv, stage_merge]
        for stage in todo[:stages]:
            stage(nc, env, io)
        if stages < 6:
            return
        env["xt"] = sb("xt", [P, KD, T])
        stage_residual(nc, env, io, "out", io["merged"], io["w_out"], [(0, KD)], load_x=True)
        with nc.sbuf_tensor("mem_kv", [P, 2 * KD, NMEM], F32) as kv:
            env["kv"] = kv
            stage_queries(nc, env, io)
            stage_cross(nc, env, io)
        stage_residual(nc, env, io, "xo", io["xo"], io["w_xo"], [(0, KD)])
        stage_up(nc, env, io)
        stage_residual(nc, env, io, "down", io["h"], io["w_down"], [(0, KF // 2), (KF // 2, KF // 2)])
        stage_final(nc, env, io)


def lay_out(i):
    c = np.ascontiguousarray
    feat = lambda x: c(x.T.reshape(-1, P, x.shape[0]).transpose(1, 0, 2))
    tiles = lambda w: c(w.reshape(w.shape[0] // P, P, w.shape[1] // P, P).transpose(2, 1, 0, 3))
    one = {k: v[0] for k, v in i.items() if k not in ("x_prompt", "x_sample", "mem_prompt", "norm_final")}
    a = {"xt": feat(np.concatenate([i["x_prompt"].reshape(SEQ, D), i["x_sample"].reshape(NB * NS, D)])),
         "memt": feat(i["mem_prompt"].reshape(NMEM, D)), "masks": shape_masks()}
    vecs = {n: (i[n] if n == "norm_final" else one[n]).reshape(-1, P) for n, _ in VEC}
    a["vec"] = c(np.concatenate([vecs[n] for n, _ in VEC]).T)
    for n in ("w_in", "w_out", "w_xq", "w_mem_kv", "w_xo", "w_up", "w_down"):
        a[n] = tiles(one[n])
    a["w_branch"] = np.concatenate([tiles(w) for w in one["w_branch"]])
    gw = np.zeros((P, 2, KM, P), np.float32)
    for g in range(2):
        for h in range(NH):
            s = slice(64 * (h % 2), 64 * (h % 2) + 64)
            gw[s, g, h // 2, s] = one["lru_gate_w"][g, h]
    a["lru_gate_w"] = gw
    a["lru_conv"] = c(one["state_lru_conv"].reshape(NB, 3, KM, P).transpose(2, 3, 0, 1))
    a["lru_h"] = c(one["state_lru_h"].reshape(NB, KM, P).transpose(2, 1, 0))
    k = one["cache_swa_k"][:, CH:]
    two = [k.transpose(2, 3, 0, 1).reshape(P, NB, CH), k[:, :, ::-1].transpose(2, 3, 0, 1).reshape(P, NB, CH)]
    a["swa_k"] = c(np.stack(two, axis=1))
    a["swa_v"] = c(one["cache_swa_v"][:, CH:].transpose(1, 0, 2, 3).reshape(CH, NB, P))
    a["swa_cache"] = np.stack([one[n][:, NS:].reshape(NB, -1) for n in ("cache_swa_k", "cache_swa_v")]).reshape(2 * NB, -1)
    a["sink"] = one["swa_sink"].reshape(1, NH)
    a["w2a2"] = np.concatenate([one["rwkv_w2"], one["rwkv_a2"]])
    a["g2"] = one["rwkv_g2"]
    a["shift"] = c(one["state_rwkv_shift"].reshape(NB, NRW, P).transpose(2, 1, 0))
    s0 = one["state_rwkv"].reshape(NB, KM, 2, HD, HD).transpose(2, 4, 1, 0, 3)
    a["s0"] = c(s0.reshape(P, KM, NB, HD))
    diag = np.zeros((2, HD, NB, KM, 2, HD), np.float32)
    for s in range(2):
        diag[s, :, :, :, s] = s0[s].transpose(0, 2, 1, 3)
    a["s0_diag"] = diag.reshape(P, NB, KM, P)
    a["mem_k"] = c(one["cache_mem_k"].reshape(NB, NMEM, KD, P).transpose(0, 3, 2, 1))
    a["mem_v"] = c(one["cache_mem_v"].reshape(NB, 2, P, D).transpose(0, 2, 1, 3))
    a["ffn_state"] = c(one["state_ffn_conv"].reshape(NB, 2, 2 * KF, P).transpose(3, 2, 0, 1))
    return a


def hand_back(o):
    c = np.ascontiguousarray
    y = c(o["y"].transpose(2, 1, 0).reshape(T, D))
    conv_s = o["o_conv_s"].transpose(2, 3, 0, 1).reshape(1, NB, 3, MIX)
    conv_p = o["o_conv_p"].transpose(2, 0, 1).reshape(1, 1, 3, MIX)
    h = o["o_h"].transpose(2, 1, 0).reshape(NB + 1, MIX)
    new = o["o_swa_new"].transpose(0, 2, 1).reshape(2, P + NB * NS, 2, HD)
    swa_p = [c(n[:P].reshape(1, 1, P, 2, HD)) for n in new]
    kept = o["o_swa_kept"].reshape(2, 1, NB, P - NS, 2, HD)
    swa_s = [np.concatenate([old, n[P:].reshape(1, NB, NS, 2, HD)], axis=2) for old, n in zip(kept, new)]
    shift = o["o_shift"].transpose(2, 1, 0).reshape(NB + 1, 1, NRW * P)
    sp = o["o_state_p"].reshape(2, HD, KM, 2, HD)
    s_p = np.stack([sp[s, :, :, s] for s in range(2)]).transpose(2, 0, 3, 1).reshape(1, 1, NH, HD, HD)
    s_s = o["o_state_s"].reshape(2, HD, KM, NB, HD).transpose(3, 2, 0, 4, 1).reshape(1, NB, NH, HD, HD)
    ffn = o["o_ffn"].transpose(2, 1, 0).reshape(NB + 1, 2, 2 * FF)
    mem = o["o_mem"].transpose(2, 1, 0).reshape(NMEM, 2, XH, XHD)
    return (y[:SEQ].reshape(1, SEQ, D), y[SEQ:].reshape(NB, NS, D),
            c(conv_p), c(h[:1][None]), swa_p[0], swa_p[1], c(shift[:1][None]), c(s_p), c(ffn[:1][None]),
            c(mem[:, 0][None, None]), c(mem[:, 1][None, None]),
            c(conv_s), c(h[1:][None]), swa_s[0], swa_s[1], c(shift[1:][None]), c(s_s), c(ffn[1:][None]))


def kernel(**inputs):
    from concourse import bacc
    from concourse.bass_utils import run_bass_kernel_spmd

    nc = bacc.Bacc("TRN2", target_bir_lowering=False, num_devices=1)
    arrays = lay_out(inputs)
    io = {n: nc.dram_tensor(f"in_{n}", a.shape, mybir.dt.from_np(a.dtype), kind="ExternalInput").ap() for n, a in arrays.items()}
    io |= {n: nc.dram_tensor(f"out_{n}", s, F32, kind="ExternalOutput").ap() for n, s in OUTS.items()}
    hybrid_stream_step(nc, io)
    r = run_bass_kernel_spmd(nc, [{f"in_{n}": a for n, a in arrays.items()}], core_ids=[0])
    return hand_back({n: r.results[0][f"out_{n}"] for n in OUTS})
```

```python
from contextlib import ExitStack

import numpy as np

import concourse.bass as bass
from concourse import mybir

F32 = mybir.dt.float32
F32R = mybir.dt.float32r
ALU = mybir.AluOpType
ACT = mybir.ActivationFunctionType
AX = mybir.AxisListType

P = 128
D = 1024
KD = D // P
SEQ = 1024
NB, NS = 8, 16
T = SEQ + NB * NS
TC = 384
NTC = T // TC
TT = T // P
MIX = 512
KM = MIX // P
NH, HD = 8, 64
CH = 64
NCH = SEQ // CH
FF = 2816
KF = FF // P
NMEM = 256
XH, XHD = 4, 256
EPS = 1e-6
GN_EPS = 64e-5
DEC = float(np.exp(-0.5))

Z_LX, Z_LY, Z_Q, Z_K, Z_V, Z_RW, Z_G, Z_N = 0, 4, 8, 12, 13, 14, 28, 52
NRW = Z_G - Z_RW

VEC = [("norm_mix", 8), ("b_gate", 24), ("lru_conv_w", 16), ("lru_conv_b", 4), ("lru_gate_b", 8),
       ("lru_lambda", 4), ("rwkv_mu", 14), ("rwkv_w0", 4), ("rwkv_a0", 4), ("rwkv_k_k", 4),
       ("rwkv_k_a", 4), ("rwkv_r_k", 4), ("rwkv_ln_w", 4), ("rwkv_ln_b", 4), ("norm_x", 8),
       ("norm_mem", 8), ("norm_ffn", 8), ("ffn_conv_w", 132), ("norm_final", 8)]
VAT = {}
for _n, _c in VEC:
    VAT[_n] = sum(c for _, c in VEC[:len(VAT)])
NVEC = sum(c for _, c in VEC)

MASKS = ["ident", "ones", "head", "off2", "off2T", "off4", "off8", "off16", "off32", "off64",
         "upS64", "upI64", "upS16", "upI16"]


def shape_masks():
    t = np.arange(P)[:, None]
    j = np.arange(P)[None, :]
    same = lambda n: t // n == j // n
    off = lambda n: same(n) & (t % n >= n // 2) & (j % n < n // 2)
    m = {"ident": t == j, "ones": (t >= 0) & (j >= 0), "head": same(HD), "off2": off(2), "off2T": off(2).T}
    for n in (4, 8, 16, 32, 64):
        m[f"off{n}"] = off(n)
    for n in (64, 16):
        m[f"upS{n}"] = same(n) & (t < j)
        m[f"upI{n}"] = same(n) & (t <= j)
    blocks = [m[n].astype(np.float32) for n in MASKS]
    col = np.arange(KM * P)[None, :] + np.zeros((P, 1), int)
    resets = [(col % n != 0).astype(np.float32) for n in (CH, NS)]
    rows = (t // NS == np.arange(NB)[None, :]).astype(np.float32)
    return np.ascontiguousarray(np.concatenate(blocks + resets + [rows], axis=1))


MW = len(MASKS) * P + 2 * KM * P + NB


class Stage:

    def __init__(self, nc, name):
        self.nc, self.name, self.ctx, self.sems = nc, name, ExitStack(), {}

    def __enter__(self):
        self.ctx.__enter__()
        return self

    def __exit__(self, *e):
        self.nc.clear_and_free_semaphores(list(self.sems.values()))
        self.nc.all_engine_barrier()
        return self.ctx.__exit__(*e)

    def sb(self, name, shape, dt=F32):
        return self.ctx.enter_context(self.nc.sbuf_tensor(f"{self.name}_{name}", shape, dt))

    def banks(self, n=8):
        return [self.ctx.enter_context(self.nc.psum_tensor(f"{self.name}_bank{i}", [P, 512], F32)) for i in range(n)]

    def sem(self, name):
        if name not in self.sems:
            self.sems[name] = self.nc.alloc_semaphore(f"{self.name}_{name}")
        return self.sems[name]


class Product:

    def __init__(self, st, tag, kt, pairs, weights, xh, xl, banks, tc=TC, ntc=NTC, bufs=None):
        self.st, self.kt, self.pairs, self.w = st, kt, pairs, weights
        self.xh, self.xl, self.tc, self.ntc = xh, xl, tc, ntc
        self.bank = [banks[:ntc], banks[ntc:2 * ntc]]
        self.raw, self.hi, self.lo = bufs or Product.buffers(st, kt, tag)
        self.arrived = [st.sem(f"{tag}_w_arrived{s}") for s in range(2)]
        self.rounded = st.sem(f"{tag}_w_rounded")
        self.rest = st.sem(f"{tag}_w_rest")
        self.ready = st.sem(f"{tag}_product_ready")
        self.used = st.sem(f"{tag}_product_used")

    @staticmethod
    def buffers(st, kt, tag):
        return tuple([st.sb(f"{tag}_{n}{s}", [P, kt, P], dt) for s in range(2)]
                     for n, dt in (("raw", F32), ("hi", F32R), ("lo", F32R)))

    def load(self, eng):
        for s in range(2):
            eng.dma_start(self.raw[s][:, 0:self.kt], self.w(0, s)).then_inc(self.arrived[s], 16)
        with eng.Fori(1, self.pairs) as p:
            for s in range(2):
                eng.wait_ge(self.rest, p * 2 + (s - 1))
                eng.dma_start(self.raw[s][:, 0:self.kt], self.w(p, s)).then_inc(self.arrived[s], 16)

    def split_hi(self, act, p, s):
        act.wait_ge(self.arrived[s], p * 16 + 16)
        if not (isinstance(p, int) and p == 0):
            act.wait_ge(self.ready, (p * 2 + (s - 1)) * self.ntc)
        act.copy(self.hi[s][:, 0:self.kt], self.raw[s][:, 0:self.kt]).then_inc(self.rounded, 1)

    def split_lo(self, dve, p, s):
        dve.wait_ge(self.rounded, p * 2 + (s + 1))
        dve.tensor_tensor(self.lo[s][:, 0:self.kt], self.raw[s][:, 0:self.kt],
                          self.hi[s][:, 0:self.kt].bitcast(F32), ALU.subtract).then_inc(self.rest, 1)

    def pipeline(self, eng, split, evac):
        def pair(p):
            if split:
                split(eng, p, 0)
            evac(p - 1, 1)
            if split:
                split(eng, p, 1)
            evac(p, 0)
        if split:
            split(eng, 0, 0)
            split(eng, 0, 1)
        evac(0, 0)
        pair(1)
        with eng.Fori(2, self.pairs) as p:
            pair(p)
        evac(self.pairs - 1, 1)

    def products(self, pe):
        def tile(p, s, wait):
            pe.wait_ge(self.rest, p * 2 + (s + 1))
            if wait:
                pe.wait_ge(self.used, (p * 2 + (s - 1)) * self.ntc)
            passes = ((self.hi, self.xh), (self.lo, self.xh), (self.hi, self.xl))
            for k in range(self.kt):
                for n, (w, x) in enumerate(passes):
                    for c in range(self.ntc):
                        last = k == self.kt - 1 and n == 2
                        mm = pe.matmul(self.bank[s][c][:, 0:self.tc], w[s][:, k, :],
                                       x[:, k, c * self.tc:(c + 1) * self.tc], start=(k == 0 and n == 0), stop=last)
                        if last:
                            mm.then_inc(self.ready, 1)
        tile(0, 0, False)
        tile(0, 1, False)
        with pe.Fori(1, self.pairs) as p:
            tile(p, 0, True)
            tile(p, 1, True)


class Norm:

    def __init__(self, st, tag, xt, gain, xh, xl, ones, banks, tc=TC, ntc=NTC, kd=KD, bufs=None):
        self.xt, self.gain, self.xh, self.xl, self.ones, self.banks = xt, gain, xh, xl, ones, banks
        self.tc, self.ntc, self.kd = tc, ntc, kd
        self.sq, self.rs, self.xn = bufs or Norm.buffers(st, tag)
        (self.squared, self.summed, self.rooted, self.inverse, self.normed, self.rounded, self.rest) = (
            st.sem(f"{tag}_{n}") for n in ("squared", "summed", "rooted", "inverse", "normed", "rounded", "rest"))

    @staticmethod
    def buffers(st, tag):
        return st.sb(f"{tag}_sq", [P, 4, TC]), st.sb(f"{tag}_rs", [P, T]), st.sb(f"{tag}_xn", [P, 2, TC])

    def cols(self, c):
        return slice(c * self.tc, (c + 1) * self.tc)

    def scalar(self, act):
        n = 0
        for c in range(self.ntc):
            for k in range(self.kd):
                if n >= 4:
                    act.wait_ge(self.summed, n - 3)
                act.activation(self.sq[:, n % 4, 0:self.tc], self.xt[:, k, self.cols(c)], ACT.Square).then_inc(self.squared, 1)
                n += 1
        for c in range(self.ntc):
            act.wait_ge(self.summed, self.kd * (c + 1))
            act.activation(self.rs[:, self.cols(c)], self.banks[c][:, 0:self.tc], ACT.Sqrt,
                           scale=1.0 / D, bias=self.eps[:, 0:1]).then_inc(self.rooted, 1)
        if self.xh is not None:
            for i in range(self.ntc * self.kd):
                c, k = divmod(i, self.kd)
                act.wait_ge(self.normed, i + 1)
                act.copy(self.xh[:, k, self.cols(c)], self.xn[:, i % 2, 0:self.tc]).then_inc(self.rounded, 1)

    def tensor(self, pe):
        n = 0
        for c in range(self.ntc):
            for k in range(self.kd):
                pe.wait_ge(self.squared, n + 1)
                pe.matmul(self.banks[c][:, 0:self.tc], self.ones, self.sq[:, n % 4, 0:self.tc],
                          start=(k == 0), stop=(k == self.kd - 1)).then_inc(self.summed, 1)
                n += 1

    def vector(self, dve):
        for c in range(self.ntc):
            dve.wait_ge(self.rooted, c + 1)
            dve.reciprocal(self.rs[:, self.cols(c)], self.rs[:, self.cols(c)]).then_inc(self.inverse, 1)
            dve.wait_ge(self.inverse, c + 1)
            for k in range(self.kd):
                i = c * self.kd + k
                out = self.xn[:, i % 2, 0:self.tc] if self.xh is not None else self.xl[:, k, self.cols(c)]
                if self.xh is not None and i >= 2:
                    dve.wait_ge(self.rest, i - 1)
                dve.scalar_tensor_tensor(out=out, in0=self.xt[:, k, self.cols(c)], scalar=self.gain[:, k:k + 1],
                                         in1=self.rs[:, self.cols(c)], op0=ALU.mult, op1=ALU.mult).then_inc(self.normed, 1)
                if self.xh is not None and i:
                    self.remainder(dve, i - 1)
        if self.xh is not None:
            self.remainder(dve, self.ntc * self.kd - 1)

    def remainder(self, dve, i):
        c, k = divmod(i, self.kd)
        dve.wait_ge(self.rounded, i + 1)
        dve.tensor_tensor(self.xl[:, k, self.cols(c)], self.xn[:, i % 2, 0:self.tc],
                          self.xh[:, k, self.cols(c)].bitcast(F32), ALU.subtract).then_inc(self.rest, 1)


def wtile(w, kt, m0=0, k0=0):
    def at(p, s):
        return w[bass.ds(p * 2 + (m0 + s), 1), :, k0:k0 + kt, :].rearrange("o p k m -> (o p) k m")
    return at


def stage_in_projection(nc, env, io):
    with Stage(nc, "inproj") as st:
        banks = st.banks()
        xt = st.sb("xt", [P, KD, T])
        xh, xl = st.sb("xh", [P, KD, T], F32R), st.sb("xl", [P, KD, T], F32R)
        out = [st.sb(f"z{s}", [P, T]) for s in range(2)]
        x_in = [st.sem(f"x_arrived{c}") for c in range(NTC)]
        vec_in = st.sem("constants_arrived")
        eps_set = st.sem("eps_set")
        stored = [st.sem(f"z_stored{s}") for s in range(2)]
        vec, masks = env["vec"], env["masks"]
        norm = Norm(st, "norm", xt, vec[:, VAT["norm_mix"]:], xh, xl, env["mask"]("ones"), banks)
        norm.eps = env["eps"]
        prod = Product(st, "win", KD, Z_N // 2, wtile(io["w_in"], KD), xh, xl, banks)
        with nc.Block() as block:
            @block.sync
            def _(sp):
                for c in range(NTC):
                    sp.dma_start(xt[:, :, c * TC:(c + 1) * TC], io["xt"][:, :, c * TC:(c + 1) * TC]).then_inc(x_in[c], 16)
                sp.dma_start(vec[:], io["vec"]).then_inc(vec_in, 16)
                sp.dma_start(masks[:], io["masks"]).then_inc(vec_in, 16)
                prod.load(sp)

            @block.gpsimd
            def _(pool):
                pool.memset(env["eps"][:, 0:1], EPS).then_inc(eps_set, 1)
                pool.memset(env["eps"][:, 1:2], GN_EPS).then_inc(eps_set, 1)

            @block.scalar
            def _(act):
                for c in range(NTC):
                    act.wait_ge(x_in[c], 16)
                act.wait_ge(eps_set, 2)
                norm.scalar(act)

                def evac(p, s):
                    if not (isinstance(p, int) and p == 0):
                        act.wait_ge(stored[s], p * 16)
                    for c in range(NTC):
                        act.wait_ge(prod.ready, (p * 2 + s) * NTC + (c + 1))
                        act.copy(out[s][:, c * TC:(c + 1) * TC], prod.bank[s][c][:, 0:TC]).then_inc(prod.used, 1)
                    act.wait_ge(prod.used, (p * 2 + (s + 1)) * NTC)
                    act.dma_start(io["z"][bass.ds(p * 2 + s, 1)].rearrange("o p t -> (o p) t"), out[s][:]).then_inc(stored[s], 16)
                prod.pipeline(act, prod.split_hi, evac)
                for s in range(2):
                    act.wait_ge(stored[s], 16 * prod.pairs)

            @block.vector
            def _(dve):
                dve.wait_ge(vec_in, 32)
                norm.vector(dve)
                prod.pipeline(dve, prod.split_lo, lambda p, s: None)

            @block.tensor
            def _(pe):
                pe.wait_ge(vec_in, 32)
                norm.tensor(pe)
                pe.wait_ge(norm.rest, KD * NTC)
                prod.products(pe)


def stage_lru(nc, env, io):
    with Stage(nc, "lru") as st:
        banks = st.banks()
        PAD = 3 + SEQ + NB * (3 + NS)
        xp = st.sb("x_padded", [P, KM, PAD])
        ly = st.sb("gate_branch", [P, KM, T])
        xc, r, i_, a, m = (st.sb(n, [P, KM, T]) for n in ("conv", "r", "i", "a", "m"))
        gw = st.sb("gate_w", [P, 2, KM, P])
        h0, hl = st.sb("h0", [P, KM, NB]), st.sb("h_last", [P, KM, NB + 1])
        sp = st.sb("softplus", [P, 8, KM])
        S = st.sem
        V = lambda n, c: env["vec"][:, VAT[n] + c:VAT[n] + c + 1]
        prompt = lambda x, ct, k=0: x[:, ct, k:k + SEQ]
        samples = lambda x, ct: x[:, ct, SEQ:T].rearrange("p (b s) -> p b s", b=NB)
        padded = lambda ct: xp[:, ct, 3 + SEQ:PAD].rearrange("p (b s) -> p b s", b=NB)
        zt = io["z"]
        with nc.Block() as block:
            @block.sync
            def _(eng):
                for ct in range(KM):
                    eng.dma_start(xp[:, ct, 3:3 + SEQ], zt[Z_LX + ct, :, 0:SEQ]).then_inc(S(f"x_in{ct}"), 16)
                    eng.dma_start(padded(ct)[:, :, 3:], zt[Z_LX + ct, :, SEQ:T].rearrange("p (b s) -> p b s", b=NB)).then_inc(S(f"x_in{ct}"), 16)
                    eng.dma_start(padded(ct)[:, :, 0:3], io["lru_conv"][ct]).then_inc(S(f"x_in{ct}"), 16)
                eng.dma_start(gw[:], io["lru_gate_w"]).then_inc(S("gate_w_in"), 16)
                eng.dma_start(h0[:], io["lru_h"]).then_inc(S("h0_in"), 16)
                for ct in range(KM):
                    eng.dma_start(ly[:, ct], zt[Z_LY + ct]).then_inc(S(f"y_in{ct}"), 16)
                for ct in range(KM):
                    eng.wait_ge(S(f"x_in{ct}"), 48)
                    eng.dma_start(io["o_conv_p"][ct], xp[:, ct, SEQ:SEQ + 3]).then_inc(S("stored"), 16)
                    eng.dma_start(io["o_conv_s"][ct], padded(ct)[:, :, NS:NS + 3]).then_inc(S("stored"), 16)
                for ct in range(KM):
                    eng.wait_ge(S("branch_out"), ct + 1)
                    eng.dma_start(io["branch"][0, :, ct], ly[:, ct]).then_inc(S("stored"), 16)
                eng.wait_ge(S("h_last"), 2 * KM)
                eng.dma_start(io["o_h"], hl[:]).then_inc(S("stored"), 16)
                eng.wait_ge(S("stored"), 16 * (3 * KM + 1))

            @block.gpsimd
            def _(pool):
                pool.memset(xp[:, :, 0:3], 0.0).then_inc(S("padding_zero"), 1)
                for ct in range(KM):
                    pool.wait_ge(S("scanned"), ct + 1)
                    pool.tensor_copy(hl[:, ct, 0:1], m[:, ct, SEQ - 1:SEQ]).then_inc(S("h_last"), 1)
                    pool.tensor_copy(hl[:, ct, 1:], samples(m, ct)[:, :, NS - 1]).then_inc(S("h_last"), 1)

            @block.scalar
            def _(act):
                lam = env["vec"][:, VAT["lru_lambda"]:VAT["lru_lambda"] + KM]
                act.activation(sp[:, 0], lam, ACT.Abs).then_inc(S("abs"), 1)
                act.wait_ge(S("abs"), 1)
                act.activation(sp[:, 1], sp[:, 0], ACT.Exp, scale=-1.0).then_inc(S("e"), 1)
                act.wait_ge(S("w"), 1)
                act.activation(sp[:, 3], sp[:, 2], ACT.Ln).then_inc(S("ln"), 1)
                for ct in range(KM):
                    for g, dst in ((0, r), (1, i_)):
                        for c in range(NTC):
                            n = (ct * 2 + g) * NTC + c
                            act.wait_ge(S("gated"), n + 1)
                            act.activation(dst[:, ct, c * TC:(c + 1) * TC], banks[n % 6][:, 0:TC], ACT.Sigmoid,
                                           bias=V("lru_gate_b", g * KM + ct)).then_inc(S("gate"), 1)
                act.wait_ge(S("rate"), 1)
                act.wait_ge(S("gate"), 6 * KM)
                for ct in range(KM):
                    act.activation(a[:, ct], r[:, ct], ACT.Exp, scale=sp[:, 6, ct:ct + 1]).then_inc(S("a"), 1)
                    act.activation(m[:, ct], r[:, ct], ACT.Tanh, scale=sp[:, 5, ct:ct + 1]).then_inc(S("tanh"), 1)
                for ct in range(KM):
                    act.wait_ge(S("square"), ct + 1)
                    act.activation(r[:, ct], m[:, ct], ACT.Sqrt).then_inc(S("mult"), 1)
                for ct in range(KM):
                    act.wait_ge(S(f"y_in{ct}"), 16)
                    act.activation(ly[:, ct], ly[:, ct], ACT.Gelu_apprx_tanh).then_inc(S("gelu"), 1)

            @block.tensor
            def _(pe):
                pe.wait_ge(S("gate_w_in"), 16)
                for ct in range(KM):
                    pe.wait_ge(S("conv"), 2 * (ct + 1))
                    for g in range(2):
                        for c in range(NTC):
                            n = (ct * 2 + g) * NTC + c
                            if n >= 6:
                                pe.wait_ge(S("gate"), n - 5)
                            pe.matmul(banks[n % 6][:, 0:TC], gw[:, g, ct], xc[:, ct, c * TC:(c + 1) * TC],
                                      start=True, stop=True).then_inc(S("gated"), 1)

            @block.vector
            def _(dve):
                steps = [0]

                def link(ins):
                    steps[0] += 1
                    ins.then_inc(S("dve_step"), 1)
                    dve.wait_ge(S("dve_step"), steps[0])
                lam = env["vec"][:, VAT["lru_lambda"]:VAT["lru_lambda"] + KM]
                dve.wait_ge(S("e"), 1)
                dve.tensor_scalar(sp[:, 2], sp[:, 1], 1.0, None, ALU.add).then_inc(S("w"), 1)
                dve.wait_ge(S("w"), 1)
                link(dve.tensor_scalar(sp[:, 4], sp[:, 2], -1.0, None, ALU.add))
                link(dve.tensor_tensor(sp[:, 4], sp[:, 1], sp[:, 4], ALU.subtract))
                link(dve.reciprocal(sp[:, 5], sp[:, 2]))
                link(dve.tensor_tensor(sp[:, 4], sp[:, 4], sp[:, 5], ALU.mult))
                dve.wait_ge(S("ln"), 1)
                link(dve.tensor_tensor(sp[:, 4], sp[:, 4], sp[:, 3], ALU.add))
                link(dve.tensor_scalar(sp[:, 5], lam, -1.0, 0.0, ALU.mult, ALU.max))
                link(dve.tensor_tensor(sp[:, 4], sp[:, 4], sp[:, 5], ALU.add))
                link(dve.tensor_scalar(sp[:, 5], sp[:, 4], 8.0, None, ALU.mult))
                dve.tensor_scalar(sp[:, 6], sp[:, 4], -8.0, None, ALU.mult).then_inc(S("rate"), 1)
                dve.wait_ge(S("padding_zero"), 1)
                for ct in range(KM):
                    dve.wait_ge(S(f"x_in{ct}"), 48)
                    w = lambda k: V("lru_conv_w", k * KM + ct)
                    srcs = (lambda k: xp[:, ct, k:k + SEQ], lambda k: padded(ct)[:, :, k:k + NS])
                    for src, dst in zip(srcs, (prompt(xc, ct), samples(xc, ct))):
                        link(dve.tensor_scalar(dst, src(0), w(0), V("lru_conv_b", ct), ALU.mult, ALU.add))
                        link(dve.scalar_tensor_tensor(out=dst, in0=src(1), scalar=w(1), in1=dst, op0=ALU.mult, op1=ALU.add))
                        link(dve.scalar_tensor_tensor(out=dst, in0=src(2), scalar=w(2), in1=dst, op0=ALU.mult, op1=ALU.add))
                        dve.scalar_tensor_tensor(out=dst, in0=src(3), scalar=w(3), in1=dst, op0=ALU.mult, op1=ALU.add).then_inc(S("conv"), 1)
                for ct in range(KM):
                    dve.wait_ge(S("tanh"), ct + 1)
                    link(dve.tensor_scalar(r[:, ct], m[:, ct], 1.0, None, ALU.add))
                    link(dve.reciprocal(r[:, ct], r[:, ct]))
                    dve.scalar_tensor_tensor(out=m[:, ct], in0=m[:, ct], scalar=2.0, in1=r[:, ct],
                                             op0=ALU.mult, op1=ALU.mult).then_inc(S("square"), 1)
                dve.wait_ge(S("h0_in"), 16)
                for ct in range(KM):
                    link(dve.tensor_tensor(xc[:, ct], xc[:, ct], i_[:, ct], ALU.mult))
                    dve.wait_ge(S("mult"), ct + 1)
                    link(dve.tensor_tensor(xc[:, ct], xc[:, ct], r[:, ct], ALU.mult))
                    dve.wait_ge(S("a"), ct + 1)
                    link(dve.tensor_tensor(h0[:, ct], h0[:, ct], samples(a, ct)[:, :, 0], ALU.mult))
                    link(dve.tensor_tensor(samples(xc, ct)[:, :, 0], samples(xc, ct)[:, :, 0], h0[:, ct], ALU.add))
                    link(dve.memset(samples(a, ct)[:, :, 0], 0.0))
                    dve.tensor_tensor_scan(m[:, ct], a[:, ct], xc[:, ct], 0.0, ALU.mult, ALU.add).then_inc(S("scanned"), 1)
                    dve.wait_ge(S("scanned"), ct + 1)
                    dve.wait_ge(S("gelu"), ct + 1)
                    dve.tensor_tensor(ly[:, ct], ly[:, ct], m[:, ct], ALU.mult).then_inc(S("branch_out"), 1)


def stage_swa(nc, env, io):
    with Stage(nc, "swa") as st:
        banks = st.banks()
        q = st.sb("q", [P, 2, T // CH, 2, CH])
        k2 = st.sb("k", [P, 2, T])
        v = st.sb("v", [P, T])
        sink, sinkq = st.sb("sink", [P, NH]), st.sb("sink_of_row", [P, 4])
        s_ = [st.sb(f"scores{i}", [P, 4, P + 1]) for i in range(3)]
        stat = [st.sb(f"stat{i}", [P, 3, 4]) for i in range(2)]
        pt = [st.sb(f"probs_t{i}", [P, 4, P]) for i in range(2)]
        vt = [st.sb(f"v_t{i}", [P, P]) for i in range(3)]
        ob = st.sb("out", [P, 4, T])
        NK = NS + CH
        kc = st.sb("k_sample", [P, 2, NB, NK])
        vc = st.sb("v_sample", [NK, NB, P])
        qm = st.sb("q_masked", [P, 4, NB, P])
        ss = st.sb("scores_sample", [P, NH, NK + 1])
        sst = st.sb("stat_sample", [P, 3, NH])
        pts = st.sb("probs_t_sample", [NK, NH, P])
        S = st.sem
        ident = env["mask"]("ident")
        SC = HD ** -0.5
        zt = io["z"]
        units = [(g, b) for g in range(2) for b in range(2)]
        with nc.Block() as block:
            @block.sync
            def _(eng):
                for ct in range(4):
                    eng.dma_start(q[:, ct // 2, :, ct % 2], zt[Z_Q + ct].rearrange("p (c t) -> p c t", t=CH)).then_inc(S("qkv_in"), 16)
                eng.dma_start(k2[:, 0], zt[Z_K]).then_inc(S("qkv_in"), 16)
                for b in range(2):
                    eng.dma_start(k2[64 * b:64 * b + 64, 1], zt[Z_K, 64 - 64 * b:128 - 64 * b]).then_inc(S("qkv_in"), 16)
                eng.dma_start(v[:], zt[Z_V]).then_inc(S("qkv_in"), 16)
                eng.dma_start(sink[:], io["sink"].broadcast_to([P, NH])).then_inc(S("qkv_in"), 16)
                eng.dma_start(kc[:, :, :, NS:NK], io["swa_k"]).then_inc(S("cache_in"), 16)
                eng.dma_start(vc[NS:NK], io["swa_v"]).then_inc(S("cache_in"), 16)
                eng.dma_start(io["o_swa_kept"], io["swa_cache"]).then_inc(S("stored"), 16)
                eng.wait_ge(S("qkv_in"), 16 * 9)
                eng.dma_start(io["o_swa_new"][0], k2[:, 0, SEQ - P:T]).then_inc(S("stored"), 16)
                eng.dma_start(io["o_swa_new"][1], v[:, SEQ - P:T]).then_inc(S("stored"), 16)
                eng.wait_ge(S("attended"), NCH)
                eng.wait_ge(S("sample_out"), 2)
                eng.dma_start(io["branch"][1], ob[:]).then_inc(S("stored"), 16)
                eng.wait_ge(S("stored"), 16 * 4)

            @block.gpsimd
            def _(pool):
                pool.memset(qm[:], 0.0).then_inc(S("q_zero"), 1)
                pool.wait_ge(S("q_zero"), 1)
                pool.wait_ge(S("qkv_in"), 16 * 9)
                for b in range(NB):
                    at = b * NS % CH
                    pool.tensor_copy(qm[:, :, b, b * NS:(b + 1) * NS].rearrange("p (g n) t -> p g n t", g=2),
                                     q[:, :, NCH + b * NS // CH, :, at:at + NS]).then_inc(S("q_masked"), 1)
                for n in range(2):
                    pool.tensor_copy(kc[:, n, :, 0:NS], k2[:, n, SEQ:T].rearrange("p (b s) -> p b s", b=NB)).then_inc(S("k_new"), 1)

            @block.tensor
            def _(pe):
                pe.wait_ge(S("qkv_in"), 16 * 9)
                def keys_of(c):
                    return max(c - 1, 0) * CH, CH * min(c + 1, 2)

                def scores(c):
                    lo, nk = keys_of(c)
                    bs = banks[0:2]
                    if c:
                        pe.wait_ge(S("scored"), 2 * c)
                    for g, b in units:
                        kk = k2[64 * b:64 * b + 64, 0 if b == g else 1, lo:lo + nk]
                        qq = q[64 * b:64 * b + 64, g, c].rearrange("p n t -> p (n t)")
                        mm = pe.matmul(bs[b][:, g * P:g * P + nk], qq, kk, start=True, stop=True, skip_group_check=True)
                    mm.then_inc(S("scores"), 1)
                    if c >= 1:
                        pe.wait_ge(S("v_turned_copied"), c)
                    pe.transpose(banks[2][0:nk, 0:P], v[:, lo:lo + nk], ident).then_inc(S("v_turned"), 1)

                def turn_probs(c):
                    nk = keys_of(c)[1]
                    pe.wait_ge(S("probs"), c + 1)
                    if c:
                        pe.wait_ge(S("probs_t"), c)
                    for n in range(4):
                        mm = pe.transpose(banks[3][0:nk, n * P:(n + 1) * P], s_[c % 3][:, n, 0:nk], ident)
                    mm.then_inc(S("probs_turned"), 1)

                def weigh(c):
                    nk = keys_of(c)[1]
                    pe.wait_ge(S("probs_t"), c + 1)
                    pe.wait_ge(S("v_turned_copied"), c + 1)
                    if c:
                        pe.wait_ge(S("attended"), c)
                    for n, (g, b) in enumerate(units):
                        mm = pe.matmul(banks[4 + g][64 * b:64 * b + 64, 0:P], vt[c % 3][0:nk, g * HD:(g + 1) * HD],
                                       pt[c % 2][0:nk, n, :], start=True, stop=True, skip_group_check=True)
                    mm.then_inc(S("weighted"), 1)

                for i in range(NCH + 2):
                    if i < NCH:
                        scores(i)
                    if i >= 2:
                        turn_probs(i - 2)
                        weigh(i - 2)
                pe.wait_ge(S("q_masked"), NB)
                pe.wait_ge(S("k_new"), 2)
                pe.wait_ge(S("cache_in"), 32)
                for h in range(NH):
                    g, b = h // 4, h % 2
                    for s in range(NB):
                        mm = pe.matmul(banks[6 + b][:, (h // 2) * NK:(h // 2 + 1) * NK], qm[64 * b:64 * b + 64, h // 2, s, :],
                                       kc[64 * b:64 * b + 64, 0 if b == g else 1, s, :], start=(s == 0), stop=(s == NB - 1),
                                       skip_group_check=True)
                mm.then_inc(S("scores_sample"), 1)
                pe.wait_ge(S("v_turned_copied"), NCH)
                for s in range(NB):
                    if s:
                        pe.wait_ge(S("v_sample_copied"), s)
                    pe.transpose(banks[2][0:NS, 0:P], v[:, SEQ + s * NS:SEQ + (s + 1) * NS], ident).then_inc(S("v_sample_turned"), 1)
                pe.wait_ge(S("probs_sample"), 1)
                for n in range(2):
                    pe.wait_ge(S("probs_t_sample") if n else S("probs_t"), n or NCH)
                    for h in range(4 * n, 4 * n + 4):
                        mm = pe.transpose(banks[3][0:NK, (h % 4) * P:(h % 4 + 1) * P], ss[:, h, 0:NK], ident)
                    mm.then_inc(S("probs_turned_sample"), 1)
                pe.wait_ge(S("probs_t_sample"), 2)
                pe.wait_ge(S("v_sample_copied"), NB)
                pe.wait_ge(S("attended"), NCH)
                for g in range(2):
                    for b in range(2):
                        for s in range(NB):
                            mm = pe.matmul(banks[4 + g][64 * b:64 * b + 64, s * 2 * NS:(s + 1) * 2 * NS], vc[:, s, g * HD:(g + 1) * HD],
                                           pts[:, 4 * g + b:4 * g + b + 3:2, s * NS:(s + 1) * NS],
                                           start=True, stop=True, skip_group_check=True)
                mm.then_inc(S("weighted_sample"), 1)

            @block.scalar
            def _(act):
                for i in range(NCH + 2):
                    if i < NCH:
                        nk = CH * min(i + 1, 2)
                        act.wait_ge(S("v_turned"), i + 1)
                        if i >= 3:
                            act.wait_ge(S("weighted"), i - 2)
                        act.copy(vt[i % 3][0:nk, :], banks[2][0:nk, 0:P]).then_inc(S("v_turned_copied"), 1)
                    if i >= 2:
                        c = i - 2
                        nk = CH * min(c + 1, 2)
                        act.wait_ge(S("probs_turned"), c + 1)
                        if c >= 2:
                            act.wait_ge(S("weighted"), c - 1)
                        act.copy(pt[c % 2][0:nk], banks[3][0:nk, :].rearrange("p (n t) -> p n t", n=4)).then_inc(S("probs_t"), 1)
                    if i < NCH:
                        nk = CH * min(i + 1, 2)
                        act.wait_ge(S("centred"), i + 1)
                        n = nk if i == 0 else P + 1
                        act.activation(s_[i % 3][:, :, 0:n], s_[i % 3][:, :, 0:n], ACT.Exp).then_inc(S("exp"), 1)
                        if i == 0:
                            act.activation(s_[0][:, :, P:P + 1], s_[0][:, :, P:P + 1], ACT.Exp).then_inc(S("exp_sink0"), 1)
                act.wait_ge(S("cache_in"), 32)
                for s in range(NB):
                    act.wait_ge(S("v_sample_turned"), s + 1)
                    act.copy(vc[0:NS, s, :], banks[2][0:NS, 0:P]).then_inc(S("v_sample_copied"), 1)
                act.wait_ge(S("centred_sample"), 1)
                act.activation(ss[:], ss[:], ACT.Exp).then_inc(S("exp_sample"), 1)
                for n in range(2):
                    act.wait_ge(S("probs_turned_sample"), n + 1)
                    act.copy(pts[:, 4 * n:4 * n + 4], banks[3][0:NK, :].rearrange("p (n t) -> p n t", n=4)).then_inc(S("probs_t_sample"), 1)

            @block.vector
            def _(dve):
                steps = [0]

                def link(ins):
                    steps[0] += 1
                    ins.then_inc(S("dve_step"), 1)
                    dve.wait_ge(S("dve_step"), steps[0])
                dve.wait_ge(S("qkv_in"), 16 * 9)
                for n, (g, b) in enumerate(units):
                    for half in range(2):
                        h = 4 * g + 2 * half + b
                        link(dve.tensor_copy(sinkq[64 * half:64 * half + 64, n:n + 1], sink[64 * half:64 * half + 64, h:h + 1]))
                def centre(c):
                    nk = CH * min(c + 1, 2)
                    x, z = s_[c % 3], stat[c % 2]
                    dve.wait_ge(S("scores"), c + 1)
                    if c >= 3:
                        dve.wait_ge(S("probs_turned"), c - 2)
                    for b in range(2):
                        dve.tensor_scalar(x[:, b::2, 0:nk], banks[b][:, 0:2 * P].rearrange("p (g k) -> p g k", g=2)[:, :, 0:nk],
                                          SC, None, ALU.mult).then_inc(S("scored"), 1)
                    dve.tensor_copy(x[:, :, P], sinkq[:]).then_inc(S("sink_put"), 1)
                    dve.wait_ge(S("scored"), 2 * c + 2)
                    dve.wait_ge(S("sink_put"), c + 1)
                    link(dve.tensor_reduce(z[:, 0], x[:, :, 0:nk], AX.X, ALU.max))
                    link(dve.tensor_tensor(z[:, 0], z[:, 0], sinkq[:], ALU.max))
                    m = z[:, 0].rearrange("p (n o) -> p n o", o=1)
                    if c == 0:
                        link(dve.tensor_tensor(x[:, :, P:P + 1], x[:, :, P:P + 1], m, ALU.subtract))
                        dve.tensor_tensor(x[:, :, 0:nk], x[:, :, 0:nk], m.broadcast_to([P, 4, nk]), ALU.subtract).then_inc(S("centred"), 1)
                    else:
                        dve.tensor_tensor(x[:], x[:], m.broadcast_to([P, 4, P + 1]), ALU.subtract).then_inc(S("centred"), 1)

                def normalise(c):
                    nk = CH * min(c + 1, 2)
                    x, z = s_[c % 3], stat[c % 2]
                    if c == 0:
                        dve.wait_ge(S("exp_sink0"), 1)
                    dve.wait_ge(S("exp"), c + 1)
                    link(dve.tensor_reduce(z[:, 1], x[:, :, 0:nk], AX.X, ALU.add))
                    link(dve.tensor_tensor(z[:, 1], z[:, 1], x[:, :, P], ALU.add))
                    link(dve.reciprocal(z[:, 2], z[:, 1]))
                    dve.tensor_tensor(x[:, :, 0:nk], x[:, :, 0:nk], z[:, 2].rearrange("p (n o) -> p n o", o=1).broadcast_to([P, 4, nk]),
                                      ALU.mult).then_inc(S("probs"), 1)

                for i in range(NCH + 3):
                    if i < NCH:
                        centre(i)
                    if 1 <= i <= NCH:
                        normalise(i - 1)
                    if i >= 3:
                        c = i - 3
                        dve.wait_ge(S("weighted"), c + 1)
                        for g in range(2):
                            o = dve.tensor_copy(ob[:, 2 * g:2 * g + 2, c * CH:(c + 1) * CH],
                                                banks[4 + g][:, 0:P].rearrange("p (n t) -> p n t", n=2))
                        o.then_inc(S("attended"), 1)
                dve.wait_ge(S("scores_sample"), 1)
                for b in range(2):
                    link(dve.tensor_scalar(ss[:, b::2, 0:NK], banks[6 + b][:, 0:4 * NK].rearrange("p (n k) -> p n k", n=4), SC, None, ALU.mult))
                link(dve.tensor_copy(ss[:, :, NK], sink[:]))
                link(dve.tensor_reduce(sst[:, 0], ss[:], AX.X, ALU.max))
                up = lambda x, n: x.rearrange("p (n o) -> p n o", o=1).broadcast_to([P, NH, n])
                dve.tensor_tensor(ss[:], ss[:], up(sst[:, 0], NK + 1), ALU.subtract).then_inc(S("centred_sample"), 1)
                dve.wait_ge(S("exp_sample"), 1)
                link(dve.tensor_reduce(sst[:, 1], ss[:], AX.X, ALU.add))
                link(dve.reciprocal(sst[:, 2], sst[:, 1]))
                dve.tensor_tensor(ss[:, :, 0:NK], ss[:, :, 0:NK], up(sst[:, 2], NK), ALU.mult).then_inc(S("probs_sample"), 1)
                dve.wait_ge(S("weighted_sample"), 1)
                for g in range(2):
                    dve.tensor_copy(ob[:, 2 * g:2 * g + 2, SEQ:T].rearrange("p n (s t) -> p s n t", s=NB),
                                    banks[4 + g][:, 0:NB * 2 * NS].rearrange("p (s n t) -> p s n t", s=NB, n=2)).then_inc(S("sample_out"), 1)


def stage_rwkv(nc, env, io):
    with Stage(nc, "rwkv") as st:
        banks = st.banks()
        W4 = KM * P
        t4 = [P, KM, P]
        z = [st.sb(f"z{i}", [P, NRW, P + 1]) for i in range(2)]
        HR = NRW // 2
        dz = st.sb("z_difference", [P, HR, P])
        shift = st.sb("shift_state", [P, NRW, NB])
        zlast = st.sb("z_last", [P, NRW, NB + 1])
        w2, a2, g2 = (st.sb(n, [P, MIX]) for n in ("w2", "a2", "g2"))
        wl, gl = st.sb("tanh_w_and_a", [P, P]), st.sb("sig_g", [P, P])
        names = ["sw", "asig", "c", "cprev", "Pi", "kk", "sq", "B", "K", "kh", "rk"]
        (sw, asig, c_, cprev, Pi, kk, sq, B, K, kh, rk) = (st.sb(n, t4) for n in names)
        Pp, Pv, nrm = c_, cprev, sq
        two = lambda name, shape: [st.sb(f"{name}_{i}", shape) for i in range(2)]
        three = lambda name, shape: [st.sb(f"{name}_{i}", shape) for i in range(3)]
        AR = three("AR", [P, KM, 2, P])
        Bt, Kt, Vt = (three(n, [P, W4]) for n in ("B_tok", "K_tok", "V_tok"))
        GO, BO = ([st.sb(f"{name}_{i}", t4) for i in range(4)] for name in ("gate", "bonus"))
        pend = three("decay_end", [P, KM, 2])
        Z1 = two("LakV", [P, W4])
        MrbT, MrkT, TiT = ([two(f"{n}{i}", t4) for i in range(2)] for n in ("MrbT", "MrkT", "TT"))
        Bs, Ks = two("B_side", t4), two("K_side", t4)
        OT = two("o", t4)
        L, Ti, O_, Zm, LakT = (two(n, t4) for n in ("L", "T", "O", "Z", "LakT"))
        Pcm = st.sb("decay_diag", t4)
        X, U = st.sb("X", [P, W4]), st.sb("U", [P, W4])
        dev2 = dev = st.sb("dev", t4)
        Sbd, Stmp = st.sb("state", t4), st.sb("state_sum", t4)
        S0bd, S0c = st.sb("state0_diag", [P, NB, KM, P]), st.sb("state0", [P, KM, NB, HD])
        X0T = Zm[0]
        Um = S0bd[:].rearrange("p b k v -> p b (k v)")
        S = st.sem
        mask, vec = env["mask"], env["vec"]
        ident, head = mask("ident"), mask("head")
        vb = lambda n, k, cols=P, k0=0: vec[:, VAT[n] + k0:VAT[n] + k0 + k].rearrange("p (k o) -> p k o", o=1).broadcast_to([P, k, cols])
        vb1 = lambda n, k: vec[:, VAT[n] + k:VAT[n] + k + 1]
        mb = lambda n, k=KM: mask(n).rearrange("p (o t) -> p o t", o=1).broadcast_to([P, k, P])
        bank4 = lambda i: banks[i][:].rearrange("p (n t) -> p n t", n=KM)
        flat = lambda x: x.rearrange("p n t -> p (n t)")
        zt = io["z"]
        rows = lambda s: slice(64 * s, 64 * s + 64)
        heads = [(p, s, slice((2 * p + s) * HD, (2 * p + s + 1) * HD), slice(p * P, (p + 1) * P)) for p in range(KM) for s in range(2)]
        LAST = TT - 1
        SBANK = (0, 1, 4, 5)
        PREP = 6
        zs = lambda u: z[u % 2][:, :, 1:P + 1]
        ROUNDS = range(-1, TT + 2)
        is_tile = lambda i: 0 <= i < TT

        def levels(t):
            return [n for n in (4, 8, 16, 32, 64) if n <= (CH if t < LAST else NS)] if is_tile(t) else []
        merges = [sum(len(levels(u)) for u in range(t)) for t in range(TT + 1)]
        written = lambda t: sum(4 * len(levels(u)) + 2 for u in range(t))

        with nc.Block() as block:
            @block.sync
            def _(eng):
                def load_z(u):
                    lo = u * P
                    first = 1 if u in (0, LAST) else 0
                    eng.dma_start(z[u % 2][:, :, first:P + 1], zt[Z_RW:Z_G, :, lo - 1 + first:lo + P].rearrange("n p t -> p n t")).then_inc(S(f"z_in{u % 2}"), 16)

                def store_branch(n):
                    eng.wait_ge(S("branch_out"), n + 1)
                    eng.dma_start(io["branch"][2, :, :, n * P:(n + 1) * P], OT[n % 2][:]).then_inc(S(f"out_stored{n % 2}"), 16)

                load_z(0)
                load_z(1)
                eng.dma_start(w2[0:64, :], io["w2a2"][0:64]).then_inc(S("weights_in"), 16)
                eng.dma_start(a2[64:128, :], io["w2a2"][64:128]).then_inc(S("weights_in"), 16)
                eng.dma_start(g2[:], io["g2"]).then_inc(S("weights_in"), 16)
                eng.dma_start(shift[:], io["shift"]).then_inc(S("shift_in"), 16)
                eng.dma_start(S0bd[:], io["s0_diag"]).then_inc(S("state0_in"), 16)
                eng.dma_start(S0c[:], io["s0"]).then_inc(S("state0_in"), 16)
                for r in ROUNDS:
                    u, n = r + 1, r - 2
                    if is_tile(u + 2):
                        eng.wait_ge(S("lora_in"), 3 * u + 3)
                        eng.wait_ge(S("kh"), u + 1)
                        eng.wait_ge(S("rrk"), u + 1)
                        eng.wait_ge(S("AR"), 2 * u + 2)
                        eng.wait_ge(S("bonus_out"), u + 1)
                        eng.wait_ge(S("tok"), 3 * u + 1)
                        load_z(u + 2)
                    if is_tile(n):
                        store_branch(n)
                    if u == LAST:
                        eng.wait_ge(S("z_last"), 2)
                        eng.dma_start(io["o_shift"], zlast[:]).then_inc(S("stored"), 16)
                eng.wait_ge(S("state"), NCH)
                eng.dma_start(io["o_state_p"], Sbd[:]).then_inc(S("stored"), 16)
                eng.wait_ge(S("state_sample"), KM)
                eng.dma_start(io["o_state_s"], S0c[:]).then_inc(S("stored"), 16)
                eng.wait_ge(S("stored"), 16 * 3)
                for slot in range(2):
                    eng.wait_ge(S(f"out_stored{slot}"), 16 * ((TT + 1 - slot) // 2))

            @block.gpsimd
            def _(pool):
                tt = pool.tensor_tensor
                steps = [0]

                def link(ins):
                    steps[0] += 1
                    ins.then_inc(S("pool_step"), 1)
                    pool.wait_ge(S("pool_step"), steps[0])

                def shifted(u, h):
                    zz, f = z[u % 2], slice(h * HR, (h + 1) * HR)
                    if h == 0:
                        pool.wait_ge(S(f"z_in{u % 2}"), 16 * (u // 2 + 1))
                        if u == 0:
                            pool.wait_ge(S("z_start"), 1)
                        if u == LAST - 1:
                            pool.tensor_copy(zlast[:, :, 0:1], zz[:, :, P:P + 1]).then_inc(S("z_last"), 1)
                        if u == LAST:
                            pool.tensor_copy(zlast[:, :, 1:], zz[:, :, NS:P + 1:NS]).then_inc(S("z_last"), 1)
                        if u >= LAST - 1:
                            pool.wait_ge(S("z_last"), u - LAST + 2)
                    link(tt(dz[:], zz[:, f, 0:P], zz[:, f, 1:P + 1], ALU.subtract))
                    if u == LAST:
                        pool.wait_ge(S("shift_in"), 16)
                        link(tt(dz[:, :, 0:P:NS], shift[:, f], zz[:, f, 1:P + 1:NS], ALU.subtract))
                    link(tt(dz[:], dz[:], vb("rwkv_mu", HR, k0=h * HR), ALU.mult))
                    mixed = tt(zz[:, f, 1:P + 1], dz[:], zz[:, f, 1:P + 1], ALU.add)
                    mixed.then_inc(S("zs"), 1)
                    pool.wait_ge(S("zs"), 2 * u + h + 1)

                def decay_diag(b, c):
                    if b or c:
                        pool.wait_ge(S("state"), 2 * b + c)
                    pool.wait_ge(S("pend"), b + 1)
                    tt(Pcm[:], mb("head"), pend[b % 3][:, :, c:c + 1].broadcast_to(t4), ALU.mult).then_inc(S("decay_end"), 1)

                def off_blocks(t, i):
                    for s in range(2):
                        at = merges[t] + i
                        pool.wait_ge(S("L"), 2 * t + s + 1)
                        if at:
                            pool.wait_ge(S("Z"), 2 * (at - 1) + s + 1)
                        tt(O_[s][:], L[s][:], mb(f"off{levels(t)[i]}"), ALU.mult).then_inc(S("O"), 1)

                pool.memset(z[0][:, :, 0:1], 0.0).then_inc(S("z_start"), 1)
                shifted(0, 0)
                shifted(0, 1)
                halves = [w2[64:128], a2[0:64]] + [x[s][rows(1 - s)] for x in (Ks, Bs) for s in range(2)]
                for i, x in enumerate(halves):
                    pool.memset(x, 0.0).then_inc(S("zeros"), 1)
                    pool.wait_ge(S("zeros"), i + 1)
                pool.memset(Sbd[:], 0.0).then_inc(S("state_zero"), 1)
                for r in range(-1, TT + 3):
                    t, u, b, last = r, r + 1, r - 1, r - 3
                    nl = len(levels(t))
                    serial = 0 <= b < LAST
                    if nl:
                        off_blocks(t, 0)
                    if is_tile(last):
                        o = OT[last % 2]
                        pool.wait_ge(S("affine"), KM * (last + 1))
                        pool.wait_ge(S("bonus_out"), last + 1)
                        pool.wait_ge(S("g"), last + 1)
                        link(tt(o[:], o[:], BO[last % 4][:], ALU.add))
                        tt(o[:], o[:], GO[last % 4][:], ALU.mult).then_inc(S("branch_out"), 1)
                    if serial:
                        decay_diag(b, 0)
                    if nl:
                        off_blocks(t, 1)
                    if is_tile(u):
                        if u:
                            pool.wait_ge(S("bonus"), u)
                        tt(rk[:], zs(u)[:, 0:KM], vb("rwkv_r_k", KM), ALU.mult).then_inc(S("rrk"), 1)
                        pool.wait_ge(S("rrk"), u + 1)
                        pool.wait_ge(S("kh"), u + 1)
                        tt(rk[:], rk[:], kh[:], ALU.mult).then_inc(S("rk"), 1)
                    if nl > 2:
                        off_blocks(t, 2)
                    if serial:
                        decay_diag(b, 1)
                    if u < LAST:
                        pool.wait_ge(S("P"), 3 * u + 2)
                        pool.tensor_copy(pend[u % 3][:], Pp[:, :, CH - 1:P:CH]).then_inc(S("pend"), 1)
                    if nl > 3:
                        off_blocks(t, 3)
                    if is_tile(u + 1):
                        shifted(u + 1, 0)
                    if nl > 4:
                        off_blocks(t, 4)
                    if is_tile(u + 1):
                        shifted(u + 1, 1)

            @block.scalar
            def _(act):
                def lora_inputs(u):
                    act.wait_ge(S("zs"), 2 * u + 2)
                    if u:
                        act.wait_ge(S("lora"), 3 * u)
                    act.activation(wl[0:64, :], zs(u)[0:64, 12, :], ACT.Tanh).then_inc(S("lora_in"), 1)
                    act.activation(gl[:], zs(u)[:, 13, :], ACT.Sigmoid).then_inc(S("lora_in"), 1)
                    act.copy(wl[64:128, :], zs(u)[64:128, 12, :]).then_inc(S("lora_in"), 1)

                def copy_u(b, c):
                    act.wait_ge(S("U"), 2 * b + c + 1)
                    act.copy(U[rows(c), :], banks[0][rows(c), :]).then_inc(S("U_copied"), 1)

                def copy_z(t, i):
                    for s in range(2):
                        act.wait_ge(S("Z"), 2 * (merges[t] + i) + s + 1)
                        act.copy(flat(Zm[s][:]), banks[2 + s][:]).then_inc(S("Z_copied"), 1)

                def copy_l(t, s):
                    act.wait_ge(S("grams"), 4 * t + 2 * s + 2)
                    act.copy(flat(L[s][:]), banks[2][:]).then_inc(S("L"), 1)

                def copy_tokens(u, n, dst):
                    act.wait_ge(S("tok"), 3 * u + n + 1)
                    if u >= 3:
                        act.wait_ge(S("O_sum"), u - 2)
                    act.copy(dst[u % 3][:], banks[PREP][:]).then_inc(S("tok_copied"), 1)

                def sides(src, dst, ready, u):
                    act.wait_ge(ready, u + 1)
                    if u:
                        act.wait_ge(S("grams"), 4 * u)
                    for s in range(2):
                        act.copy(dst[s][rows(s)], src[rows(s)]).then_inc(S("sides"), 1)

                def deviation2(n):
                    act.wait_ge(S("centred"), n + 1)
                    act.activation(dev2[:], OT[n % 2][:], ACT.Square).then_inc(S("dev2"), 1)

                def deviation(n):
                    act.wait_ge(S("var"), n + 1)
                    act.activation(flat(dev[:]), banks[1 if n < LAST else 2][:], ACT.Sqrt, scale=1.0 / HD,
                                   bias=env["eps"][:, 1:2]).then_inc(S("dev"), 1)

                act.wait_ge(S("zeros"), 6)
                for r in ROUNDS:
                    t, u, b, n = r, r + 1, r - 1, r - 2
                    nl, prep, serial, norm = len(levels(t)), is_tile(u), 0 <= b < LAST, is_tile(n)
                    if prep:
                        lora_inputs(u)
                    if nl:
                        copy_l(t, 0)
                    if norm:
                        deviation2(n)
                    if prep:
                        act.wait_ge(S("kk"), u + 1)
                        act.activation(sq[:], kk[:], ACT.Square).then_inc(S("sq"), 1)
                    if nl:
                        copy_l(t, 1)
                    if norm:
                        deviation(n)
                    if b == LAST:
                        act.wait_ge(S("X0T"), 1)
                        act.copy(flat(X0T[:]), banks[3][:]).then_inc(S("X0T_copied"), 1)
                        act.wait_ge(S("U"), NCH + 1)
                        act.copy(U[:], banks[6][:]).then_inc(S("U_copied"), 1)
                    if nl:
                        copy_z(t, 0)
                    if serial:
                        copy_u(b, 0)
                    if prep:
                        act.wait_ge(S("wa"), 2 * u + 1)
                        act.activation(sw[:], sw[:], ACT.Sigmoid).then_inc(S("sw"), 1)
                        act.wait_ge(S("wa"), 2 * u + 2)
                        act.activation(asig[:], asig[:], ACT.Sigmoid).then_inc(S("asig"), 1)
                    if nl:
                        copy_z(t, 1)
                    if prep:
                        act.wait_ge(S("lora"), 3 * u + 3)
                        if u >= 4:
                            act.wait_ge(S("branch_out"), u - 3)
                        act.copy(GO[u % 4][:], bank4(PREP)).then_inc(S("g"), 1)
                        act.wait_ge(S("norm2"), u + 1)
                        act.activation(flat(nrm[:]), banks[PREP][:], ACT.Sqrt).then_inc(S("norm"), 1)
                        act.wait_ge(S("cprev"), u + 1)
                        if u:
                            act.wait_ge(S("B"), u)
                        act.activation(Pi[:], c_[:], ACT.Exp, scale=DEC).then_inc(S("P"), 1)
                        act.activation(Pp[:], c_[:], ACT.Exp, scale=-DEC).then_inc(S("P"), 1)
                        act.activation(Pv[:], cprev[:], ACT.Exp, scale=-DEC).then_inc(S("P"), 1)
                    if nl > 2:
                        copy_z(t, 2)
                    if prep:
                        copy_tokens(u, 0, Vt)
                    if nl > 3:
                        copy_z(t, 3)
                    if serial:
                        copy_u(b, 1)
                    if prep:
                        copy_tokens(u, 1, Kt)
                        sides(K, Ks, S("K"), u)
                    if nl > 4:
                        copy_z(t, 4)
                    if prep:
                        sides(B, Bs, S("B"), u)
                        copy_tokens(u, 2, Bt)
                    if is_tile(b):
                        act.wait_ge(S("O_sum"), b + 1)
                        if b >= 2:
                            act.wait_ge(S(f"out_stored{b % 2}"), 16 * (b // 2))
                        act.copy(OT[b % 2][:], bank4(7)).then_inc(S("o"), 1)
                    if norm:
                        act.wait_ge(S("normed"), n + 1)
                        for ct in range(KM):
                            o = OT[n % 2][:, ct]
                            act.activation(o, o, ACT.Identity, scale=vb1("rwkv_ln_w", ct), bias=vb1("rwkv_ln_b", ct)).then_inc(S("affine"), 1)

            @block.vector
            def _(dve):
                steps = [0]

                def link(ins):
                    steps[0] += 1
                    ins.then_inc(S("dve_step"), 1)
                    dve.wait_ge(S("dve_step"), steps[0])
                tt, stt = dve.tensor_tensor, dve.scalar_tensor_tensor

                def add_x(b, c):
                    dve.wait_ge(S("X"), 2 * b + c + 1)
                    tt(X[rows(c), :], banks[0][rows(c), :], Z1[b % 2][rows(c), :], ALU.add).then_inc(S("X_added"), 1)

                def new_state(b, c):
                    n = 2 * b + c
                    dve.wait_ge(S("S_update"), n + 1)
                    dve.wait_ge(S("decay_end"), n + 1)
                    if n == 0:
                        dve.wait_ge(S("state_zero"), 1)
                    link(tt(flat(Stmp[:]), banks[1][:], flat(Sbd[:]), ALU.add))
                    tt(Sbd[:], Stmp[:], Pcm[:], ALU.mult).then_inc(S("state"), 1)

                def merge(t, i):
                    TT_ = TiT[t % 2]
                    for s in range(2):
                        dve.wait_ge(S("merged"), 2 * (merges[t] + i) + s + 1)
                        tt(flat(TT_[s][:]), banks[4 + s][:], flat(TT_[s][:]), ALU.add).then_inc(S("T"), 1)
                        if i < len(levels(t)) - 1:
                            tt(flat(Ti[s][:]), banks[2 + s][:], flat(Ti[s][:]), ALU.add).then_inc(S("T"), 1)

                def masked(t, s):
                    up, q = "16" if t == LAST else "64", t % 2
                    half_of = lambda i: banks[i][:].rearrange("p (n w t) -> p n w t", n=2, w=2)
                    for half in range(2):
                        dve.wait_ge(S("grams"), 4 * t + 2 * s + half + 1)
                        b1, b2 = half_of(3 + half), half_of(5 + half)
                        two_ = slice(2 * half, 2 * half + 2)
                        tt(TiT[q][s][:, two_], b1[:, :, 0], mb("off2T", 2), ALU.mult).then_inc(S("masked"), 1)
                        tt(MrbT[q][s][:, two_], b1[:, :, 1], mb("upI" + up, 2), ALU.mult).then_inc(S("masked"), 1)
                        tt(LakT[s][:, two_], b2[:, :, 0], mb("upS" + up, 2), ALU.mult).then_inc(S("masked"), 1)
                        tt(MrkT[q][s][:, two_], b2[:, :, 1], mb("upI" + up, 2), ALU.mult).then_inc(S("masked"), 1)
                    dve.wait_ge(S("masked"), 16 * t + 8 * s + 8)
                    tt(TiT[q][s][:], TiT[q][s][:], mb("ident"), ALU.add).then_inc(S("T"), 1)
                    dve.wait_ge(S("L"), 2 * t + s + 1)
                    link(tt(Ti[s][:], L[s][:], mb("off2"), ALU.mult))
                    tt(Ti[s][:], Ti[s][:], mb("ident"), ALU.add).then_inc(S("T"), 1)

                def lora_part(u, part, dst, bias):
                    dve.wait_ge(S("lora"), 3 * u + part + 1)
                    tt(dst[:], bank4(PREP), vb(bias, KM), ALU.add).then_inc(S("wa"), 1)

                dve.wait_ge(S("weights_in"), 48)
                for r in ROUNDS:
                    t, u, b, n = r, r + 1, r - 1, r - 2
                    nl, prep, serial, norm = len(levels(t)), is_tile(u), 0 <= b < LAST, is_tile(n)
                    q3 = u % 3
                    sample = u == LAST
                    if prep:
                        rr, k, v = (zs(u)[:, 4 * i:4 * i + 4] for i in range(3))
                        dve.wait_ge(S("zs"), 2 * u + 2)
                        if u:
                            dve.wait_ge(S("B"), u)
                        tt(kk[:], k, vb("rwkv_k_k", KM), ALU.mult).then_inc(S("kk"), 1)
                    if norm:
                        o = OT[n % 2]
                        dve.wait_ge(S("mean"), n + 1)
                        stt(out=flat(o[:]), in0=banks[0 if n < LAST else 3][:], scalar=-1.0 / HD, in1=flat(o[:]),
                            op0=ALU.mult, op1=ALU.add).then_inc(S("centred"), 1)
                    if nl:
                        masked(t, 0)
                    if serial:
                        add_x(b, 0)
                    if nl:
                        masked(t, 1)
                        dve.wait_ge(S("Z1"), t + 1)
                        dve.tensor_copy(Z1[t % 2][:], banks[PREP][:]).then_inc(S("Z1_copied"), 1)
                    if b == LAST:
                        dve.wait_ge(S("X"), NCH + 1)
                        tt(X[:], banks[4][:], Z1[b % 2][:], ALU.add).then_inc(S("X_added"), 1)
                        dve.wait_ge(S("U_copied"), NCH + 1)
                        for part, src in enumerate((U, Vt[b % 3])):
                            if part:
                                dve.wait_ge(S("S_update"), NCH + 1)
                            for s in range(NB):
                                dve.tensor_scalar(Um[:, s, :], src[:], env["sample_rows"][:, s:s + 1], None, ALU.mult).then_inc(S("row_masked"), 1)
                        dve.wait_ge(S("S_update"), NCH + 2)
                        for ct in range(KM):
                            bk = banks[SBANK[ct]][:].rearrange("p (b v) -> p b v", b=NB)
                            link(tt(S0c[:, ct], S0c[:, ct], bk, ALU.add))
                            tt(S0c[:, ct], S0c[:, ct], Pp[:, ct, NS - 1:P:NS].rearrange("p (b o) -> p b o", o=1).broadcast_to([P, NB, HD]),
                               ALU.mult).then_inc(S("state_sample"), 1)
                    if prep:
                        lora_part(u, 0, sw, "rwkv_w0")
                    if nl:
                        merge(t, 0)
                    if prep:
                        lora_part(u, 1, asig, "rwkv_a0")
                        dve.wait_ge(S("sw"), u + 1)
                        if 0 < u:
                            dve.wait_ge(S("pend"), u)
                        link(dve.tensor_tensor_scan(flat(c_[:]), env["resets"][1 if sample else 0], flat(sw[:]), 0.0, ALU.mult, ALU.add))
                        tt(cprev[:], c_[:], sw[:], ALU.subtract).then_inc(S("cprev"), 1)
                    if serial:
                        new_state(b, 0)
                    if prep:
                        dve.wait_ge(S("asig"), u + 1)
                        if u:
                            dve.wait_ge(S("rk"), u)
                            dve.wait_ge(S("K"), u)
                        link(stt(out=kh[:], in0=asig[:], scalar=-1.0, in1=vb("rwkv_k_a", KM), op0=ALU.add, op1=ALU.mult))
                        stt(out=kh[:], in0=kh[:], scalar=1.0, in1=k, op0=ALU.add, op1=ALU.mult).then_inc(S("kh"), 1)
                    if nl:
                        merge(t, 1)
                    if serial:
                        add_x(b, 1)
                    if nl > 2:
                        merge(t, 2)
                    if prep:
                        dve.wait_ge(S("bonus"), u + 1)
                        if u >= 4:
                            dve.wait_ge(S("branch_out"), u - 3)
                        tt(BO[u % 4][:], bank4(PREP), v, ALU.mult).then_inc(S("bonus_out"), 1)
                        dve.wait_ge(S("P"), 3 * u + 3)
                        dve.wait_ge(S("kh"), u + 1)
                        if u:
                            dve.wait_ge(S("sides"), 4 * u)
                            dve.wait_ge(S("tok_copied"), 3 * u)
                        tt(K[:], kh[:], Pi[:], ALU.mult).then_inc(S("K"), 1)
                        if u >= 3:
                            dve.wait_ge(S("O_sum"), u - 2)
                        tt(AR[q3][:, :, 1, :], rr, Pp[:], ALU.mult).then_inc(S("AR"), 1)
                        dve.wait_ge(S("norm"), u + 1)
                        link(dve.tensor_scalar(nrm[:], nrm[:], 1e-12, None, ALU.max))
                        link(dve.reciprocal(nrm[:], nrm[:]))
                        dve.wait_ge(S("sq"), u + 1)
                        link(tt(kk[:], kk[:], nrm[:], ALU.mult))
                    if nl > 3:
                        merge(t, 3)
                    if prep:
                        stt(out=AR[q3][:, :, 0, :], in0=kk[:], scalar=-1.0, in1=Pv[:], op0=ALU.mult, op1=ALU.mult).then_inc(S("AR"), 1)
                        dve.wait_ge(S("AR"), 2 * u + 2)
                        link(tt(kk[:], kk[:], asig[:], ALU.mult))
                        tt(B[:], kk[:], Pi[:], ALU.mult).then_inc(S("B"), 1)
                    if serial:
                        new_state(b, 1)
                    if norm:
                        dve.wait_ge(S("dev"), n + 1)
                        link(dve.reciprocal(dev[:], dev[:]))
                        tt(o[:], o[:], dev[:], ALU.mult).then_inc(S("normed"), 1)
                    if nl > 4:
                        merge(t, 4)

            @block.tensor
            def _(pe):
                mm_ = lambda *a, **k: pe.matmul(*a, skip_group_check=True, **k)

                def lora(u, part, weight, x):
                    if part == 0:
                        pe.wait_ge(S("lora_in"), 3 * u + 3)
                        if u:
                            pe.wait_ge(S("Z1_copied"), u)
                    else:
                        pe.wait_ge(S("wa"), 2 * u + part)
                    for ct in range(KM):
                        cs = slice(ct * P, (ct + 1) * P)
                        mm = mm_(banks[PREP][:, cs], weight[:, cs], x[:], start=True, stop=True)
                    mm.then_inc(S("lora"), 1)

                def turn(src):
                    for ct in range(KM):
                        mm = pe.transpose(banks[PREP][:, ct * P:(ct + 1) * P], src[:, ct, :], ident)
                    mm.then_inc(S("tok"), 1)

                def from_state(b, c):
                    n, cc, rc, q = 2 * b + c, slice(c * CH, (c + 1) * CH), rows(c), b % 3
                    if n:
                        pe.wait_ge(S("state"), n)
                    else:
                        pe.wait_ge(S("state_zero"), 1)
                    if b and c == 0:
                        pe.wait_ge(S("U_copied"), n)
                    if b and c == 0:
                        pe.wait_ge(S("centred"), b)
                    for p in range(KM):
                        mm = mm_(banks[0][rc, p * P:(p + 1) * P], AR[q][:, p, 0, cc], Sbd[:, p, :], start=True, stop=True)
                    mm.then_inc(S("X"), 1)
                    if b and c == 0:
                        pe.wait_ge(S("o"), b)
                    for p in range(KM):
                        mm_(banks[7][:, p * P + c * CH:p * P + (c + 1) * CH], Sbd[:, p, :], AR[q][:, p, 1, cc],
                            start=(c == 0 and p == 0), stop=False)

                def solve(b, c):
                    n, cc, rc = 2 * b + c, slice(c * CH, (c + 1) * CH), rows(c)
                    pe.wait_ge(S("X_added"), n + 1)
                    for p, s, hs, _ in heads:
                        mm = mm_(banks[0][rc, hs], TiT[b % 2][s][rc, p, cc], X[rc, hs], start=True, stop=True)
                    mm.then_inc(S("U"), 1)

                def to_state(b, c):
                    n, rc, q = 2 * b + c, rows(c), b % 3
                    if n:
                        pe.wait_ge(S("state"), n)
                    if b and c == 0:
                        pe.wait_ge(S("dev"), b)
                    pe.wait_ge(S("U_copied"), n + 1)
                    for p in range(KM):
                        ps = slice(p * P, (p + 1) * P)
                        mm_(banks[1][:, ps], Bt[q][rc, ps], U[rc, ps], start=True, stop=False)
                        mm = mm_(banks[1][:, ps], Kt[q][rc, ps], Vt[q][rc, ps], start=False, stop=True)
                    mm.then_inc(S("S_update"), 1)

                def grams(t, s):
                    q = t % 3
                    if s:
                        pe.wait_ge(S("L"), 2 * t + 1)
                    for p in range(KM):
                        if s and p % 2 == 0:
                            pe.wait_ge(S("masked"), 16 * t + 2 * p + 4)
                        mm_(banks[2][:, p * P:(p + 1) * P], AR[q][:, p, 0, :], Bs[s][:, p, :], start=True, stop=True)
                        w = slice((p % 2) * 2 * P, (p % 2 + 1) * 2 * P)
                        ar = AR[q][:, p].rearrange("p w t -> p (w t)")
                        mm_(banks[3 + p // 2][:, w], Bs[s][:, p, :], ar, start=True, stop=True)
                        mm = mm_(banks[5 + p // 2][:, w], Ks[s][:, p, :], ar, start=True, stop=True)
                        if p % 2:
                            mm.then_inc(S("grams"), 1)

                def off_times_t(t, i):
                    for s in range(2):
                        pe.wait_ge(S("T"), written(t) + 4 * i + 2 * s + 2)
                        pe.wait_ge(S("O"), 2 * (merges[t] + i) + s + 1)
                        for p in range(KM):
                            mm = mm_(banks[2 + s][:, p * P:(p + 1) * P], O_[s][:, p, :], TiT[t % 2][s][:, p, :], start=True, stop=True)
                        mm.then_inc(S("Z"), 1)

                def merge(t, i):
                    for s in range(2):
                        pe.wait_ge(S("Z_copied"), 2 * (merges[t] + i) + s + 1)
                        for p in range(KM):
                            mm = mm_(banks[4 + s][:, p * P:(p + 1) * P], Ti[s][:, p, :], Zm[s][:, p, :], start=True, stop=True)
                            if i < len(levels(t)) - 1:
                                mm = mm_(banks[2 + s][:, p * P:(p + 1) * P], Zm[s][:, p, :], Ti[s][:, p, :], start=True, stop=True)
                        mm.then_inc(S("merged"), 1)

                def outputs(b):
                    for p, s, hs, ps in heads:
                        mm_(banks[7][rows(s), ps], U[:, hs], MrbT[b % 2][s][:, p, :], start=False, stop=False)
                        mm = mm_(banks[7][rows(s), ps], Vt[b % 3][:, hs], MrkT[b % 2][s][:, p, :], start=False, stop=True)
                    mm.then_inc(S("O_sum"), 1)

                def samples():
                    q = LAST % 3
                    pe.wait_ge(S("state0_in"), 32)
                    pe.wait_ge(S("o"), LAST)
                    pe.wait_ge(S("Z1_copied"), TT)
                    pe.wait_ge(S("T"), written(TT))
                    for p in range(KM):
                        for i in range(NB):
                            bc = slice(i * NS, (i + 1) * NS)
                            pc = slice(p * P + i * NS, p * P + (i + 1) * NS)
                            first = p == 0 and i == 0
                            mm_(banks[7][:, pc], S0bd[:, i, p, :], AR[q][:, p, 1, bc], start=first, stop=False)
                            mm = mm_(banks[3][:, pc], S0bd[:, i, p, :], AR[q][:, p, 0, bc], start=first, stop=True)
                    mm.then_inc(S("X0T"), 1)
                    pe.wait_ge(S("X0T_copied"), 1)
                    for p in range(KM):
                        mm = pe.transpose(banks[4][:, p * P:(p + 1) * P], X0T[:, p, :], ident)
                    mm.then_inc(S("X"), 1)
                    pe.wait_ge(S("X_added"), NCH + 1)
                    for p, s, hs, _ in heads:
                        mm = mm_(banks[6][:, hs], TiT[LAST % 2][s][:, p, :], X[:, hs], start=True, stop=True)
                    mm.then_inc(S("U"), 1)
                    pe.wait_ge(S("U_copied"), NCH + 1)
                    outputs(LAST)
                    pe.wait_ge(S("centred"), LAST)
                    pe.wait_ge(S("dev"), LAST)
                    for part, tok in enumerate((Bt[q], Kt[q])):
                        pe.wait_ge(S("row_masked"), NB * (part + 1))
                        for p, s, hs, _ in heads:
                            mm = mm_(banks[SBANK[p]][rows(s), :], tok[:, hs], Um[:, :, hs], start=(part == 0), stop=(part == 1))
                        mm.then_inc(S("S_update"), 1)

                pe.wait_ge(S("weights_in"), 48)
                pe.wait_ge(S("zeros"), 6)
                for r in ROUNDS:
                    t, u, b, n = r, r + 1, r - 1, r - 2
                    nl, prep, serial, norm = len(levels(t)), is_tile(u), 0 <= b < LAST, is_tile(n)
                    if norm:
                        if n < LAST:
                            pe.wait_ge(S("U_copied"), 2 * n + 2)
                        pe.wait_ge(S("o"), n + 1)
                        mm_(banks[0 if n < LAST else 3][:], head, flat(OT[n % 2][:]), start=True, stop=True).then_inc(S("mean"), 1)
                    if nl:
                        pe.wait_ge(S("AR"), 2 * t + 2)
                        pe.wait_ge(S("sides"), 4 * t + 4)
                        pe.wait_ge(S("tok_copied"), 3 * t + 3)
                        if t:
                            pe.wait_ge(S("T"), written(t))
                        grams(t, 0)
                    if norm:
                        if n < LAST:
                            pe.wait_ge(S("state"), 2 * n + 2)
                        pe.wait_ge(S("dev2"), n + 1)
                        mm_(banks[1 if n < LAST else 2][:], head, flat(dev2[:]), start=True, stop=True).then_inc(S("var"), 1)
                    if serial:
                        from_state(b, 0)
                    if nl:
                        grams(t, 1)
                    if serial:
                        solve(b, 0)
                    if nl:
                        pe.wait_ge(S("masked"), 16 * t + 16)
                        pe.wait_ge(S("L"), 2 * t + 2)
                        for p, s, hs, _ in heads:
                            mm = mm_(banks[PREP][:, hs], LakT[s][:, p, :], Vt[t % 3][:, hs], start=True, stop=True)
                        mm.then_inc(S("Z1"), 1)
                    if b == LAST:
                        samples()
                    if nl:
                        off_times_t(t, 0)
                    if prep:
                        lora(u, 0, w2, wl)
                    if nl:
                        merge(t, 0)
                    if serial:
                        to_state(b, 0)
                    if prep:
                        lora(u, 1, a2, wl)
                    if nl:
                        off_times_t(t, 1)
                    if prep:
                        lora(u, 2, g2, gl)
                    if nl:
                        merge(t, 1)
                    if prep:
                        pe.wait_ge(S("sq"), u + 1)
                        pe.wait_ge(S("g"), u + 1)
                        mm_(banks[PREP][:], head, flat(sq[:]), start=True, stop=True).then_inc(S("norm2"), 1)
                    if serial:
                        from_state(b, 1)
                    if nl > 2:
                        off_times_t(t, 2)
                    if prep:
                        pe.wait_ge(S("rk"), u + 1)
                        pe.wait_ge(S("norm"), u + 1)
                        mm_(banks[PREP][:], head, flat(rk[:]), start=True, stop=True).then_inc(S("bonus"), 1)
                    if serial:
                        solve(b, 1)
                    if nl > 2:
                        merge(t, 2)
                    if nl > 3:
                        off_times_t(t, 3)
                    if prep:
                        pe.wait_ge(S("bonus_out"), u + 1)
                        turn(zs(u)[:, 8:12])
                    if nl > 3:
                        merge(t, 3)
                    if prep:
                        pe.wait_ge(S("K"), u + 1)
                        pe.wait_ge(S("tok_copied"), 3 * u + 1)
                        turn(K[:])
                    if serial:
                        to_state(b, 1)
                    if nl > 4:
                        off_times_t(t, 4)
                    if serial:
                        outputs(b)
                    if nl > 4:
                        merge(t, 4)
                    if prep:
                        pe.wait_ge(S("B"), u + 1)
                        pe.wait_ge(S("tok_copied"), 3 * u + 2)
                        turn(B[:])


class StreamSplit:

    SLOTS = 3

    def __init__(self, st, tag, src, xh, xl, n, ring):
        self.src, self.xh, self.xl, self.n, self.ring = src, xh, xl, n, ring
        self.arrived = [st.sem(f"{tag}_x_arrived{s}") for s in range(self.SLOTS)]
        self.rounded, self.rest = st.sem(f"{tag}_x_rounded"), st.sem(f"{tag}_x_rest")

    def load(self, eng):
        for k in range(self.n):
            if k >= self.SLOTS:
                eng.wait_ge(self.rest, k - self.SLOTS + 1)
            eng.dma_start(self.ring[:, k % self.SLOTS], self.src(k)).then_inc(self.arrived[k % self.SLOTS], 16)

    def scalar(self, act):
        for k in range(self.n):
            act.wait_ge(self.arrived[k % self.SLOTS], 16 * (k // self.SLOTS + 1))
            act.copy(self.xh[:, k], self.ring[:, k % self.SLOTS]).then_inc(self.rounded, 1)

    def vector(self, dve):
        for k in range(self.n):
            dve.wait_ge(self.rounded, k + 1)
            dve.tensor_tensor(self.xl[:, k], self.ring[:, k % self.SLOTS], self.xh[:, k].bitcast(F32), ALU.subtract).then_inc(self.rest, 1)


def add_to_residual(dve, prod, xt, added):
    def evac(p, s):
        for c in range(NTC):
            dve.wait_ge(prod.ready, (p * 2 + s) * NTC + (c + 1))
            row = xt[:, bass.ds(p * 2 + s, 1), c * TC:(c + 1) * TC].rearrange("p o t -> p (o t)")
            dve.tensor_tensor(row, prod.bank[s][c][:, 0:TC], row, ALU.add).then_inc(prod.used, 1)
    return evac


def stage_merge(nc, env, io):
    with Stage(nc, "merge") as st:
        banks = st.banks()
        S = st.sem
        ring = st.sb("branch", [P, 3, T])
        bh, bl = st.sb("branch_hi", [P, KM, T], F32R), st.sb("branch_lo", [P, KM, T], F32R)
        merged = st.sb("merged", [P, KD, T])
        gz = [st.sb(f"gate_z{s}", [P, T]) for s in range(2)]
        gs = [st.sb(f"gate{s}", [P, T]) for s in range(2)]
        tmp = st.sb("gated", [P, NTC, TC])
        bufs = Product.buffers(st, KM, "wb")
        prods = [Product(st, f"wb{n}", KM, KD // 2, wtile(io["w_branch"], KM, m0=KD * n), bh, bl, banks, bufs=bufs) for n in range(3)]
        splits = [StreamSplit(st, f"br{n}", lambda k, n=n: io["branch"][n, :, k], bh, bl, KM, ring) for n in range(3)]
        half = KD // 2
        with nc.Block() as block:
            @block.sync
            def _(sp):
                for n in range(3):
                    if n:
                        sp.wait_ge(splits[n - 1].rest, KM)
                        sp.wait_ge(prods[n - 1].rest, KD)
                    splits[n].load(sp)
                    prods[n].load(sp)
                sp.wait_ge(S("merged_done"), 1)
                sp.dma_start(io["merged"], merged[:]).then_inc(S("stored"), 16)
                sp.wait_ge(S("stored"), 16)

            @block.gpsimd
            def _(pool):
                for n in range(3):
                    def load(p, s, wait=True):
                        if wait:
                            pool.wait_ge(S(f"gate{n}"), p * 2 + (s - 1))
                        pool.dma_start(gz[s][:], io["z"][bass.ds(p * 2 + (Z_G + n * KD + s), 1)].rearrange("o p t -> (o p) t")).then_inc(S(f"gate_in{n}_{s}"), 16)
                    if n:
                        pool.wait_ge(S(f"gate{n - 1}"), KD)
                    load(0, 0, False)
                    load(0, 1, False)
                    with pool.Fori(1, half) as p:
                        load(p, 0)
                        load(p, 1)

            @block.scalar
            def _(act):
                for n in range(3):
                    if n:
                        act.wait_ge(prods[n - 1].ready, KD * NTC)
                    splits[n].scalar(act)

                    def gate(p, s):
                        act.wait_ge(S(f"gate_in{n}_{s}"), p * 16 + 16)
                        if not (isinstance(p, int) and p == 0):
                            act.wait_ge(prods[n].used, (p * 2 + (s - 1)) * NTC)
                        at = VAT["b_gate"] + n * KD
                        act.activation(gs[s][:], gz[s][:], ACT.Sigmoid, bias=env["vec"][:, bass.ds(p * 2 + (at + s), 1)]).then_inc(S(f"gate{n}"), 1)
                    if n:
                        act.wait_ge(prods[n - 1].used, KD * NTC)
                    prods[n].pipeline(act, prods[n].split_hi, gate)

            @block.vector
            def _(dve):
                for n in range(3):
                    splits[n].vector(dve)
                    prod = prods[n]

                    def evac(p, s):
                        dve.wait_ge(S(f"gate{n}"), p * 2 + (s + 1))
                        if n and not (isinstance(p, int) and p == 0 and s == 0):
                            dve.wait_ge(S(f"summed{n}"), (p * 2 + s) * NTC)
                        elif n == 2:
                            dve.wait_ge(S("summed1"), KD * NTC)
                        for c in range(NTC):
                            cs = slice(c * TC, (c + 1) * TC)
                            row = merged[:, bass.ds(p * 2 + s, 1), cs].rearrange("p o t -> p (o t)")
                            dve.wait_ge(prod.ready, (p * 2 + s) * NTC + (c + 1))
                            if n == 0:
                                dve.tensor_tensor(row, prod.bank[s][c][:, 0:TC], gs[s][:, cs], ALU.mult).then_inc(prod.used, 1)
                            else:
                                dve.tensor_tensor(tmp[:, c, :], prod.bank[s][c][:, 0:TC], gs[s][:, cs], ALU.mult).then_inc(prod.used, 1)
                                dve.wait_ge(prod.used, (p * 2 + s) * NTC + (c + 1))
                                dve.tensor_tensor(row, tmp[:, c, :], row, ALU.add).then_inc(S(f"summed{n}"), 1)
                    prod.pipeline(dve, prod.split_lo, evac)
                    if n:
                        dve.wait_ge(S(f"summed{n}"), KD * NTC)
                    else:
                        dve.wait_ge(prod.used, KD * NTC)
                dve.tensor_copy(tmp[:, 0, 0:1], tmp[:, 1, 0:1]).then_inc(S("merged_done"), 1)

            @block.tensor
            def _(pe):
                for n in range(3):
                    pe.wait_ge(splits[n].rest, KM)
                    if n:
                        pe.wait_ge(prods[n - 1].used, KD * NTC)
                    prods[n].products(pe)




def stage_residual(nc, env, io, name, src, w, parts, load_x=False):
    with Stage(nc, name) as st:
        banks = st.banks()
        S = st.sem
        kt = max(n for _, n in parts)
        xt = env["xt"]
        ring = st.sb("x", [P, 3, T])
        xh, xl = st.sb("x_hi", [P, kt, T], F32R), st.sb("x_lo", [P, kt, T], F32R)
        bufs = Product.buffers(st, kt, "w")
        prods = [Product(st, f"w{i}", n, KD // 2, wtile(w, n, k0=k0), xh, xl, banks, bufs=bufs) for i, (k0, n) in enumerate(parts)]
        splits = [StreamSplit(st, f"x{i}", lambda k, k0=k0: src[:, k0 + k], xh, xl, n, ring) for i, (k0, n) in enumerate(parts)]
        whole = lambda eng, i: eng.wait_ge(prods[i].ready, KD * NTC)
        with nc.Block() as block:
            @block.sync
            def _(sp):
                for i, prod in enumerate(prods):
                    if i:
                        sp.wait_ge(splits[i - 1].rest, splits[i - 1].n)
                        sp.wait_ge(prods[i - 1].rest, KD)
                    splits[i].load(sp)
                    if load_x and i == 0:
                        sp.dma_start(xt[:], io["xt"]).then_inc(S("residual_in"), 16)
                    prod.load(sp)

            @block.scalar
            def _(act):
                for i, prod in enumerate(prods):
                    if i:
                        whole(act, i - 1)
                    splits[i].scalar(act)
                    prod.pipeline(act, prod.split_hi, lambda p, s: None)

            @block.vector
            def _(dve):
                for i, prod in enumerate(prods):
                    splits[i].vector(dve)
                    if load_x and i == 0:
                        dve.wait_ge(S("residual_in"), 16)
                    if i:
                        dve.wait_ge(prods[i - 1].used, KD * NTC)
                    prod.pipeline(dve, prod.split_lo, add_to_residual(dve, prod, xt, None))

            @block.tensor
            def _(pe):
                for i, prod in enumerate(prods):
                    pe.wait_ge(splits[i].rest, splits[i].n)
                    if i:
                        pe.wait_ge(prods[i - 1].used, KD * NTC)
                    prod.products(pe)


def stage_queries(nc, env, io):
    with Stage(nc, "xq") as st:
        banks = st.banks()
        S = st.sem
        xt, vec = env["xt"], env["vec"]
        xh, xl = st.sb("xh", [P, KD, T], F32R), st.sb("xl", [P, KD, T], F32R)
        mem = st.sb("mem", [P, KD, NMEM])
        out = [st.sb(f"q{s}", [P, T]) for s in range(2)]
        bufs, nbufs = Product.buffers(st, KD, "w"), Norm.buffers(st, "norm")
        ones = env["mask"]("ones")
        nx = Norm(st, "nx", xt, vec[:, VAT["norm_x"]:], xh, xl, ones, banks, bufs=nbufs)
        nm = Norm(st, "nm", mem, vec[:, VAT["norm_mem"]:], xh, xl, ones, banks, tc=NMEM, ntc=1, bufs=nbufs)
        nx.eps = nm.eps = env["eps"]
        pq = Product(st, "wq", KD, KD // 2, wtile(io["w_xq"], KD), xh, xl, banks, bufs=bufs)
        pm = Product(st, "wm", KD, KD, wtile(io["w_mem_kv"], KD), xh, xl, banks[6:8], tc=NMEM, ntc=1, bufs=bufs)
        kv = env["kv"]
        with nc.Block() as block:
            @block.sync
            def _(sp):
                sp.dma_start(mem[:], io["memt"]).then_inc(S("mem_in"), 16)
                pm.load(sp)
                sp.wait_ge(pm.rest, 2 * KD)
                pq.load(sp)

            @block.scalar
            def _(act):
                act.wait_ge(S("mem_in"), 16)
                nm.scalar(act)
                pm.pipeline(act, pm.split_hi, lambda p, s: None)
                act.wait_ge(pm.ready, 2 * KD)
                nx.scalar(act)

                def evac(p, s):
                    if not (isinstance(p, int) and p == 0):
                        act.wait_ge(S(f"q_stored{s}"), p * 16)
                    for c in range(NTC):
                        act.wait_ge(pq.ready, (p * 2 + s) * NTC + (c + 1))
                        act.copy(out[s][:, c * TC:(c + 1) * TC], pq.bank[s][c][:, 0:TC]).then_inc(pq.used, 1)
                    act.wait_ge(pq.used, (p * 2 + (s + 1)) * NTC)
                    act.dma_start(io["q"][:, bass.ds(p * 2 + s, 1)].rearrange("p o t -> p (o t)"), out[s][:]).then_inc(S(f"q_stored{s}"), 16)
                pq.pipeline(act, pq.split_hi, evac)
                act.dma_start(io["o_mem"], kv[:]).then_inc(S("kv_stored"), 16)
                act.wait_ge(S("kv_stored"), 16)
                for s in range(2):
                    act.wait_ge(S(f"q_stored{s}"), 16 * pq.pairs)

            @block.vector
            def _(dve):
                nm.vector(dve)

                def evac(p, s):
                    dve.wait_ge(pm.ready, p * 2 + (s + 1))
                    dve.tensor_copy(kv[:, bass.ds(p * 2 + s, 1)].rearrange("p o t -> p (o t)"), pm.bank[s][0][:, 0:NMEM]).then_inc(pm.used, 1)
                pm.pipeline(dve, pm.split_lo, evac)
                nx.vector(dve)
                pq.pipeline(dve, pq.split_lo, lambda p, s: None)

            @block.tensor
            def _(pe):
                nm.tensor(pe)
                pe.wait_ge(nm.rest, KD)
                pm.products(pe)
                pe.wait_ge(nm.rooted, 1)
                nx.tensor(pe)
                pe.wait_ge(nx.rest, KD * NTC)
                pq.products(pe)


def stage_cross(nc, env, io):
    with Stage(nc, "cross") as st:
        banks = st.banks()
        S = st.sem
        kv, ident = env["kv"], env["mask"]("ident")
        q = st.sb("q", [P, KD, T])
        v = st.sb("v", [P, 2, D])
        s_ = [st.sb(f"scores{i}", [P, XH, NMEM]) for i in range(3)]
        stat = [st.sb(f"stat{i}", [P, 3, XH]) for i in range(2)]
        pt = st.sb("probs_t", [P, XH, 2, P])
        o = [st.sb(f"out{i}", [P, KD, P]) for i in range(2)]
        qm = st.sb("q_masked", [P, KD, 2, P])
        ks = [st.sb(f"k_sample{i}", [P, KD, NMEM]) for i in range(2)]
        vs = [st.sb(f"v_sample{i}", [P, 2, D]) for i in range(2)]
        SC = XHD ** -0.5
        NT = TT - 1
        b2 = lambda i: banks[i][:].rearrange("p (h m) -> p h m", h=2)
        dt_ = lambda i: banks[i][:].rearrange("p (n t) -> p n t", n=4)
        with nc.Block() as block:
            @block.sync
            def _(sp):
                sp.dma_start(q[:], io["q"]).then_inc(S("q_in"), 16)
                for b in range(NB):
                    if b >= 2:
                        sp.wait_ge(S("k_used"), b - 1)
                    sp.dma_start(ks[b % 2][:], io["mem_k"][b]).then_inc(S(f"k_in{b % 2}"), 16)
                for b in range(NB):
                    if b >= 2:
                        sp.wait_ge(S("v_used"), b - 1)
                    sp.dma_start(vs[b % 2][:], io["mem_v"][b]).then_inc(S(f"v_in{b % 2}"), 16)

            @block.gpsimd
            def _(pool):
                pool.wait_ge(S("q_in"), 16)
                for b in range(NB):
                    if b >= 2:
                        pool.wait_ge(S("k_used"), b - 1)
                    pool.memset(qm[:, :, b % 2], 0.0).then_inc(S("q_zero"), 1)
                    pool.wait_ge(S("q_zero"), b + 1)
                    pool.tensor_copy(qm[:, :, b % 2, b * NS:(b + 1) * NS], q[:, :, SEQ + b * NS:SEQ + (b + 1) * NS]).then_inc(S("q_masked"), 1)

            def softmax_scores(pe, t, keys):
                if t:
                    pe.wait_ge(S("scored"), 2 * t)
                for h in range(XH):
                    for d in range(2):
                        mm = pe.matmul(banks[h // 2][:, (h % 2) * NMEM:(h % 2 + 1) * NMEM], q[:, 2 * h + d, t * P:(t + 1) * P],
                                       keys(h, d), start=(d == 0), stop=(d == 1), skip_group_check=True)
                mm.then_inc(S("scores"), 1)

            def turn_probs(pe, t):
                pe.wait_ge(S("probs"), t + 1)
                if t:
                    pe.wait_ge(S("probs_t"), 2 * t)
                for h in range(XH):
                    for m in range(2):
                        mm = pe.transpose(banks[2 + h // 2][:, ((h % 2) * 2 + m) * P:((h % 2) * 2 + m + 1) * P],
                                          s_[t % 3][:, h, m * P:(m + 1) * P], ident)
                mm.then_inc(S("probs_turned"), 1)
                pe.wait_ge(S("probs_t"), 2 * (t + 1))
                if t:
                    pe.wait_ge(S("out_copied"), 2 * t)

            @block.tensor
            def _(pe):
                def sample_scores():
                    pe.wait_ge(S("scored"), 2 * NT)
                    for b in range(NB):
                        pe.wait_ge(S("q_masked"), b + 1)
                        pe.wait_ge(S(f"k_in{b % 2}"), 16 * (b // 2 + 1))
                        for h in range(XH):
                            for d in range(2):
                                first = b == 0 and d == 0
                                mm = pe.matmul(banks[h // 2][:, (h % 2) * NMEM:(h % 2 + 1) * NMEM], qm[:, 2 * h + d, b % 2, :],
                                               ks[b % 2][:, 2 * h + d, :], start=(first and h % 2 == 0), stop=(b == NB - 1 and d == 1),
                                               skip_group_check=True)
                        mm.then_inc(S("k_used"), 1)
                    mm_scores = pe.matmul(banks[7][:, 0:2], ident, ident[:, 0:2], start=True, stop=True)
                    mm_scores.then_inc(S("scores"), 1)

                for n in range(4):
                    if n >= 2:
                        pe.wait_ge(S("v_copied"), n - 1)
                    for j in range(4):
                        m, f = n // 2, (n % 2) * 4 + j
                        mm = pe.transpose(banks[6 + n % 2][:, j * P:(j + 1) * P], kv[:, KD + f, m * P:(m + 1) * P], ident)
                    mm.then_inc(S("v_turned"), 1)
                pe.wait_ge(S("v_copied"), 4)
                pe.wait_ge(S("q_in"), 16)
                for t in range(NT + 2):
                    if t < NT:
                        softmax_scores(pe, t, lambda h, d: kv[:, 2 * h + d, :])
                    elif t == NT:
                        sample_scores()
                    if t < 2:
                        continue
                    turn_probs(pe, t - 2)
                    for f in range(KD):
                        for m in range(2):
                            mm = pe.matmul(banks[4 + f // 4][:, (f % 4) * P:(f % 4 + 1) * P], v[:, m, f * P:(f + 1) * P],
                                           pt[:, f // 2, m, :], start=(m == 0), stop=(m == 1), skip_group_check=True)
                    mm.then_inc(S("weighted"), 1)
                turn_probs(pe, NT)
                for b in range(NB):
                    pe.wait_ge(S(f"v_in{b % 2}"), 16 * (b // 2 + 1))
                    for f in range(KD):
                        for m in range(2):
                            mm = pe.matmul(banks[4 + f // 4][:, (f % 4) * P + b * NS:(f % 4) * P + (b + 1) * NS],
                                           vs[b % 2][:, m, f * P:(f + 1) * P], pt[:, f // 2, m, b * NS:(b + 1) * NS],
                                           start=(m == 0), stop=(m == 1), skip_group_check=True)
                    mm.then_inc(S("v_used"), 1)
                pe.matmul(banks[7][:, 0:2], ident, ident[:, 0:2], start=True, stop=True).then_inc(S("weighted"), 1)

            @block.scalar
            def _(act):
                for n in range(4):
                    m, f = n // 2, (n % 2) * 512
                    act.wait_ge(S("v_turned"), n + 1)
                    act.copy(v[:, m, f:f + 512], banks[6 + n % 2][:]).then_inc(S("v_copied"), 1)
                def exponentials(i):
                    act.wait_ge(S("centred"), i + 1)
                    act.activation(s_[i % 3][:], s_[i % 3][:], ACT.Exp, scale=SC).then_inc(S("exp"), 1)

                for i in range(TT + 2):
                    if i < 2:
                        exponentials(i)
                        continue
                    t = i - 2
                    act.wait_ge(S("probs_turned"), t + 1)
                    for n in range(2):
                        act.copy(pt[:, 2 * n:2 * n + 2].rearrange("p h m t -> p (h m t)"), banks[2 + n][:]).then_inc(S("probs_t"), 1)
                    if t >= 2:
                        act.wait_ge(S(f"out_stored{t % 2}"), 16 * (t // 2))
                    if i < TT:
                        exponentials(i)
                    act.wait_ge(S("weighted"), t + 1)
                    for n in range(2):
                        act.copy(o[t % 2][:, 4 * n:4 * n + 4], dt_(4 + n)).then_inc(S("out_copied"), 1)
                    act.wait_ge(S("out_copied"), 2 * t + 2)
                    act.dma_start(io["xo"][:, :, t * P:(t + 1) * P], o[t % 2][:]).then_inc(S(f"out_stored{t % 2}"), 16)
                act.wait_ge(S("out_stored0"), 16 * 5)
                act.wait_ge(S("out_stored1"), 16 * 4)

            @block.vector
            def _(dve):
                steps = [0]

                def link(ins):
                    steps[0] += 1
                    ins.then_inc(S("dve_step"), 1)
                    dve.wait_ge(S("dve_step"), steps[0])
                up = lambda x: x.rearrange("p (h o) -> p h o", o=1).broadcast_to([P, XH, NMEM])

                def centre(t):
                    x, z = s_[t % 3], stat[t % 2]
                    dve.wait_ge(S("scores"), t + 1)
                    if t >= 3:
                        dve.wait_ge(S("probs_turned"), t - 2)
                    for n in range(2):
                        dve.tensor_reduce(z[:, 0, 2 * n:2 * n + 2], b2(n), AX.X, ALU.max).then_inc(S("maxed"), 1)
                    dve.wait_ge(S("maxed"), 2 * t + 2)
                    for n in range(2):
                        m = z[:, 0, 2 * n:2 * n + 2].rearrange("p (h o) -> p h o", o=1).broadcast_to([P, 2, NMEM])
                        dve.tensor_tensor(x[:, 2 * n:2 * n + 2], b2(n), m, ALU.subtract).then_inc(S("scored"), 1)
                    dve.wait_ge(S("scored"), 2 * t + 2)
                    dve.tensor_copy(z[:, 1], z[:, 0]).then_inc(S("centred"), 1)

                def normalise(t):
                    x, z = s_[t % 3], stat[t % 2]
                    dve.wait_ge(S("exp"), t + 1)
                    link(dve.tensor_reduce(z[:, 1], x[:], AX.X, ALU.add))
                    link(dve.reciprocal(z[:, 2], z[:, 1]))
                    dve.tensor_tensor(x[:], x[:], up(z[:, 2]), ALU.mult).then_inc(S("probs"), 1)

                for t in range(TT + 1):
                    if t < TT:
                        centre(t)
                    if t:
                        normalise(t - 1)


def stage_up(nc, env, io):
    with Stage(nc, "up") as st:
        banks = st.banks()
        S = st.sem
        xt, vec = env["xt"], env["vec"]
        xh, xl = st.sb("xh", [P, KD, T], F32R), st.sb("xl", [P, KD, T], F32R)
        PAD = 2 + SEQ + NB * (2 + NS)
        u = [st.sb(f"u{s}", [P, PAD]) for s in range(2)]
        y = [st.sb(f"y{s}", [P, T]) for s in range(2)]
        last = st.sb("last", [P, 2 * KF, 2 * (NB + 1)])
        state = st.sb("state", [P, 2 * KF, NB, 2])
        norm = Norm(st, "norm", xt, vec[:, VAT["norm_ffn"]:], xh, xl, env["mask"]("ones"), banks)
        norm.eps = env["eps"]
        w = io["w_up"]
        pair = lambda p, s: w[bass.ds(p + s * KF, 1)].rearrange("o p k m -> (o p) k m")
        prod = Product(st, "wup", KD, KF, pair, xh, xl, banks)
        prompt = lambda x: x[:, 0:SEQ]
        samples = lambda x: x[:, SEQ:T].rearrange("p (b s) -> p b s", b=NB)
        padded = lambda x: x[:, 2 + SEQ:PAD].rearrange("p (b s) -> p b s", b=NB)
        with nc.Block() as block:
            @block.sync
            def _(sp):
                sp.dma_start(state[:], io["ffn_state"]).then_inc(S("state_in"), 16)
                for s in range(2):
                    sp.dma_start(prod.raw[s][:], pair(0, s)).then_inc(prod.arrived[s], 16)

                def store(p):
                    sp.wait_ge(S("h"), p + 1)
                    sp.dma_start(io["h"][:, bass.ds(p, 1)].rearrange("p o t -> p (o t)"), y[0][:]).then_inc(S("h_stored"), 16)
                with sp.Fori(1, KF) as p:
                    for s in range(2):
                        sp.wait_ge(prod.rest, p * 2 + (s - 1))
                        sp.dma_start(prod.raw[s][:], pair(p, s)).then_inc(prod.arrived[s], 16)
                    store(p - 1)
                store(KF - 1)
                sp.wait_ge(S("h_stored"), 16 * KF)

            @block.gpsimd
            def _(pool):
                for s in range(2):
                    pool.memset(u[s][:, 0:2], 0.0).then_inc(S("padding_zero"), 1)
                pool.wait_ge(S("state_in"), 16)

                def put(p, s):
                    f = bass.ds(p + s * KF, 1)
                    if not (isinstance(p, int) and p == 0):
                        pool.wait_ge(S(f"conv{s}"), p * 2)
                        pool.wait_ge(S(f"last{s}"), p * 2)
                    pool.tensor_copy(padded(u[s])[:, :, 0:2], state[:, f].rearrange("p o b k -> p (o b) k")).then_inc(S(f"state_put{s}"), 1)
                    pool.wait_ge(S(f"u{s}"), p * 4 + 4)
                    pool.tensor_copy(last[:, f, 0:2].rearrange("p o k -> p (o k)"), u[s][:, SEQ:SEQ + 2]).then_inc(S(f"last{s}"), 1)
                    pool.tensor_copy(last[:, f, 2:].rearrange("p o (b k) -> p (o b) k", k=2), padded(u[s])[:, :, NS:NS + 2]).then_inc(S(f"last{s}"), 1)
                put(0, 0)
                put(0, 1)
                with pool.Fori(1, KF) as p:
                    put(p, 0)
                    put(p, 1)

            @block.scalar
            def _(act):
                norm.scalar(act)

                def evac(p, s):
                    if not (isinstance(p, int) and p == 0):
                        act.wait_ge(S(f"conv{s}"), p * 2)
                        act.wait_ge(S(f"last{s}"), p * 2)
                    for c in range(NTC):
                        act.wait_ge(prod.ready, (p * 2 + s) * NTC + (c + 1))
                        n = TC if c < NTC - 1 else SEQ - c * TC
                        f = act.copy(u[s][:, 2 + c * TC:2 + c * TC + n], prod.bank[s][c][:, 0:n]).then_inc(S(f"u{s}"), 1)
                    act.copy(padded(u[s])[:, :, 2:], prod.bank[s][NTC - 1][:, TC - NB * NS:TC].rearrange("p (b s) -> p b s", b=NB)).then_inc(S(f"u{s}"), 1)
                    act.wait_ge(S(f"u{s}"), p * 4 + 4)
                    act.sem_inc(prod.used, NTC)
                    if s == 1:
                        act.wait_ge(S("conv0"), p * 2 + 2)
                        act.activation(y[0][:], y[0][:], ACT.Gelu_apprx_tanh).then_inc(S("gelu"), 1)
                prod.pipeline(act, prod.split_hi, evac)
                act.wait_ge(S("last0"), 2 * KF)
                act.wait_ge(S("last1"), 2 * KF)
                act.dma_start(io["o_ffn"], last[:]).then_inc(S("last_stored"), 16)
                act.wait_ge(S("last_stored"), 16)

            @block.vector
            def _(dve):
                norm.vector(dve)
                dve.wait_ge(S("padding_zero"), 2)

                def evac(p, s):
                    dve.wait_ge(S(f"u{s}"), p * 4 + 4)
                    dve.wait_ge(S(f"state_put{s}"), p + 1)
                    tap = lambda k: vec[:, bass.ds(p + (VAT["ffn_conv_w"] + k * 2 * KF + s * KF), 1)]
                    if not (isinstance(p, int) and p == 0):
                        dve.wait_ge(S("h"), p)
                        dve.wait_ge(S("h_stored"), p * 16)
                    srcs = (lambda k: u[s][:, k:k + SEQ], lambda k: padded(u[s])[:, :, k:k + NS])
                    dsts = (prompt(y[s]), samples(y[s]))
                    for i, (src, dst) in enumerate(zip(srcs, dsts)):
                        dve.tensor_scalar(dst, src(0), tap(0), None, ALU.mult).then_inc(S(f"tap_a{s}"), 1)
                    dve.wait_ge(S(f"tap_a{s}"), p * 2 + 2)
                    for src, dst in zip(srcs, dsts):
                        dve.scalar_tensor_tensor(out=dst, in0=src(1), scalar=tap(1), in1=dst, op0=ALU.mult, op1=ALU.add).then_inc(S(f"tap_b{s}"), 1)
                    dve.wait_ge(S(f"tap_b{s}"), p * 2 + 2)
                    for src, dst in zip(srcs, dsts):
                        dve.scalar_tensor_tensor(out=dst, in0=src(2), scalar=tap(2), in1=dst, op0=ALU.mult, op1=ALU.add).then_inc(S(f"conv{s}"), 1)
                    if s == 1:
                        dve.wait_ge(S("gelu"), p + 1)
                        dve.wait_ge(S("conv1"), p * 2 + 2)
                        dve.tensor_tensor(y[0][:], y[0][:], y[1][:], ALU.mult).then_inc(S("h"), 1)
                prod.pipeline(dve, prod.split_lo, evac)

            @block.tensor
            def _(pe):
                norm.tensor(pe)
                pe.wait_ge(norm.rest, KD * NTC)
                prod.products(pe)


def stage_final(nc, env, io):
    with Stage(nc, "final") as st:
        banks = st.banks()
        S = st.sem
        y = st.sb("y", [P, KD, T])
        norm = Norm(st, "norm", env["xt"], env["vec"][:, VAT["norm_final"]:], None, y, env["mask"]("ones"), banks)
        norm.eps = env["eps"]
        with nc.Block() as block:
            @block.sync
            def _(sp):
                for c in range(NTC):
                    sp.wait_ge(norm.normed, KD * (c + 1))
                    cs = slice(c * TC, (c + 1) * TC)
                    sp.dma_start(io["y"][:, :, cs], y[:, :, cs]).then_inc(S("stored"), 16)
                sp.wait_ge(S("stored"), 16 * NTC)

            @block.scalar
            def _(act):
                norm.scalar(act)

            @block.vector
            def _(dve):
                norm.vector(dve)

            @block.tensor
            def _(pe):
                norm.tensor(pe)


OUTS = {"y": [P, KD, T], "o_conv_p": [KM, P, 3], "o_conv_s": [KM, P, NB, 3], "o_h": [P, KM, NB + 1],
        "o_swa_new": [2, P, P + NB * NS], "o_swa_kept": [2 * NB, (P - NS) * P], "o_shift": [P, NRW, NB + 1], "o_state_p": [P, KM, P], "o_state_s": [P, KM, NB, HD],
        "o_mem": [P, 2 * KD, NMEM], "o_ffn": [P, 2 * KF, 2 * (NB + 1)]}
SCRATCH = {"z": [Z_N, P, T], "branch": [3, P, KM, T], "merged": [P, KD, T], "q": [P, KD, T], "xo": [P, KD, T], "h": [P, KF, T]}


def hybrid_stream_step(nc, io, stages=99):
    for name, shape in SCRATCH.items():
        io[name] = nc.dram_tensor(f"scratch_{name}", shape, F32, kind="Internal").ap() if name not in io else io[name]
    with ExitStack() as ctx:
        sb = lambda n, s: ctx.enter_context(nc.sbuf_tensor(n, s, F32))
        vec, masks, eps = sb("vec", [P, NVEC]), sb("masks", [P, MW]), sb("eps", [P, 2])
        w = len(MASKS) * P
        env = {"vec": vec, "masks": masks, "eps": eps,
               "mask": lambda n: masks[:, MASKS.index(n) * P:(MASKS.index(n) + 1) * P],
               "resets": [masks[:, w + i * KM * P:w + (i + 1) * KM * P] for i in range(2)],
               "sample_rows": masks[:, w + 2 * KM * P:MW]}
        todo = [stage_in_projection, stage_lru, stage_swa, stage_rwkv, stage_merge]
        for stage in todo[:stages]:
            stage(nc, env, io)
        if stages < 6:
            return
        env["xt"] = sb("xt", [P, KD, T])
        stage_residual(nc, env, io, "out", io["merged"], io["w_out"], [(0, KD)], load_x=True)
        with nc.sbuf_tensor("mem_kv", [P, 2 * KD, NMEM], F32) as kv:
            env["kv"] = kv
            stage_queries(nc, env, io)
            stage_cross(nc, env, io)
        stage_residual(nc, env, io, "xo", io["xo"], io["w_xo"], [(0, KD)])
        stage_up(nc, env, io)
        stage_residual(nc, env, io, "down", io["h"], io["w_down"], [(0, KF // 2), (KF // 2, KF // 2)])
        stage_final(nc, env, io)


def lay_out(i):
    c = np.ascontiguousarray
    feat = lambda x: c(x.T.reshape(-1, P, x.shape[0]).transpose(1, 0, 2))
    tiles = lambda w: c(w.reshape(w.shape[0] // P, P, w.shape[1] // P, P).transpose(2, 1, 0, 3))
    one = {k: v[0] for k, v in i.items() if k not in ("x_prompt", "x_sample", "mem_prompt", "norm_final")}
    a = {"xt": feat(np.concatenate([i["x_prompt"].reshape(SEQ, D), i["x_sample"].reshape(NB * NS, D)])),
         "memt": feat(i["mem_prompt"].reshape(NMEM, D)), "masks": shape_masks()}
    vecs = {n: (i[n] if n == "norm_final" else one[n]).reshape(-1, P) for n, _ in VEC}
    a["vec"] = c(np.concatenate([vecs[n] for n, _ in VEC]).T)
    for n in ("w_in", "w_out", "w_xq", "w_mem_kv", "w_xo", "w_up", "w_down"):
        a[n] = tiles(one[n])
    a["w_branch"] = np.concatenate([tiles(w) for w in one["w_branch"]])
    gw = np.zeros((P, 2, KM, P), np.float32)
    for g in range(2):
        for h in range(NH):
            s = slice(64 * (h % 2), 64 * (h % 2) + 64)
            gw[s, g, h // 2, s] = one["lru_gate_w"][g, h]
    a["lru_gate_w"] = gw
    a["lru_conv"] = c(one["state_lru_conv"].reshape(NB, 3, KM, P).transpose(2, 3, 0, 1))
    a["lru_h"] = c(one["state_lru_h"].reshape(NB, KM, P).transpose(2, 1, 0))
    k = one["cache_swa_k"][:, CH:]
    two = [k.transpose(2, 3, 0, 1).reshape(P, NB, CH), k[:, :, ::-1].transpose(2, 3, 0, 1).reshape(P, NB, CH)]
    a["swa_k"] = c(np.stack(two, axis=1))
    a["swa_v"] = c(one["cache_swa_v"][:, CH:].transpose(1, 0, 2, 3).reshape(CH, NB, P))
    a["swa_cache"] = np.stack([one[n][:, NS:].reshape(NB, -1) for n in ("cache_swa_k", "cache_swa_v")]).reshape(2 * NB, -1)
    a["sink"] = one["swa_sink"].reshape(1, NH)
    a["w2a2"] = np.concatenate([one["rwkv_w2"], one["rwkv_a2"]])
    a["g2"] = one["rwkv_g2"]
    a["shift"] = c(one["state_rwkv_shift"].reshape(NB, NRW, P).transpose(2, 1, 0))
    s0 = one["state_rwkv"].reshape(NB, KM, 2, HD, HD).transpose(2, 4, 1, 0, 3)
    a["s0"] = c(s0.reshape(P, KM, NB, HD))
    diag = np.zeros((2, HD, NB, KM, 2, HD), np.float32)
    for s in range(2):
        diag[s, :, :, :, s] = s0[s].transpose(0, 2, 1, 3)
    a["s0_diag"] = diag.reshape(P, NB, KM, P)
    a["mem_k"] = c(one["cache_mem_k"].reshape(NB, NMEM, KD, P).transpose(0, 3, 2, 1))
    a["mem_v"] = c(one["cache_mem_v"].reshape(NB, 2, P, D).transpose(0, 2, 1, 3))
    a["ffn_state"] = c(one["state_ffn_conv"].reshape(NB, 2, 2 * KF, P).transpose(3, 2, 0, 1))
    return a


def hand_back(o):
    c = np.ascontiguousarray
    y = c(o["y"].transpose(2, 1, 0).reshape(T, D))
    conv_s = o["o_conv_s"].transpose(2, 3, 0, 1).reshape(1, NB, 3, MIX)
    conv_p = o["o_conv_p"].transpose(2, 0, 1).reshape(1, 1, 3, MIX)
    h = o["o_h"].transpose(2, 1, 0).reshape(NB + 1, MIX)
    new = o["o_swa_new"].transpose(0, 2, 1).reshape(2, P + NB * NS, 2, HD)
    swa_p = [c(n[:P].reshape(1, 1, P, 2, HD)) for n in new]
    kept = o["o_swa_kept"].reshape(2, 1, NB, P - NS, 2, HD)
    swa_s = [np.concatenate([old, n[P:].reshape(1, NB, NS, 2, HD)], axis=2) for old, n in zip(kept, new)]
    shift = o["o_shift"].transpose(2, 1, 0).reshape(NB + 1, 1, NRW * P)
    sp = o["o_state_p"].reshape(2, HD, KM, 2, HD)
    s_p = np.stack([sp[s, :, :, s] for s in range(2)]).transpose(2, 0, 3, 1).reshape(1, 1, NH, HD, HD)
    s_s = o["o_state_s"].reshape(2, HD, KM, NB, HD).transpose(3, 2, 0, 4, 1).reshape(1, NB, NH, HD, HD)
    ffn = o["o_ffn"].transpose(2, 1, 0).reshape(NB + 1, 2, 2 * FF)
    mem = o["o_mem"].transpose(2, 1, 0).reshape(NMEM, 2, XH, XHD)
    return (y[:SEQ].reshape(1, SEQ, D), y[SEQ:].reshape(NB, NS, D),
            c(conv_p), c(h[:1][None]), swa_p[0], swa_p[1], c(shift[:1][None]), c(s_p), c(ffn[:1][None]),
            c(mem[:, 0][None, None]), c(mem[:, 1][None, None]),
            c(conv_s), c(h[1:][None]), swa_s[0], swa_s[1], c(shift[1:][None]), c(s_s), c(ffn[1:][None]))


def kernel(**inputs):
    from concourse import bacc
    from concourse.bass_utils import run_bass_kernel_spmd

    nc = bacc.Bacc("TRN2", target_bir_lowering=False, num_devices=1)
    arrays = lay_out(inputs)
    io = {n: nc.dram_tensor(f"in_{n}", a.shape, mybir.dt.from_np(a.dtype), kind="ExternalInput").ap() for n, a in arrays.items()}
    io |= {n: nc.dram_tensor(f"out_{n}", s, F32, kind="ExternalOutput").ap() for n, s in OUTS.items()}
    hybrid_stream_step(nc, io)
    r = run_bass_kernel_spmd(nc, [{f"in_{n}": a for n, a in arrays.items()}], core_ids=[0])
    return hand_back({n: r.results[0][f"out_{n}"] for n in OUTS})
```

```python
from contextlib import ExitStack

import numpy as np

import concourse.bass as bass
from concourse import mybir

F32 = mybir.dt.float32
F32R = mybir.dt.float32r
ALU = mybir.AluOpType
ACT = mybir.ActivationFunctionType
AX = mybir.AxisListType

P = 128
D = 1024
KD = D // P
SEQ = 1024
NB, NS = 8, 16
T = SEQ + NB * NS
TC = 384
NTC = T // TC
TT = T // P
MIX = 512
KM = MIX // P
NH, HD = 8, 64
CH = 64
NCH = SEQ // CH
FF = 2816
KF = FF // P
NMEM = 256
XH, XHD = 4, 256
EPS = 1e-6
GN_EPS = 64e-5
DEC = float(np.exp(-0.5))

Z_LX, Z_LY, Z_Q, Z_K, Z_V, Z_RW, Z_G, Z_N = 0, 4, 8, 12, 13, 14, 28, 52
NRW = Z_G - Z_RW

VEC = [("norm_mix", 8), ("b_gate", 24), ("lru_conv_w", 16), ("lru_conv_b", 4), ("lru_gate_b", 8),
       ("lru_lambda", 4), ("rwkv_mu", 14), ("rwkv_w0", 4), ("rwkv_a0", 4), ("rwkv_k_k", 4),
       ("rwkv_k_a", 4), ("rwkv_r_k", 4), ("rwkv_ln_w", 4), ("rwkv_ln_b", 4), ("norm_x", 8),
       ("norm_mem", 8), ("norm_ffn", 8), ("ffn_conv_w", 132), ("norm_final", 8)]
VAT = {}
for _n, _c in VEC:
    VAT[_n] = sum(c for _, c in VEC[:len(VAT)])
NVEC = sum(c for _, c in VEC)

MASKS = ["ident", "ones", "head", "off2", "off2T", "off4", "off8", "off16", "off32", "off64",
         "upS64", "upI64", "upS16", "upI16"]


def shape_masks():
    t = np.arange(P)[:, None]
    j = np.arange(P)[None, :]
    same = lambda n: t // n == j // n
    off = lambda n: same(n) & (t % n >= n // 2) & (j % n < n // 2)
    m = {"ident": t == j, "ones": (t >= 0) & (j >= 0), "head": same(HD), "off2": off(2), "off2T": off(2).T}
    for n in (4, 8, 16, 32, 64):
        m[f"off{n}"] = off(n)
    for n in (64, 16):
        m[f"upS{n}"] = same(n) & (t < j)
        m[f"upI{n}"] = same(n) & (t <= j)
    blocks = [m[n].astype(np.float32) for n in MASKS]
    col = np.arange(KM * P)[None, :] + np.zeros((P, 1), int)
    resets = [(col % n != 0).astype(np.float32) for n in (CH, NS)]
    rows = (t // NS == np.arange(NB)[None, :]).astype(np.float32)
    return np.ascontiguousarray(np.concatenate(blocks + resets + [rows], axis=1))


MW = len(MASKS) * P + 2 * KM * P + NB


class Stage:

    def __init__(self, nc, name):
        self.nc, self.name, self.ctx, self.sems = nc, name, ExitStack(), {}

    def __enter__(self):
        self.ctx.__enter__()
        return self

    def __exit__(self, *e):
        self.nc.clear_and_free_semaphores(list(self.sems.values()))
        self.nc.all_engine_barrier()
        return self.ctx.__exit__(*e)

    def sb(self, name, shape, dt=F32):
        return self.ctx.enter_context(self.nc.sbuf_tensor(f"{self.name}_{name}", shape, dt))

    def banks(self, n=8):
        return [self.ctx.enter_context(self.nc.psum_tensor(f"{self.name}_bank{i}", [P, 512], F32)) for i in range(n)]

    def sem(self, name):
        if name not in self.sems:
            self.sems[name] = self.nc.alloc_semaphore(f"{self.name}_{name}")
        return self.sems[name]


class Product:

    def __init__(self, st, tag, kt, pairs, weights, xh, xl, banks, tc=TC, ntc=NTC, bufs=None):
        self.st, self.kt, self.pairs, self.w = st, kt, pairs, weights
        self.xh, self.xl, self.tc, self.ntc = xh, xl, tc, ntc
        self.bank = [banks[:ntc], banks[ntc:2 * ntc]]
        self.raw, self.hi, self.lo = bufs or Product.buffers(st, kt, tag)
        self.arrived = [st.sem(f"{tag}_w_arrived{s}") for s in range(2)]
        self.rounded = st.sem(f"{tag}_w_rounded")
        self.rest = st.sem(f"{tag}_w_rest")
        self.ready = st.sem(f"{tag}_product_ready")
        self.used = st.sem(f"{tag}_product_used")

    @staticmethod
    def buffers(st, kt, tag):
        return tuple([st.sb(f"{tag}_{n}{s}", [P, kt, P], dt) for s in range(2)]
                     for n, dt in (("raw", F32), ("hi", F32R), ("lo", F32R)))

    def load(self, eng):
        self.load_first(eng)
        self.load_rest(eng)

    def load_first(self, eng):
        for s in range(2):
            eng.dma_start(self.raw[s][:, 0:self.kt], self.w(0, s)).then_inc(self.arrived[s], 16)

    def load_rest(self, eng, beside=None):
        def pair(p, extra=None):
            for s in range(2):
                eng.wait_ge(self.rest, p * 2 + (s - 1))
                eng.dma_start(self.raw[s][:, 0:self.kt], self.w(p, s)).then_inc(self.arrived[s], 16)
                if extra:
                    extra(p, s)
        if not beside:
            with eng.Fori(1, self.pairs) as p:
                pair(p)
            return
        with eng.Fori(1, beside.first) as p:
            pair(p)
        pair(beside.first, beside.load)
        with eng.Fori(beside.first + 1, beside.end) as p:
            pair(p, beside.load)
        with eng.Fori(beside.end, self.pairs) as p:
            pair(p)

    def split_hi(self, act, p, s):
        act.wait_ge(self.arrived[s], p * 16 + 16)
        if not (isinstance(p, int) and p == 0):
            act.wait_ge(self.ready, (p * 2 + (s - 1)) * self.ntc)
        act.copy(self.hi[s][:, 0:self.kt], self.raw[s][:, 0:self.kt]).then_inc(self.rounded, 1)

    def split_lo(self, dve, p, s):
        dve.wait_ge(self.rounded, p * 2 + (s + 1))
        dve.tensor_tensor(self.lo[s][:, 0:self.kt], self.raw[s][:, 0:self.kt],
                          self.hi[s][:, 0:self.kt].bitcast(F32), ALU.subtract).then_inc(self.rest, 1)

    def first_splits(self, eng, split):
        split(eng, 0, 0)
        split(eng, 0, 1)

    def pipeline(self, eng, split, evac, beside=None):
        def pair(p):
            if split:
                split(eng, p, 0)
            evac(p - 1, 1)
            if split:
                split(eng, p, 1)
            evac(p, 0)
        def pair_beside(p):
            before, after = beside.work
            before(p, 0)
            evac(p - 1, 1)
            split(eng, p, 1)
            after(p, 0)
            before(p, 1)
            evac(p, 0)
            split(eng, p + 1, 0)
            after(p, 1)
        evac(0, 0)
        pair(1)
        if not beside:
            with eng.Fori(2, self.pairs) as p:
                pair(p)
            evac(self.pairs - 1, 1)
            return
        with eng.Fori(2, beside.first) as p:
            pair(p)
        split(eng, beside.first, 0)
        pair_beside(beside.first)
        with eng.Fori(beside.first + 1, beside.end) as p:
            pair_beside(p)
        beside.work[0](beside.end, 0)
        evac(beside.end - 1, 1)
        split(eng, beside.end, 1)
        beside.finish()
        evac(beside.end, 0)
        with eng.Fori(beside.end + 1, self.pairs) as p:
            pair(p)
        evac(self.pairs - 1, 1)

    def products(self, pe, x_rest, by_chunk, beside=None):
        def tile(p, s, wait, extra=None):
            pe.wait_ge(self.rest, p * 2 + (s + 1))
            if wait:
                pe.wait_ge(self.used, (p * 2 + (s - 1)) * self.ntc)
            passes = ((self.hi, self.xh), (self.lo, self.xh), (self.hi, self.xl))
            for k in range(self.kt):
                for n, (w, x) in enumerate(passes):
                    for c in range(self.ntc):
                        last = k == self.kt - 1 and n == 2
                        mm = pe.matmul(self.bank[s][c][:, 0:self.tc], w[s][:, k, :],
                                       x[:, k, c * self.tc:(c + 1) * self.tc], start=(k == 0 and n == 0), stop=last)
                        if last:
                            mm.then_inc(self.ready, 1)
                if extra:
                    extra(pe, p, s, k)

        def first_tile():
            pe.wait_ge(self.rest, 1)
            passes = ((self.hi, self.xh), (self.lo, self.xh), (self.hi, self.xl))
            order = [(c, k) for c in range(self.ntc) for k in range(self.kt)] if by_chunk else [(c, k) for k in range(self.kt) for c in range(self.ntc)]
            for c, k in order:
                if by_chunk or c == 0:
                    pe.wait_ge(x_rest, c * self.kt + k + 1)
                for n, (w, x) in enumerate(passes):
                    last = k == self.kt - 1 and n == 2
                    mm = pe.matmul(self.bank[0][c][:, 0:self.tc], w[0][:, k, :],
                                   x[:, k, c * self.tc:(c + 1) * self.tc], start=(k == 0 and n == 0), stop=last)
                    if last:
                        mm.then_inc(self.ready, 1)
        first_tile()
        tile(0, 1, False)
        if not beside:
            with pe.Fori(1, self.pairs) as p:
                tile(p, 0, True)
                tile(p, 1, True)
            return
        with pe.Fori(1, beside.first) as p:
            tile(p, 0, True)
            tile(p, 1, True)
        tile(beside.first, 0, True, beside.tensor)
        tile(beside.first, 1, True, beside.tensor)
        with pe.Fori(beside.first + 1, beside.end) as p:
            tile(p, 0, True, beside.tensor)
            tile(p, 1, True, beside.tensor)
        tile(beside.end, 0, True, beside.tensor_last)
        tile(beside.end, 1, True)
        with pe.Fori(beside.end + 1, self.pairs) as p:
            tile(p, 0, True)
            tile(p, 1, True)


class Norm:

    def __init__(self, st, tag, xt, gain, xh, xl, ones, banks, tc=TC, ntc=NTC, kd=KD, bufs=None):
        self.xt, self.gain, self.xh, self.xl, self.ones, self.banks = xt, gain, xh, xl, ones, banks
        self.tc, self.ntc, self.kd = tc, ntc, kd
        self.sq, self.rs, self.xn = bufs or Norm.buffers(st, tag)
        (self.squared, self.summed, self.rooted, self.inverse, self.normed, self.rounded, self.rest) = (
            st.sem(f"{tag}_{n}") for n in ("squared", "summed", "rooted", "inverse", "normed", "rounded", "rest"))

    @staticmethod
    def buffers(st, tag):
        return st.sb(f"{tag}_sq", [P, 4, TC]), st.sb(f"{tag}_rs", [P, T]), st.sb(f"{tag}_xn", [P, 2, TC])

    def cols(self, c):
        return slice(c * self.tc, (c + 1) * self.tc)

    def scalar(self, act):
        self.squares(act)
        self.roots(act)

    def squares(self, act, arrived=None, weights=None):
        n = 0
        for c in range(self.ntc):
            if weights and c == 1:
                weights.first_splits(act, weights.split_hi)
            if arrived:
                act.wait_ge(arrived[c], 16)
            for k in range(self.kd):
                if n >= 4:
                    act.wait_ge(self.summed, n - 3)
                act.activation(self.sq[:, n % 4, 0:self.tc], self.xt[:, k, self.cols(c)], ACT.Square).then_inc(self.squared, 1)
                n += 1
            if c:
                self.root(act, c - 1)

    def root(self, act, c):
        act.wait_ge(self.summed, self.kd * (c + 1))
        act.activation(self.rs[:, self.cols(c)], self.banks[c][:, 0:self.tc], ACT.Sqrt,
                       scale=1.0 / D, bias=self.eps[:, 0:1]).then_inc(self.rooted, 1)

    def roots(self, act):
        self.root(act, self.ntc - 1)
        if self.xh is not None:
            for i in range(self.ntc * self.kd):
                c, k = divmod(i, self.kd)
                act.wait_ge(self.normed, i + 1)
                act.copy(self.xh[:, k, self.cols(c)], self.xn[:, i % 2, 0:self.tc]).then_inc(self.rounded, 1)

    def tensor(self, pe):
        n = 0
        for c in range(self.ntc):
            for k in range(self.kd):
                pe.wait_ge(self.squared, n + 1)
                pe.matmul(self.banks[c][:, 0:self.tc], self.ones, self.sq[:, n % 4, 0:self.tc],
                          start=(k == 0), stop=(k == self.kd - 1)).then_inc(self.summed, 1)
                n += 1

    def vector(self, dve):
        for c in range(self.ntc):
            dve.wait_ge(self.rooted, c + 1)
            dve.reciprocal(self.rs[:, self.cols(c)], self.rs[:, self.cols(c)]).then_inc(self.inverse, 1)
            dve.wait_ge(self.inverse, c + 1)
            for k in range(self.kd):
                i = c * self.kd + k
                out = self.xn[:, i % 2, 0:self.tc] if self.xh is not None else self.xl[:, k, self.cols(c)]
                if self.xh is not None and i >= 2:
                    dve.wait_ge(self.rest, i - 1)
                dve.scalar_tensor_tensor(out=out, in0=self.xt[:, k, self.cols(c)], scalar=self.gain[:, k:k + 1],
                                         in1=self.rs[:, self.cols(c)], op0=ALU.mult, op1=ALU.mult).then_inc(self.normed, 1)
                if self.xh is not None and i:
                    self.remainder(dve, i - 1)
        if self.xh is not None:
            self.remainder(dve, self.ntc * self.kd - 1)

    def remainder(self, dve, i):
        c, k = divmod(i, self.kd)
        dve.wait_ge(self.rounded, i + 1)
        dve.tensor_tensor(self.xl[:, k, self.cols(c)], self.xn[:, i % 2, 0:self.tc],
                          self.xh[:, k, self.cols(c)].bitcast(F32), ALU.subtract).then_inc(self.rest, 1)


def wtile(w, kt, m0=0, k0=0):
    def at(p, s):
        return w[bass.ds(p * 2 + (m0 + s), 1), :, k0:k0 + kt, :].rearrange("o p k m -> (o p) k m")
    return at


class Beside:

    def __init__(self, first, end, work=None, finish=None, load=None):
        self.first, self.end, self.work, self.finish, self.load = first, end, work, finish, load


class PromptWindows:

    UNITS = [(g, b) for g in range(2) for b in range(2)]

    def __init__(self, st, env, io, banks, first):
        self.st, self.io, self.banks, self.ident = st, io, banks, env["mask"]("ident")
        self.first, self.end = first, first + NCH // 2
        two = lambda name, shape: [st.sb(f"{name}{i}", shape) for i in range(2)]
        self.q, self.k, self.v = two("q", [P, 4, CH]), two("k", [P, 2, P]), two("v", [P, P])
        self.x, self.stat, self.vt = two("scores", [P, 4, P + 1]), two("stat", [P, 3, 4]), two("v_t", [P, P])
        self.pt, self.ob = st.sb("probs_t", [P, 4, P]), two("attended", [P, 4, CH])
        self.sink, self.sinkq = st.sb("sink", [P, NH]), st.sb("sink_of_row", [P, 4])

    def chunk(self, p, s):
        if isinstance(p, int):
            c = 2 * (p - self.first) + s
            return c, max(c - 1, 0) * CH, CH * min(c + 1, 2)
        return p * 2 + (s - 2 * self.first), p * (2 * CH) + (s - 2 * self.first - 1) * CH, P

    def past_first_pair(self, p):
        return not (isinstance(p, int) and p == self.first)

    def load_sinks(self, sp):
        sp.dma_start(self.sink[:], self.io["sink"].broadcast_to([P, NH])).then_inc(self.st.sem("sink_in"), 16)

    def load(self, sp, p, s):
        S, zt = self.st.sem, self.io["z"]
        c, lo, nk = self.chunk(p, s)
        if self.past_first_pair(p):
            sp.wait_ge(S("scores"), c - 1)
        elif s == 0:
            for slot in range(2):
                sp.wait_ge(S(f"z_stored{slot}"), 16 * (Z_RW // 2))
        keys = bass.ds(lo, nk)
        arrived = S(f"chunk_in{s}")
        sp.dma_start(self.q[s][:], zt[Z_Q:Z_K, :, bass.ds(c * CH, CH)].rearrange("n p t -> p n t")).then_inc(arrived, 16)
        sp.dma_start(self.k[s][:, 0, 0:nk], zt[Z_K, :, keys]).then_inc(arrived, 16)
        for b in range(2):
            sp.dma_start(self.k[s][64 * b:64 * b + 64, 1, 0:nk], zt[Z_K, 64 - 64 * b:128 - 64 * b, keys]).then_inc(arrived, 16)
        sp.dma_start(self.v[s][:, 0:nk], zt[Z_V, :, keys]).then_inc(arrived, 16)

    def weigh(self, pe, c, s, nk):
        S = self.st.sem
        pe.wait_ge(S("probs_t"), c * 2 + 2)
        for n, (g, b) in enumerate(self.UNITS):
            mm = pe.matmul(self.banks[7][64 * b:64 * b + 64, 2 * P + g * P:3 * P + g * P], self.vt[s][0:nk, g * HD:(g + 1) * HD],
                           self.pt[0:nk, n, :], start=True, stop=True, skip_group_check=True)
        mm.then_inc(S("weighted"), 1)

    def tensor(self, pe, p, s, k):
        S = self.st.sem
        c, lo, nk = self.chunk(p, s)
        later = self.past_first_pair(p) or s == 1
        if k == 0 and later:
            self.weigh(pe, c - 1, 1 - s, CH if isinstance(c, int) and c == 1 else P)
        if k == 1:
            pe.wait_ge(S(f"chunk_in{s}"), (p - self.first) * 80 + 80)
            if later:
                pe.wait_ge(S("attended"), c)
            for g, b in self.UNITS:
                pe.matmul(self.banks[6 + b][:, g * P:g * P + nk], self.q[s][64 * b:64 * b + 64, 2 * g:2 * g + 2].rearrange("p n t -> p (n t)"),
                          self.k[s][64 * b:64 * b + 64, 0 if b == g else 1, 0:nk], start=True, stop=True, skip_group_check=True)
            pe.transpose(self.banks[6][0:nk, 2 * P:3 * P], self.v[s][:, 0:nk], self.ident).then_inc(S("scores"), 1)
        if k == KD - 1:
            pe.wait_ge(S("probs"), c + 1)
            for n in range(4):
                mm = pe.transpose(self.banks[6 + n // 2][0:nk, (n % 2) * P:(n % 2 + 1) * P], self.x[s][:, n, 0:nk], self.ident)
            mm.then_inc(S("probs_turned"), 1)

    def tensor_last(self, pe, p, s, k):
        if k == 0:
            self.weigh(pe, NCH - 1, 1, P)

    def scalar(self, act):
        S = self.st.sem

        def before(p, s):
            c, _, nk = self.chunk(p, s)
            if isinstance(c, int) and c == 0:
                return
            nk = CH if isinstance(c, int) and c == 1 else P
            act.wait_ge(S("probs_turned"), c)
            for half in range(2):
                act.copy(self.pt[0:nk, 2 * half:2 * half + 2], self.banks[6 + half][0:nk, 0:2 * P].rearrange("p (n t) -> p n t", n=2)).then_inc(S("probs_t"), 1)

        def store(c, s):
            act.wait_ge(S("attended"), c + 1)
            act.dma_start(self.io["branch"][1][:, :, bass.ds(c * CH, CH)], self.ob[s][:]).then_inc(S(f"slot_free{s}"), 16)

        def after(p, s):
            c, _, nk = self.chunk(p, s)
            if not (isinstance(c, int) and c == 0):
                store(c - 1, 1 - s)
            act.wait_ge(S("centred"), c + 1)
            if isinstance(c, int) and c == 0:
                act.activation(self.x[0][:, :, 0:nk], self.x[0][:, :, 0:nk], ACT.Exp).then_inc(S("exp_keys0"), 1)
                act.activation(self.x[0][:, :, P:P + 1], self.x[0][:, :, P:P + 1], ACT.Exp).then_inc(S("exp"), 1)
            else:
                act.activation(self.x[s][:], self.x[s][:], ACT.Exp).then_inc(S("exp"), 1)

        return Beside(self.first, self.end, (before, after), lambda: store(NCH - 1, 1))

    def put_sinks(self, dve):
        S = self.st.sem
        dve.memset(self.ob[1][:], 0.0).then_inc(S("slot_free1"), 16)
        dve.wait_ge(S("slot_free1"), 16)
        dve.wait_ge(S("sink_in"), 16)
        for n, (g, b) in enumerate(self.UNITS):
            for half in range(2):
                h = 4 * g + 2 * half + b
                dve.tensor_copy(self.sinkq[64 * half:64 * half + 64, n:n + 1], self.sink[64 * half:64 * half + 64, h:h + 1]).then_inc(S("sink_of_row"), 1)

    def vector(self, dve):
        S = self.st.sem

        def before(p, s):
            c, _, _ = self.chunk(p, s)
            if isinstance(c, int) and c == 0:
                return
            dve.wait_ge(S("weighted"), c)
            if not isinstance(c, int):
                dve.wait_ge(S(f"slot_free{1 - s}"), (p - self.first) * 16)
            elif c == 2 * (self.end - self.first):
                dve.wait_ge(S(f"slot_free{1 - s}"), 16 * (self.end - self.first))
            for g in range(2):
                o = dve.tensor_copy(self.ob[1 - s][:, 2 * g:2 * g + 2], self.banks[7][:, 2 * P + g * P:3 * P + g * P].rearrange("p (n t) -> p n t", n=2))
            o.then_inc(S("attended"), 1)

        def after(p, s):
            c, _, nk = self.chunk(p, s)
            x, z = self.x[s], self.stat[s]
            zero = isinstance(c, int) and c == 0
            dve.wait_ge(S("scores"), c + 1)
            if zero:
                dve.wait_ge(S("sink_of_row"), 8)
            for b in range(2):
                dve.tensor_scalar(x[:, b::2, 0:nk], self.banks[6 + b][:, 0:2 * P].rearrange("p (g k) -> p g k", g=2)[:, :, 0:nk],
                                  HD ** -0.5, None, ALU.mult).then_inc(S("scored"), 1)
            dve.tensor_copy(self.vt[s][0:nk, :], self.banks[6][0:nk, 2 * P:3 * P]).then_inc(S("v_turned"), 1)
            dve.tensor_copy(x[:, :, P], self.sinkq[:]).then_inc(S("scored"), 1)
            dve.wait_ge(S("scored"), c * 3 + 3)
            dve.wait_ge(S("v_turned"), c + 1)
            dve.tensor_reduce(z[:, 0], x[:, :, 0:nk], AX.X, ALU.max).then_inc(S("maxed"), 1)
            dve.wait_ge(S("maxed"), c * 2 + 1)
            dve.tensor_tensor(z[:, 0], z[:, 0], self.sinkq[:], ALU.max).then_inc(S("maxed"), 1)
            dve.wait_ge(S("maxed"), c * 2 + 2)
            m = z[:, 0].rearrange("p (n o) -> p n o", o=1)
            if zero:
                dve.tensor_tensor(x[:, :, P:P + 1], x[:, :, P:P + 1], m, ALU.subtract).then_inc(S("sink_centred0"), 1)
                dve.wait_ge(S("sink_centred0"), 1)
                dve.tensor_tensor(x[:, :, 0:nk], x[:, :, 0:nk], m.broadcast_to([P, 4, nk]), ALU.subtract).then_inc(S("centred"), 1)
                dve.wait_ge(S("exp_keys0"), 1)
            else:
                dve.tensor_tensor(x[:], x[:], m.broadcast_to([P, 4, P + 1]), ALU.subtract).then_inc(S("centred"), 1)
            dve.wait_ge(S("exp"), c + 1)
            dve.tensor_reduce(z[:, 1], x[:, :, 0:nk], AX.X, ALU.add).then_inc(S("norm_of_row"), 1)
            dve.wait_ge(S("norm_of_row"), c * 3 + 1)
            dve.tensor_tensor(z[:, 1], z[:, 1], x[:, :, P], ALU.add).then_inc(S("norm_of_row"), 1)
            dve.wait_ge(S("norm_of_row"), c * 3 + 2)
            dve.reciprocal(z[:, 2], z[:, 1]).then_inc(S("norm_of_row"), 1)
            dve.wait_ge(S("norm_of_row"), c * 3 + 3)
            dve.tensor_tensor(x[:, :, 0:nk], x[:, :, 0:nk], z[:, 2].rearrange("p (n o) -> p n o", o=1).broadcast_to([P, 4, nk]),
                              ALU.mult).then_inc(S("probs"), 1)

        return Beside(self.first, self.end, (before, after), lambda: None)


def stage_in_projection(nc, env, io):
    with Stage(nc, "inproj") as st:
        banks = st.banks()
        xt = st.sb("xt", [P, KD, T])
        xh, xl = st.sb("xh", [P, KD, T], F32R), st.sb("xl", [P, KD, T], F32R)
        out = [st.sb(f"z{s}", [P, T]) for s in range(2)]
        x_in = [st.sem(f"x_arrived{c}") for c in range(NTC)]
        vec_in = st.sem("constants_arrived")
        eps_set = st.sem("eps_set")
        stored = [st.sem(f"z_stored{s}") for s in range(2)]
        vec, masks = env["vec"], env["masks"]
        norm = Norm(st, "norm", xt, vec[:, VAT["norm_mix"]:], xh, xl, env["mask"]("ones"), banks)
        norm.eps = env["eps"]
        prod = Product(st, "win", KD, Z_N // 2, wtile(io["w_in"], KD), xh, xl, banks)
        windows = PromptWindows(st, env, io, banks, Z_G // 2)
        with nc.Block() as block:
            @block.sync
            def _(sp):
                sp.dma_start(vec[:], io["vec"]).then_inc(vec_in, 16)
                sp.dma_start(masks[:], io["masks"]).then_inc(vec_in, 16)
                for c in range(NTC):
                    sp.dma_start(xt[:, :, c * TC:(c + 1) * TC], io["xt"][:, :, c * TC:(c + 1) * TC]).then_inc(x_in[c], 16)
                    if c == 0:
                        prod.load_first(sp)
                windows.load_sinks(sp)
                windows_load = lambda p, s: windows.load(sp, p, s)
                prod.load_rest(sp, Beside(windows.first, windows.end, load=windows_load))
                for s in range(2):
                    sp.wait_ge(st.sem(f"slot_free{s}"), 16 * (NCH // 2 + s))

            @block.gpsimd
            def _(pool):
                pool.memset(env["eps"][:, 0:1], EPS).then_inc(eps_set, 1)
                pool.memset(env["eps"][:, 1:2], GN_EPS).then_inc(eps_set, 1)

            @block.scalar
            def _(act):
                act.wait_ge(eps_set, 2)
                norm.squares(act, x_in, prod)
                norm.roots(act)

                def evac(p, s):
                    if not (isinstance(p, int) and p == 0):
                        act.wait_ge(stored[s], p * 16)
                    for c in range(NTC):
                        act.wait_ge(prod.ready, (p * 2 + s) * NTC + (c + 1))
                        act.copy(out[s][:, c * TC:(c + 1) * TC], prod.bank[s][c][:, 0:TC]).then_inc(prod.used, 1)
                    act.wait_ge(prod.used, (p * 2 + (s + 1)) * NTC)
                    act.dma_start(io["z"][bass.ds(p * 2 + s, 1)].rearrange("o p t -> (o p) t"), out[s][:]).then_inc(stored[s], 16)
                prod.pipeline(act, prod.split_hi, evac, windows.scalar(act))
                for s in range(2):
                    act.wait_ge(stored[s], 16 * prod.pairs)

            @block.vector
            def _(dve):
                dve.wait_ge(vec_in, 32)
                prod.first_splits(dve, prod.split_lo)
                windows.put_sinks(dve)
                norm.vector(dve)
                prod.pipeline(dve, prod.split_lo, lambda p, s: None, windows.vector(dve))

            @block.tensor
            def _(pe):
                pe.wait_ge(vec_in, 32)
                norm.tensor(pe)
                prod.products(pe, norm.rest, True, windows)


def sample_windows(st, env, io, banks):
    q = st.sb("q", [P, 4, NB * NS])
    k2 = st.sb("k", [P, 2, T - SEQ + P])
    v = st.sb("v", [P, T - SEQ + P])
    sink = st.sb("sink", [P, NH])
    ob = st.sb("out", [P, 4, NB * NS])
    NK = NS + CH
    kc = st.sb("k_sample", [P, 2, NB, NK])
    vc = st.sb("v_sample", [NK, NB, P])
    qm = st.sb("q_masked", [P, 4, NB, P])
    ss = st.sb("scores_sample", [P, NH, NK + 1])
    sst = st.sb("stat_sample", [P, 3, NH])
    pts = st.sb("probs_t_sample", [NK, NH, P])
    ident = env["mask"]("ident")
    SC = HD ** -0.5
    zt = io["z"]
    S = lambda n: st.sem("windows_" + n)

    def load(eng):
        eng.dma_start(q[:], zt[Z_Q:Z_K, :, SEQ:T].rearrange("n p t -> p n t")).then_inc(S("qkv_in"), 16)
        eng.dma_start(k2[:, 0], zt[Z_K, :, SEQ - P:T]).then_inc(S("qkv_in"), 16)
        for b in range(2):
            eng.dma_start(k2[64 * b:64 * b + 64, 1], zt[Z_K, 64 - 64 * b:128 - 64 * b, SEQ - P:T]).then_inc(S("qkv_in"), 16)
        eng.dma_start(v[:], zt[Z_V, :, SEQ - P:T]).then_inc(S("qkv_in"), 16)
        eng.dma_start(sink[:], io["sink"].broadcast_to([P, NH])).then_inc(S("qkv_in"), 16)
        eng.dma_start(kc[:, :, :, NS:NK], io["swa_k"]).then_inc(S("cache_in"), 16)
        eng.dma_start(vc[NS:NK], io["swa_v"]).then_inc(S("cache_in"), 16)
        eng.dma_start(io["o_swa_kept"], io["swa_cache"]).then_inc(S("stored"), 16)
        eng.wait_ge(S("qkv_in"), 16 * 6)
        eng.dma_start(io["o_swa_new"][0], k2[:, 0]).then_inc(S("stored"), 16)
        eng.dma_start(io["o_swa_new"][1], v[:]).then_inc(S("stored"), 16)

    def store(eng):
        eng.wait_ge(S("sample_out"), 2)
        eng.dma_start(io["branch"][1][:, :, SEQ:T], ob[:]).then_inc(S("stored"), 16)
        eng.wait_ge(S("stored"), 16 * 4)

    def gpsimd(pool):
        pool.memset(qm[:], 0.0).then_inc(S("q_zero"), 1)
        pool.wait_ge(S("q_zero"), 1)
        pool.wait_ge(S("qkv_in"), 16 * 6)
        for b in range(NB):
            pool.tensor_copy(qm[:, :, b, b * NS:(b + 1) * NS], q[:, :, b * NS:(b + 1) * NS]).then_inc(S("q_masked"), 1)
        for n in range(2):
            pool.tensor_copy(kc[:, n, :, 0:NS], k2[:, n, P:].rearrange("p (b s) -> p b s", b=NB)).then_inc(S("k_new"), 1)

    def tensor(pe):
        pe.wait_ge(S("qkv_in"), 16 * 6)
        pe.wait_ge(S("q_masked"), NB)
        pe.wait_ge(S("k_new"), 2)
        pe.wait_ge(S("cache_in"), 32)
        for h in range(NH):
            g, b = h // 4, h % 2
            for s in range(NB):
                mm = pe.matmul(banks[6 + b][:, (h // 2) * NK:(h // 2 + 1) * NK], qm[64 * b:64 * b + 64, h // 2, s, :],
                               kc[64 * b:64 * b + 64, 0 if b == g else 1, s, :], start=(s == 0), stop=(s == NB - 1),
                               skip_group_check=True)
        mm.then_inc(S("scores_sample"), 1)
        for s in range(NB):
            if s:
                pe.wait_ge(S("v_sample_copied"), s)
            pe.transpose(banks[2][0:NS, 0:P], v[:, P + s * NS:P + (s + 1) * NS], ident).then_inc(S("v_sample_turned"), 1)
        pe.wait_ge(S("probs_sample"), 1)
        for n in range(2):
            if n:
                pe.wait_ge(S("probs_t_sample"), n)
            for h in range(4 * n, 4 * n + 4):
                mm = pe.transpose(banks[3][0:NK, (h % 4) * P:(h % 4 + 1) * P], ss[:, h, 0:NK], ident)
            mm.then_inc(S("probs_turned_sample"), 1)
        pe.wait_ge(S("probs_t_sample"), 2)
        pe.wait_ge(S("v_sample_copied"), NB)
        for g in range(2):
            for b in range(2):
                for s in range(NB):
                    mm = pe.matmul(banks[4 + g][64 * b:64 * b + 64, s * 2 * NS:(s + 1) * 2 * NS], vc[:, s, g * HD:(g + 1) * HD],
                                   pts[:, 4 * g + b:4 * g + b + 3:2, s * NS:(s + 1) * NS],
                                   start=True, stop=True, skip_group_check=True)
        mm.then_inc(S("weighted_sample"), 1)

    def scalar(act):
        act.wait_ge(S("cache_in"), 32)
        for s in range(NB):
            act.wait_ge(S("v_sample_turned"), s + 1)
            act.copy(vc[0:NS, s, :], banks[2][0:NS, 0:P]).then_inc(S("v_sample_copied"), 1)
        act.wait_ge(S("centred_sample"), 1)
        act.activation(ss[:], ss[:], ACT.Exp).then_inc(S("exp_sample"), 1)
        for n in range(2):
            act.wait_ge(S("probs_turned_sample"), n + 1)
            act.copy(pts[:, 4 * n:4 * n + 4], banks[3][0:NK, :].rearrange("p (n t) -> p n t", n=4)).then_inc(S("probs_t_sample"), 1)

    def vector(dve):
        steps = [0]

        def link(ins):
            steps[0] += 1
            ins.then_inc(S("dve_step"), 1)
            dve.wait_ge(S("dve_step"), steps[0])
        dve.wait_ge(S("qkv_in"), 16 * 6)
        dve.wait_ge(S("scores_sample"), 1)
        for b in range(2):
            link(dve.tensor_scalar(ss[:, b::2, 0:NK], banks[6 + b][:, 0:4 * NK].rearrange("p (n k) -> p n k", n=4), SC, None, ALU.mult))
        link(dve.tensor_copy(ss[:, :, NK], sink[:]))
        link(dve.tensor_reduce(sst[:, 0], ss[:], AX.X, ALU.max))
        up = lambda x, n: x.rearrange("p (n o) -> p n o", o=1).broadcast_to([P, NH, n])
        dve.tensor_tensor(ss[:], ss[:], up(sst[:, 0], NK + 1), ALU.subtract).then_inc(S("centred_sample"), 1)

        def finish():
            dve.wait_ge(S("exp_sample"), 1)
            link(dve.tensor_reduce(sst[:, 1], ss[:], AX.X, ALU.add))
            link(dve.reciprocal(sst[:, 2], sst[:, 1]))
            dve.tensor_tensor(ss[:, :, 0:NK], ss[:, :, 0:NK], up(sst[:, 2], NK), ALU.mult).then_inc(S("probs_sample"), 1)

        def put_out():
            dve.wait_ge(S("weighted_sample"), 1)
            for g in range(2):
                dve.tensor_copy(ob[:, 2 * g:2 * g + 2].rearrange("p n (s t) -> p s n t", s=NB),
                                banks[4 + g][:, 0:NB * 2 * NS].rearrange("p (s n t) -> p s n t", s=NB, n=2)).then_inc(S("sample_out"), 1)
        return finish, put_out

    return load, store, gpsimd, tensor, scalar, vector


def stage_lru(nc, env, io):
    with Stage(nc, "lru") as st:
        banks = st.banks()
        PAD = 3 + SEQ + NB * (3 + NS)
        xp = st.sb("x_padded", [P, KM, PAD])
        ly = st.sb("gate_branch", [P, KM, T])
        xc, r, i_, a, m = (st.sb(n, [P, KM, T]) for n in ("conv", "r", "i", "a", "m"))
        gw = st.sb("gate_w", [P, 2, KM, P])
        h0, hl = st.sb("h0", [P, KM, NB]), st.sb("h_last", [P, KM, NB + 1])
        sp = st.sb("softplus", [P, 8, KM])
        S = st.sem
        V = lambda n, c: env["vec"][:, VAT[n] + c:VAT[n] + c + 1]
        prompt = lambda x, ct, k=0: x[:, ct, k:k + SEQ]
        samples = lambda x, ct: x[:, ct, SEQ:T].rearrange("p (b s) -> p b s", b=NB)
        padded = lambda ct: xp[:, ct, 3 + SEQ:PAD].rearrange("p (b s) -> p b s", b=NB)
        zt = io["z"]
        windows_load, windows_store, windows_gpsimd, windows_tensor, windows_scalar, windows_vector = sample_windows(st, env, io, banks)
        with nc.Block() as block:
            @block.sync
            def _(eng):
                for ct in range(KM):
                    eng.dma_start(xp[:, ct, 3:3 + SEQ], zt[Z_LX + ct, :, 0:SEQ]).then_inc(S(f"x_in{ct}"), 16)
                    eng.dma_start(padded(ct)[:, :, 3:], zt[Z_LX + ct, :, SEQ:T].rearrange("p (b s) -> p b s", b=NB)).then_inc(S(f"x_in{ct}"), 16)
                    eng.dma_start(padded(ct)[:, :, 0:3], io["lru_conv"][ct]).then_inc(S(f"x_in{ct}"), 16)
                eng.dma_start(gw[:], io["lru_gate_w"]).then_inc(S("gate_w_in"), 16)
                eng.dma_start(h0[:], io["lru_h"]).then_inc(S("h0_in"), 16)
                for ct in range(KM):
                    eng.dma_start(ly[:, ct], zt[Z_LY + ct]).then_inc(S(f"y_in{ct}"), 16)
                windows_load(eng)
                for ct in range(KM):
                    eng.wait_ge(S(f"x_in{ct}"), 48)
                    eng.dma_start(io["o_conv_p"][ct], xp[:, ct, SEQ:SEQ + 3]).then_inc(S("stored"), 16)
                    eng.dma_start(io["o_conv_s"][ct], padded(ct)[:, :, NS:NS + 3]).then_inc(S("stored"), 16)
                for ct in range(KM):
                    eng.wait_ge(S("branch_out"), ct + 1)
                    eng.dma_start(io["branch"][0, :, ct], ly[:, ct]).then_inc(S("stored"), 16)
                eng.wait_ge(S("h_last"), 2 * KM)
                eng.dma_start(io["o_h"], hl[:]).then_inc(S("stored"), 16)
                windows_store(eng)
                eng.wait_ge(S("stored"), 16 * (3 * KM + 1))

            @block.gpsimd
            def _(pool):
                pool.memset(xp[:, :, 0:3], 0.0).then_inc(S("padding_zero"), 1)
                windows_gpsimd(pool)
                for ct in range(KM):
                    pool.wait_ge(S("gate"), 6 * (ct + 1))
                    pool.tensor_tensor(xc[:, ct], xc[:, ct], i_[:, ct], ALU.mult).then_inc(S("gated_x"), 1)
                for ct in range(KM):
                    pool.wait_ge(S("scanned"), ct + 1)
                    pool.tensor_copy(hl[:, ct, 0:1], m[:, ct, SEQ - 1:SEQ]).then_inc(S("h_last"), 1)
                    pool.tensor_copy(hl[:, ct, 1:], samples(m, ct)[:, :, NS - 1]).then_inc(S("h_last"), 1)

            @block.scalar
            def _(act):
                lam = env["vec"][:, VAT["lru_lambda"]:VAT["lru_lambda"] + KM]
                act.activation(sp[:, 0], lam, ACT.Abs).then_inc(S("abs"), 1)
                act.wait_ge(S("abs"), 1)
                act.activation(sp[:, 1], sp[:, 0], ACT.Exp, scale=-1.0).then_inc(S("e"), 1)
                act.wait_ge(S("w"), 1)
                act.activation(sp[:, 3], sp[:, 2], ACT.Ln).then_inc(S("ln"), 1)
                for ct in range(KM):
                    for g, dst in ((0, r), (1, i_)):
                        for c in range(NTC):
                            n = (ct * 2 + g) * NTC + c
                            act.wait_ge(S("gated"), n + 1)
                            act.activation(dst[:, ct, c * TC:(c + 1) * TC], banks[n % 6][:, 0:TC], ACT.Sigmoid,
                                           bias=V("lru_gate_b", g * KM + ct)).then_inc(S("gate"), 1)
                act.wait_ge(S("rate"), 1)
                act.wait_ge(S("gate"), 6 * KM)
                for ct in range(KM):
                    act.activation(a[:, ct], r[:, ct], ACT.Exp, scale=sp[:, 6, ct:ct + 1]).then_inc(S("a"), 1)
                    act.activation(m[:, ct], r[:, ct], ACT.Tanh, scale=sp[:, 5, ct:ct + 1]).then_inc(S("tanh"), 1)
                for ct in range(KM):
                    act.wait_ge(S("square"), ct + 1)
                    act.activation(r[:, ct], m[:, ct], ACT.Sqrt).then_inc(S("mult"), 1)
                for ct in range(KM):
                    act.wait_ge(S(f"y_in{ct}"), 16)
                    act.activation(ly[:, ct], ly[:, ct], ACT.Gelu_apprx_tanh).then_inc(S("gelu"), 1)
                windows_scalar(act)

            @block.tensor
            def _(pe):
                pe.wait_ge(S("gate_w_in"), 16)
                for ct in range(KM):
                    pe.wait_ge(S("conv"), 2 * (ct + 1))
                    for g in range(2):
                        for c in range(NTC):
                            n = (ct * 2 + g) * NTC + c
                            if n >= 6:
                                pe.wait_ge(S("gate"), n - 5)
                            pe.matmul(banks[n % 6][:, 0:TC], gw[:, g, ct], xc[:, ct, c * TC:(c + 1) * TC],
                                      start=True, stop=True).then_inc(S("gated"), 1)
                pe.wait_ge(S("gate"), 6 * KM)
                windows_tensor(pe)

            @block.vector
            def _(dve):
                steps = [0]

                def link(ins):
                    steps[0] += 1
                    ins.then_inc(S("dve_step"), 1)
                    dve.wait_ge(S("dve_step"), steps[0])
                lam = env["vec"][:, VAT["lru_lambda"]:VAT["lru_lambda"] + KM]
                dve.wait_ge(S("e"), 1)
                dve.tensor_scalar(sp[:, 2], sp[:, 1], 1.0, None, ALU.add).then_inc(S("w"), 1)
                dve.wait_ge(S("w"), 1)
                link(dve.tensor_scalar(sp[:, 4], sp[:, 2], -1.0, None, ALU.add))
                link(dve.tensor_tensor(sp[:, 4], sp[:, 1], sp[:, 4], ALU.subtract))
                link(dve.reciprocal(sp[:, 5], sp[:, 2]))
                link(dve.tensor_tensor(sp[:, 4], sp[:, 4], sp[:, 5], ALU.mult))
                dve.wait_ge(S("ln"), 1)
                link(dve.tensor_tensor(sp[:, 4], sp[:, 4], sp[:, 3], ALU.add))
                link(dve.tensor_scalar(sp[:, 5], lam, -1.0, 0.0, ALU.mult, ALU.max))
                link(dve.tensor_tensor(sp[:, 4], sp[:, 4], sp[:, 5], ALU.add))
                link(dve.tensor_scalar(sp[:, 5], sp[:, 4], 8.0, None, ALU.mult))
                dve.tensor_scalar(sp[:, 6], sp[:, 4], -8.0, None, ALU.mult).then_inc(S("rate"), 1)
                dve.wait_ge(S("padding_zero"), 1)
                for ct in range(KM):
                    dve.wait_ge(S(f"x_in{ct}"), 48)
                    w = lambda k: V("lru_conv_w", k * KM + ct)
                    srcs = (lambda k: xp[:, ct, k:k + SEQ], lambda k: padded(ct)[:, :, k:k + NS])
                    for src, dst in zip(srcs, (prompt(xc, ct), samples(xc, ct))):
                        link(dve.tensor_scalar(dst, src(0), w(0), V("lru_conv_b", ct), ALU.mult, ALU.add))
                        link(dve.scalar_tensor_tensor(out=dst, in0=src(1), scalar=w(1), in1=dst, op0=ALU.mult, op1=ALU.add))
                        link(dve.scalar_tensor_tensor(out=dst, in0=src(2), scalar=w(2), in1=dst, op0=ALU.mult, op1=ALU.add))
                        dve.scalar_tensor_tensor(out=dst, in0=src(3), scalar=w(3), in1=dst, op0=ALU.mult, op1=ALU.add).then_inc(S("conv"), 1)
                for ct in range(KM):
                    dve.wait_ge(S("tanh"), ct + 1)
                    dve.wait_ge(S("a"), ct + 1)
                    link(dve.tensor_tensor(r[:, ct], a[:, ct], a[:, ct], ALU.mult))
                    dve.scalar_tensor_tensor(out=m[:, ct], in0=r[:, ct], scalar=1.0, in1=m[:, ct],
                                             op0=ALU.add, op1=ALU.mult).then_inc(S("square"), 1)
                dve.wait_ge(S("h0_in"), 16)
                for ct in range(KM):
                    if ct == KM - 2:
                        normalise_windows, put_windows_out = windows_vector(dve)
                    if ct == KM - 1:
                        normalise_windows()
                    dve.wait_ge(S("gated_x"), ct + 1)
                    dve.wait_ge(S("mult"), ct + 1)
                    link(dve.tensor_tensor(xc[:, ct], xc[:, ct], r[:, ct], ALU.mult))
                    dve.wait_ge(S("a"), ct + 1)
                    link(dve.tensor_tensor(h0[:, ct], h0[:, ct], samples(a, ct)[:, :, 0], ALU.mult))
                    link(dve.tensor_tensor(samples(xc, ct)[:, :, 0], samples(xc, ct)[:, :, 0], h0[:, ct], ALU.add))
                    link(dve.memset(samples(a, ct)[:, :, 0], 0.0))
                    dve.tensor_tensor_scan(m[:, ct], a[:, ct], xc[:, ct], 0.0, ALU.mult, ALU.add).then_inc(S("scanned"), 1)
                    dve.wait_ge(S("scanned"), ct + 1)
                    dve.wait_ge(S("gelu"), ct + 1)
                    dve.tensor_tensor(ly[:, ct], ly[:, ct], m[:, ct], ALU.mult).then_inc(S("branch_out"), 1)
                put_windows_out()


def stage_rwkv(nc, env, io):
    with Stage(nc, "rwkv") as st:
        banks = st.banks()
        W4 = KM * P
        t4 = [P, KM, P]
        z = [st.sb(f"z{i}", [P, NRW, P + 1]) for i in range(2)]
        HR = NRW // 2
        dz = st.sb("z_difference", [P, HR, P])
        shift = st.sb("shift_state", [P, NRW, NB])
        zlast = st.sb("z_last", [P, NRW, NB + 1])
        w2, a2, g2 = (st.sb(n, [P, MIX]) for n in ("w2", "a2", "g2"))
        wl, gl = st.sb("tanh_w_and_a", [P, P]), st.sb("sig_g", [P, P])
        names = ["sw", "asig", "c", "cprev", "Pi", "kk", "sq", "B", "K", "kh", "rk"]
        (sw, asig, c_, cprev, Pi, kk, sq, B, K, kh, rk) = (st.sb(n, t4) for n in names)
        Pp, Pv, nrm = c_, cprev, sq
        two = lambda name, shape: [st.sb(f"{name}_{i}", shape) for i in range(2)]
        three = lambda name, shape: [st.sb(f"{name}_{i}", shape) for i in range(3)]
        AR = three("AR", [P, KM, 2, P])
        Bt, Kt, Vt = (three(n, [P, W4]) for n in ("B_tok", "K_tok", "V_tok"))
        GO, BO = ([st.sb(f"{name}_{i}", t4) for i in range(4)] for name in ("gate", "bonus"))
        pend = three("decay_end", [P, KM, 2])
        Z1 = two("LakV", [P, W4])
        MrbT, MrkT, TiT = ([two(f"{n}{i}", t4) for i in range(2)] for n in ("MrbT", "MrkT", "TT"))
        Bs, Ks = two("B_side", t4), two("K_side", t4)
        OT = two("o", t4)
        L, Ti, O_, Zm, LakT = (two(n, t4) for n in ("L", "T", "O", "Z", "LakT"))
        Pcm = st.sb("decay_diag", t4)
        X, U = st.sb("X", [P, W4]), st.sb("U", [P, W4])
        dev2 = dev = st.sb("dev", t4)
        Sbd, Stmp = st.sb("state", t4), st.sb("state_sum", t4)
        S0bd, S0c = st.sb("state0_diag", [P, NB, KM, P]), st.sb("state0", [P, KM, NB, HD])
        X0T, O0 = Zm
        Um = S0bd[:].rearrange("p b k v -> p b (k v)")
        S = st.sem
        mask, vec = env["mask"], env["vec"]
        ident, head = mask("ident"), mask("head")
        vb = lambda n, k, cols=P, k0=0: vec[:, VAT[n] + k0:VAT[n] + k0 + k].rearrange("p (k o) -> p k o", o=1).broadcast_to([P, k, cols])
        vb1 = lambda n, k: vec[:, VAT[n] + k:VAT[n] + k + 1]
        mb = lambda n, k=KM: mask(n).rearrange("p (o t) -> p o t", o=1).broadcast_to([P, k, P])
        bank4 = lambda i: banks[i][:].rearrange("p (n t) -> p n t", n=KM)
        flat = lambda x: x.rearrange("p n t -> p (n t)")
        zt = io["z"]
        rows = lambda s: slice(64 * s, 64 * s + 64)
        heads = [(p, s, slice((2 * p + s) * HD, (2 * p + s + 1) * HD), slice(p * P, (p + 1) * P)) for p in range(KM) for s in range(2)]
        LAST = TT - 1
        SBANK = (0, 1, 4, 5)
        PREP = 6
        from_start = lambda p: banks[3 + p // 2][:, (p % 2) * 2 * P:(p % 2 + 1) * 2 * P].rearrange("p (w t) -> p w t", w=2)
        zs = lambda u: z[u % 2][:, :, 1:P + 1]
        ROUNDS = range(-1, TT + 2)
        is_tile = lambda i: 0 <= i < TT

        def levels(t):
            return [n for n in (4, 8, 16, 32, 64) if n <= (CH if t < LAST else NS)] if is_tile(t) else []
        merges = [sum(len(levels(u)) for u in range(t)) for t in range(TT + 1)]
        written = lambda t: sum(4 * len(levels(u)) + 2 for u in range(t))

        with nc.Block() as block:
            @block.sync
            def _(eng):
                def load_z(u):
                    lo = u * P
                    first = 1 if u in (0, LAST) else 0
                    eng.dma_start(z[u % 2][:, :, first:P + 1], zt[Z_RW:Z_G, :, lo - 1 + first:lo + P].rearrange("n p t -> p n t")).then_inc(S(f"z_in{u % 2}"), 16)

                def store_branch(n):
                    eng.wait_ge(S("branch_out"), n + 1)
                    eng.dma_start(io["branch"][2, :, :, n * P:(n + 1) * P], OT[n % 2][:]).then_inc(S(f"out_stored{n % 2}"), 16)

                load_z(0)
                load_z(1)
                eng.dma_start(w2[0:64, :], io["w2a2"][0:64]).then_inc(S("weights_in"), 16)
                eng.dma_start(a2[64:128, :], io["w2a2"][64:128]).then_inc(S("weights_in"), 16)
                eng.dma_start(g2[:], io["g2"]).then_inc(S("weights_in"), 16)
                eng.dma_start(shift[:], io["shift"]).then_inc(S("shift_in"), 16)
                eng.dma_start(S0bd[:], io["s0_diag"]).then_inc(S("state0_in"), 16)
                eng.dma_start(S0c[:], io["s0"]).then_inc(S("state0_in"), 16)
                for r in ROUNDS:
                    u, n = r + 1, r - 2
                    if is_tile(u + 2):
                        eng.wait_ge(S("lora_in"), 3 * u + 3)
                        eng.wait_ge(S("kh"), u + 1)
                        eng.wait_ge(S("rrk"), u + 1)
                        eng.wait_ge(S("AR"), 2 * u + 2)
                        eng.wait_ge(S("bonus_out"), u + 1)
                        eng.wait_ge(S("tok"), 3 * u + 1)
                        load_z(u + 2)
                    if is_tile(n):
                        store_branch(n)
                    if u == LAST:
                        eng.wait_ge(S("z_last"), 2)
                        eng.dma_start(io["o_shift"], zlast[:]).then_inc(S("stored"), 16)
                eng.wait_ge(S("state"), NCH)
                eng.dma_start(io["o_state_p"], Sbd[:]).then_inc(S("stored"), 16)
                eng.wait_ge(S("state_sample"), KM)
                eng.dma_start(io["o_state_s"], S0c[:]).then_inc(S("stored"), 16)
                eng.wait_ge(S("stored"), 16 * 3)
                for slot in range(2):
                    eng.wait_ge(S(f"out_stored{slot}"), 16 * ((TT + 1 - slot) // 2))

            @block.gpsimd
            def _(pool):
                tt = pool.tensor_tensor
                steps = [0]

                def link(ins):
                    steps[0] += 1
                    ins.then_inc(S("pool_step"), 1)
                    pool.wait_ge(S("pool_step"), steps[0])

                def shifted(u, h):
                    zz, f = z[u % 2], slice(h * HR, (h + 1) * HR)
                    if h == 0:
                        pool.wait_ge(S(f"z_in{u % 2}"), 16 * (u // 2 + 1))
                        if u == 0:
                            pool.wait_ge(S("z_start"), 1)
                        if u == LAST - 1:
                            pool.tensor_copy(zlast[:, :, 0:1], zz[:, :, P:P + 1]).then_inc(S("z_last"), 1)
                        if u == LAST:
                            pool.tensor_copy(zlast[:, :, 1:], zz[:, :, NS:P + 1:NS]).then_inc(S("z_last"), 1)
                        if u >= LAST - 1:
                            pool.wait_ge(S("z_last"), u - LAST + 2)
                    link(tt(dz[:], zz[:, f, 0:P], zz[:, f, 1:P + 1], ALU.subtract))
                    if u == LAST:
                        pool.wait_ge(S("shift_in"), 16)
                        link(tt(dz[:, :, 0:P:NS], shift[:, f], zz[:, f, 1:P + 1:NS], ALU.subtract))
                    link(tt(dz[:], dz[:], vb("rwkv_mu", HR, k0=h * HR), ALU.mult))
                    mixed = tt(zz[:, f, 1:P + 1], dz[:], zz[:, f, 1:P + 1], ALU.add)
                    mixed.then_inc(S("zs"), 1)
                    pool.wait_ge(S("zs"), 2 * u + h + 1)

                def decay_diag(b, c):
                    if b or c:
                        pool.wait_ge(S("state"), 2 * b + c)
                    pool.wait_ge(S("pend"), b + 1)
                    tt(Pcm[:], mb("head"), pend[b % 3][:, :, c:c + 1].broadcast_to(t4), ALU.mult).then_inc(S("decay_end"), 1)

                def off_blocks(t, i):
                    for s in range(2):
                        at = merges[t] + i
                        pool.wait_ge(S("L"), 2 * t + s + 1)
                        if at:
                            pool.wait_ge(S("Z"), 2 * (at - 1) + s + 1)
                        tt(O_[s][:], L[s][:], mb(f"off{levels(t)[i]}"), ALU.mult).then_inc(S("O"), 1)

                pool.memset(z[0][:, :, 0:1], 0.0).then_inc(S("z_start"), 1)
                shifted(0, 0)
                pool.wait_ge(S("zs"), 2)
                halves = [w2[64:128], a2[0:64]] + [x[s][rows(1 - s)] for x in (Ks, Bs) for s in range(2)]
                for i, x in enumerate(halves):
                    pool.memset(x, 0.0).then_inc(S("zeros"), 1)
                    pool.wait_ge(S("zeros"), i + 1)
                pool.memset(Sbd[:], 0.0).then_inc(S("state_zero"), 1)
                for r in range(-1, TT + 3):
                    t, u, b, last = r, r + 1, r - 1, r - 3
                    nl = len(levels(t))
                    serial = 0 <= b < LAST
                    if nl:
                        off_blocks(t, 0)
                    if is_tile(last):
                        o = OT[last % 2]
                        pool.wait_ge(S("affine"), KM * (last + 1))
                        pool.wait_ge(S("bonus_out"), last + 1)
                        pool.wait_ge(S("g"), last + 1)
                        link(tt(o[:], o[:], BO[last % 4][:], ALU.add))
                        tt(o[:], o[:], GO[last % 4][:], ALU.mult).then_inc(S("branch_out"), 1)
                    if serial:
                        decay_diag(b, 0)
                    if nl:
                        off_blocks(t, 1)
                    if is_tile(u):
                        if u:
                            pool.wait_ge(S("bonus"), u)
                        tt(rk[:], zs(u)[:, 0:KM], vb("rwkv_r_k", KM), ALU.mult).then_inc(S("rrk"), 1)
                        pool.wait_ge(S("rrk"), u + 1)
                        pool.wait_ge(S("kh"), u + 1)
                        tt(rk[:], rk[:], kh[:], ALU.mult).then_inc(S("rk"), 1)
                    if nl > 2:
                        off_blocks(t, 2)
                    if serial:
                        decay_diag(b, 1)
                    if u < LAST:
                        pool.wait_ge(S("P"), 3 * u + 2)
                        pool.tensor_copy(pend[u % 3][:], Pp[:, :, CH - 1:P:CH]).then_inc(S("pend"), 1)
                    if nl > 3:
                        off_blocks(t, 3)
                    if is_tile(u + 1):
                        shifted(u + 1, 0)
                    if nl > 4:
                        off_blocks(t, 4)
                    if is_tile(u + 1):
                        shifted(u + 1, 1)

            @block.scalar
            def _(act):
                def lora_inputs(u):
                    act.wait_ge(S("zs"), 2 * u + 2)
                    if u:
                        act.wait_ge(S("lora"), 3 * u)
                    act.activation(wl[0:64, :], zs(u)[0:64, 12, :], ACT.Tanh).then_inc(S("lora_in"), 1)
                    act.activation(gl[:], zs(u)[:, 13, :], ACT.Sigmoid).then_inc(S("lora_in"), 1)
                    act.copy(wl[64:128, :], zs(u)[64:128, 12, :]).then_inc(S("lora_in"), 1)

                def copy_u(b, c):
                    act.wait_ge(S("U"), 2 * b + c + 1)
                    act.copy(U[rows(c), :], banks[0][rows(c), :]).then_inc(S("U_copied"), 1)

                def copy_z(t, i):
                    for s in range(2):
                        act.wait_ge(S("Z"), 2 * (merges[t] + i) + s + 1)
                        act.copy(flat(Zm[s][:]), banks[2 + s][:]).then_inc(S("Z_copied"), 1)

                def copy_l(t, s):
                    act.wait_ge(S("grams"), 4 * t + 2 * s + 2)
                    act.copy(flat(L[s][:]), banks[2][:]).then_inc(S("L"), 1)

                def copy_tokens(u, n, dst):
                    act.wait_ge(S("tok"), 3 * u + n + 1)
                    if u >= 3:
                        act.wait_ge(S("O_sum"), u - 2)
                    act.copy(dst[u % 3][:], banks[PREP][:]).then_inc(S("tok_copied"), 1)

                def sides(src, dst, ready, u):
                    act.wait_ge(ready, u + 1)
                    if u:
                        act.wait_ge(S("grams"), 4 * u)
                    for s in range(2):
                        act.copy(dst[s][rows(s)], src[rows(s)]).then_inc(S("sides"), 1)

                def deviation2(n):
                    act.wait_ge(S("centred"), n + 1)
                    act.activation(dev2[:], OT[n % 2][:], ACT.Square).then_inc(S("dev2"), 1)

                def deviation(n):
                    act.wait_ge(S("var"), n + 1)
                    act.activation(flat(dev[:]), banks[1 if n < LAST else 2][:], ACT.Sqrt, scale=1.0 / HD,
                                   bias=env["eps"][:, 1:2]).then_inc(S("dev"), 1)

                act.wait_ge(S("zeros"), 6)
                for r in ROUNDS:
                    t, u, b, n = r, r + 1, r - 1, r - 2
                    nl, prep, serial, norm = len(levels(t)), is_tile(u), 0 <= b < LAST, is_tile(n)
                    if prep:
                        lora_inputs(u)
                    if nl:
                        copy_l(t, 0)
                    if norm:
                        deviation2(n)
                    if prep:
                        act.wait_ge(S("kk"), u + 1)
                        act.activation(sq[:], kk[:], ACT.Square).then_inc(S("sq"), 1)
                    if nl:
                        copy_l(t, 1)
                    if norm:
                        deviation(n)
                    if b == LAST:
                        act.wait_ge(S("X0T"), 1)
                        for half in range(2):
                            both = banks[3 + half][:].rearrange("p (n w t) -> p n w t", n=2, w=2)
                            for w, dst in enumerate((X0T, O0)):
                                act.copy(dst[:, 2 * half:2 * half + 2], both[:, :, w]).then_inc(S("X0T_copied"), 1)
                        act.wait_ge(S("U"), NCH + 1)
                        act.copy(U[:], banks[6][:]).then_inc(S("U_copied"), 1)
                    if nl:
                        copy_z(t, 0)
                    if serial:
                        copy_u(b, 0)
                    if prep:
                        act.wait_ge(S("wa"), 2 * u + 1)
                        act.activation(sw[:], sw[:], ACT.Sigmoid).then_inc(S("sw"), 1)
                        act.wait_ge(S("wa"), 2 * u + 2)
                        act.activation(asig[:], asig[:], ACT.Sigmoid).then_inc(S("asig"), 1)
                    if nl:
                        copy_z(t, 1)
                    if prep:
                        act.wait_ge(S("lora"), 3 * u + 3)
                        if u >= 4:
                            act.wait_ge(S("branch_out"), u - 3)
                        act.copy(GO[u % 4][:], bank4(PREP)).then_inc(S("g"), 1)
                        act.wait_ge(S("norm2"), u + 1)
                        act.activation(flat(nrm[:]), banks[PREP][:], ACT.Sqrt).then_inc(S("norm"), 1)
                        act.wait_ge(S("cprev"), u + 1)
                        if u:
                            act.wait_ge(S("B"), u)
                        act.activation(Pi[:], c_[:], ACT.Exp, scale=DEC).then_inc(S("P"), 1)
                        act.activation(Pp[:], c_[:], ACT.Exp, scale=-DEC).then_inc(S("P"), 1)
                        act.activation(Pv[:], cprev[:], ACT.Exp, scale=-DEC).then_inc(S("P"), 1)
                    if nl > 2:
                        copy_z(t, 2)
                    if prep:
                        copy_tokens(u, 0, Vt)
                    if nl > 3:
                        copy_z(t, 3)
                    if serial:
                        copy_u(b, 1)
                    if prep:
                        copy_tokens(u, 1, Kt)
                        sides(K, Ks, S("K"), u)
                    if nl > 4:
                        copy_z(t, 4)
                    if prep:
                        sides(B, Bs, S("B"), u)
                        copy_tokens(u, 2, Bt)
                    if serial:
                        act.wait_ge(S("O_sum"), b + 1)
                        if b >= 2:
                            act.wait_ge(S(f"out_stored{b % 2}"), 16 * (b // 2))
                        act.copy(OT[b % 2][:], bank4(7)).then_inc(S("o"), 1)
                    if norm:
                        act.wait_ge(S("normed"), n + 1)
                        for ct in range(KM):
                            o = OT[n % 2][:, ct]
                            act.activation(o, o, ACT.Identity, scale=vb1("rwkv_ln_w", ct), bias=vb1("rwkv_ln_b", ct)).then_inc(S("affine"), 1)

            @block.vector
            def _(dve):
                steps = [0]

                def link(ins):
                    steps[0] += 1
                    ins.then_inc(S("dve_step"), 1)
                    dve.wait_ge(S("dve_step"), steps[0])
                tt, stt = dve.tensor_tensor, dve.scalar_tensor_tensor

                def add_x(b, c):
                    dve.wait_ge(S("X"), 2 * b + c + 1)
                    tt(X[rows(c), :], banks[0][rows(c), :], Z1[b % 2][rows(c), :], ALU.add).then_inc(S("X_added"), 1)

                def new_state(b, c):
                    n = 2 * b + c
                    dve.wait_ge(S("S_update"), n + 1)
                    dve.wait_ge(S("decay_end"), n + 1)
                    if n == 0:
                        dve.wait_ge(S("state_zero"), 1)
                    link(tt(flat(Stmp[:]), banks[1][:], flat(Sbd[:]), ALU.add))
                    tt(Sbd[:], Stmp[:], Pcm[:], ALU.mult).then_inc(S("state"), 1)

                def merge(t, i):
                    TT_ = TiT[t % 2]
                    for s in range(2):
                        dve.wait_ge(S("merged"), 2 * (merges[t] + i) + s + 1)
                        tt(flat(TT_[s][:]), banks[4 + s][:], flat(TT_[s][:]), ALU.add).then_inc(S("T"), 1)
                        if i < len(levels(t)) - 1:
                            tt(flat(Ti[s][:]), banks[2 + s][:], flat(Ti[s][:]), ALU.add).then_inc(S("T"), 1)

                def masked(t, s):
                    up, q = "16" if t == LAST else "64", t % 2
                    half_of = lambda i: banks[i][:].rearrange("p (n w t) -> p n w t", n=2, w=2)
                    for half in range(2):
                        dve.wait_ge(S("grams"), 4 * t + 2 * s + half + 1)
                        b1, b2 = half_of(3 + half), half_of(5 + half)
                        two_ = slice(2 * half, 2 * half + 2)
                        tt(TiT[q][s][:, two_], b1[:, :, 0], mb("off2T", 2), ALU.mult).then_inc(S("masked"), 1)
                        tt(MrbT[q][s][:, two_], b1[:, :, 1], mb("upI" + up, 2), ALU.mult).then_inc(S("masked"), 1)
                        tt(LakT[s][:, two_], b2[:, :, 0], mb("upS" + up, 2), ALU.mult).then_inc(S("masked"), 1)
                        tt(MrkT[q][s][:, two_], b2[:, :, 1], mb("upI" + up, 2), ALU.mult).then_inc(S("masked"), 1)
                    dve.wait_ge(S("masked"), 16 * t + 8 * s + 8)
                    tt(TiT[q][s][:], TiT[q][s][:], mb("ident"), ALU.add).then_inc(S("T"), 1)
                    dve.wait_ge(S("L"), 2 * t + s + 1)
                    link(tt(Ti[s][:], L[s][:], mb("off2"), ALU.mult))
                    tt(Ti[s][:], Ti[s][:], mb("ident"), ALU.add).then_inc(S("T"), 1)

                def lora_part(u, part, dst, bias):
                    dve.wait_ge(S("lora"), 3 * u + part + 1)
                    tt(dst[:], bank4(PREP), vb(bias, KM), ALU.add).then_inc(S("wa"), 1)

                d = AR[2][:].rearrange("p k w t -> p (k w) t")[:, 0:HR]
                dve.wait_ge(S("z_in0"), 16)
                dve.wait_ge(S("z_start"), 1)
                link(tt(d, z[0][:, HR:NRW, 0:P], z[0][:, HR:NRW, 1:P + 1], ALU.subtract))
                link(tt(d, d, vb("rwkv_mu", HR, k0=HR), ALU.mult))
                tt(z[0][:, HR:NRW, 1:P + 1], d, z[0][:, HR:NRW, 1:P + 1], ALU.add).then_inc(S("zs"), 1)
                dve.wait_ge(S("weights_in"), 48)
                for r in ROUNDS:
                    t, u, b, n = r, r + 1, r - 1, r - 2
                    nl, prep, serial, norm = len(levels(t)), is_tile(u), 0 <= b < LAST, is_tile(n)
                    q3 = u % 3
                    sample = u == LAST
                    if prep:
                        rr, k, v = (zs(u)[:, 4 * i:4 * i + 4] for i in range(3))
                        dve.wait_ge(S("zs"), 2 * u + 2)
                        if u:
                            dve.wait_ge(S("B"), u)
                        tt(kk[:], k, vb("rwkv_k_k", KM), ALU.mult).then_inc(S("kk"), 1)
                    if norm:
                        o = OT[n % 2]
                        dve.wait_ge(S("mean"), n + 1)
                        stt(out=flat(o[:]), in0=banks[0 if n < LAST else 3][:], scalar=-1.0 / HD, in1=flat(o[:]),
                            op0=ALU.mult, op1=ALU.add).then_inc(S("centred"), 1)
                    if nl:
                        masked(t, 0)
                    if serial:
                        add_x(b, 0)
                    if nl:
                        masked(t, 1)
                        dve.wait_ge(S("Z1"), t + 1)
                        dve.tensor_copy(Z1[t % 2][:], banks[PREP][:]).then_inc(S("Z1_copied"), 1)
                    if b == LAST:
                        dve.wait_ge(S("X"), NCH + 1)
                        tt(X[:], banks[4][:], Z1[b % 2][:], ALU.add).then_inc(S("X_added"), 1)
                        dve.wait_ge(S("U_copied"), NCH + 1)
                        for part, src in enumerate((U, Vt[b % 3])):
                            if part:
                                dve.wait_ge(S("S_update"), NCH + 1)
                            for s in range(NB):
                                dve.tensor_scalar(Um[:, s, :], src[:], env["sample_rows"][:, s:s + 1], None, ALU.mult).then_inc(S("row_masked"), 1)
                        dve.wait_ge(S("O_sum"), TT)
                        dve.wait_ge(S("X0T_copied"), 4)
                        dve.wait_ge(S(f"out_stored{b % 2}"), 16 * (b // 2))
                        tt(flat(OT[b % 2][:]), banks[7][:], flat(O0[:]), ALU.add).then_inc(S("o"), 1)
                        dve.wait_ge(S("S_update"), NCH + 2)
                        for ct in range(KM):
                            bk = banks[SBANK[ct]][:].rearrange("p (b v) -> p b v", b=NB)
                            link(tt(S0c[:, ct], S0c[:, ct], bk, ALU.add))
                            tt(S0c[:, ct], S0c[:, ct], Pp[:, ct, NS - 1:P:NS].rearrange("p (b o) -> p b o", o=1).broadcast_to([P, NB, HD]),
                               ALU.mult).then_inc(S("state_sample"), 1)
                    if prep:
                        lora_part(u, 0, sw, "rwkv_w0")
                    if nl:
                        merge(t, 0)
                    if prep:
                        lora_part(u, 1, asig, "rwkv_a0")
                        dve.wait_ge(S("sw"), u + 1)
                        if 0 < u:
                            dve.wait_ge(S("pend"), u)
                        link(dve.tensor_tensor_scan(flat(c_[:]), env["resets"][1 if sample else 0], flat(sw[:]), 0.0, ALU.mult, ALU.add))
                        tt(cprev[:], c_[:], sw[:], ALU.subtract).then_inc(S("cprev"), 1)
                    if serial:
                        new_state(b, 0)
                    if prep:
                        dve.wait_ge(S("asig"), u + 1)
                        if u:
                            dve.wait_ge(S("rk"), u)
                            dve.wait_ge(S("K"), u)
                        link(stt(out=kh[:], in0=asig[:], scalar=-1.0, in1=vb("rwkv_k_a", KM), op0=ALU.add, op1=ALU.mult))
                        stt(out=kh[:], in0=kh[:], scalar=1.0, in1=k, op0=ALU.add, op1=ALU.mult).then_inc(S("kh"), 1)
                    if nl:
                        merge(t, 1)
                    if serial:
                        add_x(b, 1)
                    if nl > 2:
                        merge(t, 2)
                    if prep:
                        dve.wait_ge(S("bonus"), u + 1)
                        if u >= 4:
                            dve.wait_ge(S("branch_out"), u - 3)
                        tt(BO[u % 4][:], bank4(PREP), v, ALU.mult).then_inc(S("bonus_out"), 1)
                        dve.wait_ge(S("P"), 3 * u + 3)
                        dve.wait_ge(S("kh"), u + 1)
                        if u:
                            dve.wait_ge(S("sides"), 4 * u)
                            dve.wait_ge(S("tok_copied"), 3 * u)
                        tt(K[:], kh[:], Pi[:], ALU.mult).then_inc(S("K"), 1)
                        if u >= 3:
                            dve.wait_ge(S("O_sum"), u - 2)
                        tt(AR[q3][:, :, 1, :], rr, Pp[:], ALU.mult).then_inc(S("AR"), 1)
                        dve.wait_ge(S("norm"), u + 1)
                        link(dve.tensor_scalar(nrm[:], nrm[:], 1e-12, None, ALU.max))
                        link(dve.reciprocal(nrm[:], nrm[:]))
                        dve.wait_ge(S("sq"), u + 1)
                        link(tt(kk[:], kk[:], nrm[:], ALU.mult))
                    if nl > 3:
                        merge(t, 3)
                    if prep:
                        stt(out=AR[q3][:, :, 0, :], in0=kk[:], scalar=-1.0, in1=Pv[:], op0=ALU.mult, op1=ALU.mult).then_inc(S("AR"), 1)
                        dve.wait_ge(S("AR"), 2 * u + 2)
                        link(tt(kk[:], kk[:], asig[:], ALU.mult))
                        tt(B[:], kk[:], Pi[:], ALU.mult).then_inc(S("B"), 1)
                    if serial:
                        new_state(b, 1)
                    if norm:
                        dve.wait_ge(S("dev"), n + 1)
                        link(dve.reciprocal(dev[:], dev[:]))
                        tt(o[:], o[:], dev[:], ALU.mult).then_inc(S("normed"), 1)
                    if nl > 4:
                        merge(t, 4)

            @block.tensor
            def _(pe):
                mm_ = lambda *a, **k: pe.matmul(*a, skip_group_check=True, **k)

                def lora(u, part, weight, x):
                    if part == 0:
                        pe.wait_ge(S("lora_in"), 3 * u + 3)
                        if u:
                            pe.wait_ge(S("Z1_copied"), u)
                    else:
                        pe.wait_ge(S("wa"), 2 * u + part)
                    for ct in range(KM):
                        cs = slice(ct * P, (ct + 1) * P)
                        mm = mm_(banks[PREP][:, cs], weight[:, cs], x[:], start=True, stop=True)
                    mm.then_inc(S("lora"), 1)

                def turn(src):
                    for ct in range(KM):
                        mm = pe.transpose(banks[PREP][:, ct * P:(ct + 1) * P], src[:, ct, :], ident)
                    mm.then_inc(S("tok"), 1)

                def from_state(b, c):
                    n, cc, rc, q = 2 * b + c, slice(c * CH, (c + 1) * CH), rows(c), b % 3
                    if n:
                        pe.wait_ge(S("state"), n)
                    else:
                        pe.wait_ge(S("state_zero"), 1)
                    if b and c == 0:
                        pe.wait_ge(S("U_copied"), n)
                    if b and c == 0:
                        pe.wait_ge(S("centred"), b)
                    for p in range(KM):
                        mm = mm_(banks[0][rc, p * P:(p + 1) * P], AR[q][:, p, 0, cc], Sbd[:, p, :], start=True, stop=True)
                    mm.then_inc(S("X"), 1)
                    if b and c == 0:
                        pe.wait_ge(S("o"), b)
                    for p in range(KM):
                        mm_(banks[7][:, p * P + c * CH:p * P + (c + 1) * CH], Sbd[:, p, :], AR[q][:, p, 1, cc],
                            start=(c == 0 and p == 0), stop=False)

                def solve(b, c):
                    n, cc, rc = 2 * b + c, slice(c * CH, (c + 1) * CH), rows(c)
                    pe.wait_ge(S("X_added"), n + 1)
                    for p, s, hs, _ in heads:
                        mm = mm_(banks[0][rc, hs], TiT[b % 2][s][rc, p, cc], X[rc, hs], start=True, stop=True)
                    mm.then_inc(S("U"), 1)

                def to_state(b, c):
                    n, rc, q = 2 * b + c, rows(c), b % 3
                    if n:
                        pe.wait_ge(S("state"), n)
                    if b and c == 0:
                        pe.wait_ge(S("dev"), b)
                    pe.wait_ge(S("U_copied"), n + 1)
                    for p in range(KM):
                        ps = slice(p * P, (p + 1) * P)
                        mm_(banks[1][:, ps], Bt[q][rc, ps], U[rc, ps], start=True, stop=False)
                        mm = mm_(banks[1][:, ps], Kt[q][rc, ps], Vt[q][rc, ps], start=False, stop=True)
                    mm.then_inc(S("S_update"), 1)

                def grams(t, s):
                    q = t % 3
                    if s:
                        pe.wait_ge(S("L"), 2 * t + 1)
                    for p in range(KM):
                        if s and p % 2 == 0:
                            pe.wait_ge(S("masked"), 16 * t + 2 * p + 4)
                        mm_(banks[2][:, p * P:(p + 1) * P], AR[q][:, p, 0, :], Bs[s][:, p, :], start=True, stop=True)
                        w = slice((p % 2) * 2 * P, (p % 2 + 1) * 2 * P)
                        ar = AR[q][:, p].rearrange("p w t -> p (w t)")
                        mm_(banks[3 + p // 2][:, w], Bs[s][:, p, :], ar, start=True, stop=True)
                        mm = mm_(banks[5 + p // 2][:, w], Ks[s][:, p, :], ar, start=True, stop=True)
                        if p % 2:
                            mm.then_inc(S("grams"), 1)

                def off_times_t(t, i):
                    for s in range(2):
                        pe.wait_ge(S("T"), written(t) + 4 * i + 2 * s + 2)
                        pe.wait_ge(S("O"), 2 * (merges[t] + i) + s + 1)
                        for p in range(KM):
                            mm = mm_(banks[2 + s][:, p * P:(p + 1) * P], O_[s][:, p, :], TiT[t % 2][s][:, p, :], start=True, stop=True)
                        mm.then_inc(S("Z"), 1)

                def merge(t, i):
                    for s in range(2):
                        pe.wait_ge(S("Z_copied"), 2 * (merges[t] + i) + s + 1)
                        for p in range(KM):
                            mm = mm_(banks[4 + s][:, p * P:(p + 1) * P], Ti[s][:, p, :], Zm[s][:, p, :], start=True, stop=True)
                            if i < len(levels(t)) - 1:
                                mm = mm_(banks[2 + s][:, p * P:(p + 1) * P], Zm[s][:, p, :], Ti[s][:, p, :], start=True, stop=True)
                        mm.then_inc(S("merged"), 1)

                def outputs(b, alone=False):
                    for p, s, hs, ps in heads:
                        mm_(banks[7][rows(s), ps], U[:, hs], MrbT[b % 2][s][:, p, :], start=alone, stop=False)
                        mm = mm_(banks[7][rows(s), ps], Vt[b % 3][:, hs], MrkT[b % 2][s][:, p, :], start=False, stop=True)
                    mm.then_inc(S("O_sum"), 1)

                def samples():
                    q = LAST % 3
                    pe.wait_ge(S("state0_in"), 32)
                    pe.wait_ge(S("o"), LAST)
                    pe.wait_ge(S("Z1_copied"), TT)
                    pe.wait_ge(S("T"), written(TT))
                    for p in range(KM):
                        for i in range(NB):
                            bc = slice(i * NS, (i + 1) * NS)
                            mm = mm_(from_start(p)[:, :, bc], S0bd[:, i, p, :], AR[q][:, p, :, bc], start=True, stop=True)
                    mm.then_inc(S("X0T"), 1)
                    pe.wait_ge(S("X0T_copied"), 4)
                    for p in range(KM):
                        mm = pe.transpose(banks[4][:, p * P:(p + 1) * P], X0T[:, p, :], ident)
                    mm.then_inc(S("X"), 1)
                    pe.wait_ge(S("X_added"), NCH + 1)
                    for p, s, hs, _ in heads:
                        mm = mm_(banks[6][:, hs], TiT[LAST % 2][s][:, p, :], X[:, hs], start=True, stop=True)
                    mm.then_inc(S("U"), 1)
                    pe.wait_ge(S("U_copied"), NCH + 1)
                    outputs(LAST, alone=True)
                    pe.wait_ge(S("centred"), LAST)
                    pe.wait_ge(S("dev"), LAST)
                    for part, tok in enumerate((Bt[q], Kt[q])):
                        pe.wait_ge(S("row_masked"), NB * (part + 1))
                        for p, s, hs, _ in heads:
                            mm = mm_(banks[SBANK[p]][rows(s), :], tok[:, hs], Um[:, :, hs], start=(part == 0), stop=(part == 1))
                        mm.then_inc(S("S_update"), 1)

                pe.wait_ge(S("weights_in"), 48)
                pe.wait_ge(S("zeros"), 6)
                for r in ROUNDS:
                    t, u, b, n = r, r + 1, r - 1, r - 2
                    nl, prep, serial, norm = len(levels(t)), is_tile(u), 0 <= b < LAST, is_tile(n)
                    if norm:
                        if n < LAST:
                            pe.wait_ge(S("U_copied"), 2 * n + 2)
                        pe.wait_ge(S("o"), n + 1)
                        mm_(banks[0 if n < LAST else 3][:], head, flat(OT[n % 2][:]), start=True, stop=True).then_inc(S("mean"), 1)
                    if nl:
                        pe.wait_ge(S("AR"), 2 * t + 2)
                        pe.wait_ge(S("sides"), 4 * t + 4)
                        pe.wait_ge(S("tok_copied"), 3 * t + 3)
                        if t:
                            pe.wait_ge(S("T"), written(t))
                        grams(t, 0)
                    if norm:
                        if n < LAST:
                            pe.wait_ge(S("state"), 2 * n + 2)
                        pe.wait_ge(S("dev2"), n + 1)
                        mm_(banks[1 if n < LAST else 2][:], head, flat(dev2[:]), start=True, stop=True).then_inc(S("var"), 1)
                    if serial:
                        from_state(b, 0)
                    if nl:
                        grams(t, 1)
                    if serial:
                        solve(b, 0)
                    if nl:
                        pe.wait_ge(S("masked"), 16 * t + 16)
                        pe.wait_ge(S("L"), 2 * t + 2)
                        for p, s, hs, _ in heads:
                            mm = mm_(banks[PREP][:, hs], LakT[s][:, p, :], Vt[t % 3][:, hs], start=True, stop=True)
                        mm.then_inc(S("Z1"), 1)
                    if b == LAST:
                        samples()
                    if nl:
                        off_times_t(t, 0)
                    if prep:
                        lora(u, 0, w2, wl)
                    if nl:
                        merge(t, 0)
                    if serial:
                        to_state(b, 0)
                    if prep:
                        lora(u, 1, a2, wl)
                    if nl:
                        off_times_t(t, 1)
                    if prep:
                        lora(u, 2, g2, gl)
                    if nl:
                        merge(t, 1)
                    if prep:
                        pe.wait_ge(S("sq"), u + 1)
                        pe.wait_ge(S("g"), u + 1)
                        mm_(banks[PREP][:], head, flat(sq[:]), start=True, stop=True).then_inc(S("norm2"), 1)
                    if serial:
                        from_state(b, 1)
                    if nl > 2:
                        off_times_t(t, 2)
                    if prep:
                        pe.wait_ge(S("rk"), u + 1)
                        pe.wait_ge(S("norm"), u + 1)
                        mm_(banks[PREP][:], head, flat(rk[:]), start=True, stop=True).then_inc(S("bonus"), 1)
                    if serial:
                        solve(b, 1)
                    if nl > 2:
                        merge(t, 2)
                    if nl > 3:
                        off_times_t(t, 3)
                    if prep:
                        pe.wait_ge(S("bonus_out"), u + 1)
                        turn(zs(u)[:, 8:12])
                    if nl > 3:
                        merge(t, 3)
                    if prep:
                        pe.wait_ge(S("K"), u + 1)
                        pe.wait_ge(S("tok_copied"), 3 * u + 1)
                        turn(K[:])
                    if serial:
                        to_state(b, 1)
                    if nl > 4:
                        off_times_t(t, 4)
                    if serial:
                        outputs(b)
                    if nl > 4:
                        merge(t, 4)
                    if prep:
                        pe.wait_ge(S("B"), u + 1)
                        pe.wait_ge(S("tok_copied"), 3 * u + 2)
                        turn(B[:])


class StreamSplit:

    SLOTS = 3

    def __init__(self, st, tag, src, xh, xl, n, ring):
        self.src, self.xh, self.xl, self.n, self.ring = src, xh, xl, n, ring
        self.arrived = [st.sem(f"{tag}_x_arrived{s}") for s in range(self.SLOTS)]
        self.rounded, self.rest = st.sem(f"{tag}_x_rounded"), st.sem(f"{tag}_x_rest")

    def load(self, eng):
        for k in range(self.n):
            if k >= self.SLOTS:
                eng.wait_ge(self.rest, k - self.SLOTS + 1)
            eng.dma_start(self.ring[:, k % self.SLOTS], self.src(k)).then_inc(self.arrived[k % self.SLOTS], 16)

    def scalar(self, act):
        for k in range(self.n):
            act.wait_ge(self.arrived[k % self.SLOTS], 16 * (k // self.SLOTS + 1))
            act.copy(self.xh[:, k], self.ring[:, k % self.SLOTS]).then_inc(self.rounded, 1)

    def vector(self, dve):
        for k in range(self.n):
            dve.wait_ge(self.rounded, k + 1)
            dve.tensor_tensor(self.xl[:, k], self.ring[:, k % self.SLOTS], self.xh[:, k].bitcast(F32), ALU.subtract).then_inc(self.rest, 1)


def add_to_residual(dve, prod, xt, added):
    def evac(p, s):
        for c in range(NTC):
            dve.wait_ge(prod.ready, (p * 2 + s) * NTC + (c + 1))
            row = xt[:, bass.ds(p * 2 + s, 1), c * TC:(c + 1) * TC].rearrange("p o t -> p (o t)")
            dve.tensor_tensor(row, prod.bank[s][c][:, 0:TC], row, ALU.add).then_inc(prod.used, 1)
    return evac


def stage_merge(nc, env, io):
    with Stage(nc, "merge") as st:
        banks = st.banks()
        S = st.sem
        ring = st.sb("branch", [P, 3, T])
        bh, bl = ([st.sb(f"branch_{part}{i}", [P, KM, T], F32R) for i in range(2)] for part in ("hi", "lo"))
        merged = st.sb("merged", [P, KD, T])
        gz = [st.sb(f"gate_z{s}", [P, T]) for s in range(2)]
        gs = [st.sb(f"gate{s}", [P, T]) for s in range(2)]
        tmp = st.sb("gated", [P, NTC, TC])
        bufs = Product.buffers(st, KM, "wb")
        prods = [Product(st, f"wb{n}", KM, KD // 2, wtile(io["w_branch"], KM, m0=KD * n), bh[n % 2], bl[n % 2], banks, bufs=bufs) for n in range(3)]
        splits = [StreamSplit(st, f"br{n}", lambda k, n=n: io["branch"][n, :, k], bh[n % 2], bl[n % 2], KM, ring) for n in range(3)]
        half = KD // 2
        with nc.Block() as block:
            @block.sync
            def _(sp):
                for n in range(3):
                    if n:
                        sp.wait_ge(prods[n - 1].rest, KD)
                    prods[n].load_first(sp)
                    if n == 0:
                        splits[0].load(sp)
                    if n < 2:
                        sp.wait_ge(splits[n].rest, KM)
                        splits[n + 1].load(sp)
                    prods[n].load_rest(sp)
                for m in range(KD):
                    sp.wait_ge(S("summed2"), (m + 1) * NTC)
                    sp.dma_start(io["merged"][:, m], merged[:, m]).then_inc(S("stored"), 16)
                sp.wait_ge(S("stored"), 16 * KD)

            @block.gpsimd
            def _(pool):
                for n in range(3):
                    def load(p, s, wait=True):
                        if wait:
                            pool.wait_ge(S(f"gate{n}"), p * 2 + (s - 1))
                        pool.dma_start(gz[s][:], io["z"][bass.ds(p * 2 + (Z_G + n * KD + s), 1)].rearrange("o p t -> (o p) t")).then_inc(S(f"gate_in{n}_{s}"), 16)
                    if n:
                        pool.wait_ge(S(f"gate{n - 1}"), KD)
                    load(0, 0, False)
                    load(0, 1, False)
                    with pool.Fori(1, half) as p:
                        load(p, 0)
                        load(p, 1)

            @block.scalar
            def _(act):
                for n in range(3):
                    if n:
                        act.wait_ge(prods[n - 1].ready, KD * NTC)
                    prods[n].first_splits(act, prods[n].split_hi)
                    if n == 0:
                        splits[0].scalar(act)
                    if n < 2:
                        splits[n + 1].scalar(act)

                    def gate(p, s):
                        act.wait_ge(S(f"gate_in{n}_{s}"), p * 16 + 16)
                        if not (isinstance(p, int) and p == 0):
                            act.wait_ge(prods[n].used, (p * 2 + (s - 1)) * NTC)
                        at = VAT["b_gate"] + n * KD
                        act.activation(gs[s][:], gz[s][:], ACT.Sigmoid, bias=env["vec"][:, bass.ds(p * 2 + (at + s), 1)]).then_inc(S(f"gate{n}"), 1)
                    if n:
                        act.wait_ge(prods[n - 1].used, KD * NTC)
                    prods[n].pipeline(act, prods[n].split_hi, gate)

            @block.vector
            def _(dve):
                for n in range(3):
                    prod = prods[n]
                    prod.first_splits(dve, prod.split_lo)
                    if n == 0:
                        splits[0].vector(dve)
                    if n < 2:
                        splits[n + 1].vector(dve)

                    def evac(p, s):
                        dve.wait_ge(S(f"gate{n}"), p * 2 + (s + 1))
                        if n and not (isinstance(p, int) and p == 0 and s == 0):
                            dve.wait_ge(S(f"summed{n}"), (p * 2 + s) * NTC)
                        elif n == 2:
                            dve.wait_ge(S("summed1"), KD * NTC)
                        for c in range(NTC):
                            cs = slice(c * TC, (c + 1) * TC)
                            row = merged[:, bass.ds(p * 2 + s, 1), cs].rearrange("p o t -> p (o t)")
                            dve.wait_ge(prod.ready, (p * 2 + s) * NTC + (c + 1))
                            if n == 0:
                                dve.tensor_tensor(row, prod.bank[s][c][:, 0:TC], gs[s][:, cs], ALU.mult).then_inc(prod.used, 1)
                            else:
                                dve.tensor_tensor(tmp[:, c, :], prod.bank[s][c][:, 0:TC], gs[s][:, cs], ALU.mult).then_inc(prod.used, 1)
                                dve.wait_ge(prod.used, (p * 2 + s) * NTC + (c + 1))
                                dve.tensor_tensor(row, tmp[:, c, :], row, ALU.add).then_inc(S(f"summed{n}"), 1)
                    prod.pipeline(dve, prod.split_lo, evac)
                    if n:
                        dve.wait_ge(S(f"summed{n}"), KD * NTC)
                    else:
                        dve.wait_ge(prod.used, KD * NTC)

            @block.tensor
            def _(pe):
                for n in range(3):
                    if n:
                        pe.wait_ge(prods[n - 1].used, KD * NTC)
                    prods[n].products(pe, splits[n].rest, False)




def stage_residual(nc, env, io, name, src, w, parts, load_x=False):
    with Stage(nc, name) as st:
        banks = st.banks()
        S = st.sem
        kt = max(n for _, n in parts)
        xt = env["xt"]
        ring = st.sb("x", [P, 3, T])
        xh, xl = st.sb("x_hi", [P, kt, T], F32R), st.sb("x_lo", [P, kt, T], F32R)
        bufs = Product.buffers(st, kt, "w")
        prods = [Product(st, f"w{i}", n, KD // 2, wtile(w, n, k0=k0), xh, xl, banks, bufs=bufs) for i, (k0, n) in enumerate(parts)]
        splits = [StreamSplit(st, f"x{i}", lambda k, k0=k0: src[:, k0 + k], xh, xl, n, ring) for i, (k0, n) in enumerate(parts)]
        whole = lambda eng, i: eng.wait_ge(prods[i].ready, KD * NTC)
        with nc.Block() as block:
            @block.sync
            def _(sp):
                for i, prod in enumerate(prods):
                    if i:
                        sp.wait_ge(splits[i - 1].rest, splits[i - 1].n)
                        sp.wait_ge(prods[i - 1].rest, KD)
                    prod.load_first(sp)
                    splits[i].load(sp)
                    if load_x and i == 0:
                        sp.dma_start(xt[:], io["xt"]).then_inc(S("residual_in"), 16)
                    prod.load_rest(sp)

            @block.scalar
            def _(act):
                for i, prod in enumerate(prods):
                    if i:
                        whole(act, i - 1)
                    prod.first_splits(act, prod.split_hi)
                    splits[i].scalar(act)
                    prod.pipeline(act, prod.split_hi, lambda p, s: None)

            @block.vector
            def _(dve):
                for i, prod in enumerate(prods):
                    prod.first_splits(dve, prod.split_lo)
                    splits[i].vector(dve)
                    if load_x and i == 0:
                        dve.wait_ge(S("residual_in"), 16)
                    if i:
                        dve.wait_ge(prods[i - 1].used, KD * NTC)
                    prod.pipeline(dve, prod.split_lo, add_to_residual(dve, prod, xt, None))

            @block.tensor
            def _(pe):
                for i, prod in enumerate(prods):
                    if i:
                        pe.wait_ge(prods[i - 1].used, KD * NTC)
                    prod.products(pe, splits[i].rest, False)


def stage_queries(nc, env, io):
    with Stage(nc, "xq") as st:
        banks = st.banks()
        S = st.sem
        xt, vec = env["xt"], env["vec"]
        xh, xl = st.sb("xh", [P, KD, T], F32R), st.sb("xl", [P, KD, T], F32R)
        mem = st.sb("mem", [P, KD, NMEM])
        out = [st.sb(f"q{s}", [P, T]) for s in range(2)]
        bufs, nbufs = Product.buffers(st, KD, "w"), Norm.buffers(st, "norm")
        ones = env["mask"]("ones")
        nx = Norm(st, "nx", xt, vec[:, VAT["norm_x"]:], xh, xl, ones, banks, bufs=nbufs)
        nm = Norm(st, "nm", mem, vec[:, VAT["norm_mem"]:], xh, xl, ones, banks, tc=NMEM, ntc=1, bufs=nbufs)
        nx.eps = nm.eps = env["eps"]
        pq = Product(st, "wq", KD, KD // 2, wtile(io["w_xq"], KD), xh, xl, banks, bufs=bufs)
        pm = Product(st, "wm", KD, KD, wtile(io["w_mem_kv"], KD), xh, xl, banks[6:8], tc=NMEM, ntc=1, bufs=bufs)
        kv = env["kv"]
        with nc.Block() as block:
            @block.sync
            def _(sp):
                sp.dma_start(mem[:], io["memt"]).then_inc(S("mem_in"), 16)
                pm.load(sp)
                sp.wait_ge(pm.rest, 2 * KD)
                pq.load_first(sp)
                sp.wait_ge(pm.used, 2 * KD)
                sp.dma_start(io["o_mem"], kv[:]).then_inc(S("kv_stored"), 16)
                pq.load_rest(sp)
                sp.wait_ge(S("kv_stored"), 16)

            @block.scalar
            def _(act):
                act.wait_ge(S("mem_in"), 16)
                pm.first_splits(act, pm.split_hi)
                nm.scalar(act)
                pm.pipeline(act, pm.split_hi, lambda p, s: None)
                act.wait_ge(pm.ready, 2 * KD)
                nx.squares(act, weights=pq)
                nx.roots(act)

                def evac(p, s):
                    if not (isinstance(p, int) and p == 0):
                        act.wait_ge(S(f"q_stored{s}"), p * 16)
                    for c in range(NTC):
                        act.wait_ge(pq.ready, (p * 2 + s) * NTC + (c + 1))
                        act.copy(out[s][:, c * TC:(c + 1) * TC], pq.bank[s][c][:, 0:TC]).then_inc(pq.used, 1)
                    act.wait_ge(pq.used, (p * 2 + (s + 1)) * NTC)
                    act.dma_start(io["q"][:, bass.ds(p * 2 + s, 1)].rearrange("p o t -> p (o t)"), out[s][:]).then_inc(S(f"q_stored{s}"), 16)
                pq.pipeline(act, pq.split_hi, evac)
                for s in range(2):
                    act.wait_ge(S(f"q_stored{s}"), 16 * pq.pairs)

            @block.vector
            def _(dve):
                pm.first_splits(dve, pm.split_lo)
                nm.vector(dve)

                def evac(p, s):
                    dve.wait_ge(pm.ready, p * 2 + (s + 1))
                    dve.tensor_copy(kv[:, bass.ds(p * 2 + s, 1)].rearrange("p o t -> p (o t)"), pm.bank[s][0][:, 0:NMEM]).then_inc(pm.used, 1)
                pm.pipeline(dve, pm.split_lo, evac)
                pq.first_splits(dve, pq.split_lo)
                nx.vector(dve)
                pq.pipeline(dve, pq.split_lo, lambda p, s: None)

            @block.tensor
            def _(pe):
                nm.tensor(pe)
                pm.products(pe, nm.rest, True)
                pe.wait_ge(nm.rooted, 1)
                nx.tensor(pe)
                pq.products(pe, nx.rest, True)


def stage_cross(nc, env, io):
    with Stage(nc, "cross") as st:
        banks = st.banks()
        S = st.sem
        kv, ident = env["kv"], env["mask"]("ident")
        q = st.sb("q", [P, KD, T])
        v = st.sb("v", [P, 2, D])
        s_ = [st.sb(f"scores{i}", [P, XH, NMEM]) for i in range(3)]
        stat = [st.sb(f"stat{i}", [P, 3, XH]) for i in range(2)]
        pt = st.sb("probs_t", [P, XH, 2, P])
        pts = st.sb("probs_t_samples", [P, XH, 2, P])
        o = [st.sb(f"out{i}", [P, KD, P]) for i in range(2)]
        qm = st.sb("q_masked", [P, KD, 2, P])
        ks = [st.sb(f"k_sample{i}", [P, KD, NMEM]) for i in range(2)]
        vs = [st.sb(f"v_sample{i}", [P, 2, D]) for i in range(2)]
        SC = XHD ** -0.5
        NT = TT - 1
        SAMPLES = NB // 2
        unit_tile = lambda u: None if u == SAMPLES else u - (u > SAMPLES)
        score_bank = lambda u: 6 if u == SAMPLES else 0
        b2 = lambda i: banks[i][:].rearrange("p (h m) -> p h m", h=2)
        dt_ = lambda i: banks[i][:].rearrange("p (n t) -> p n t", n=4)
        with nc.Block() as block:
            @block.sync
            def _(sp):
                def load_q(c):
                    cs = slice(c * TC, (c + 1) * TC)
                    sp.dma_start(q[:, :, cs], io["q"][:, :, cs]).then_inc(S(f"q_in{c}"), 16)

                def load(b, slots, used, name, src):
                    if b >= 2:
                        sp.wait_ge(S(used), b - 1)
                    sp.dma_start(slots[b % 2][:], src[b]).then_inc(S(f"{name}{b % 2}"), 16)
                keys = lambda b: load(b, ks, "k_used", "k_in", io["mem_k"])
                values = lambda b: load(b, vs, "v_used", "v_in", io["mem_v"])
                load_q(0)
                load_q(NTC - 1)
                for b in range(2):
                    keys(b)
                for c in range(1, NTC - 1):
                    load_q(c)
                for b in range(2):
                    values(b)
                for b in range(2, NB):
                    keys(b)
                for b in range(2, NB):
                    values(b)

            @block.gpsimd
            def _(pool):
                pool.wait_ge(S(f"q_in{NTC - 1}"), 16)
                for b in range(NB):
                    if b >= 2:
                        pool.wait_ge(S("k_used"), b - 1)
                    pool.memset(qm[:, :, b % 2], 0.0).then_inc(S("q_zero"), 1)
                    pool.wait_ge(S("q_zero"), b + 1)
                    pool.tensor_copy(qm[:, :, b % 2, b * NS:(b + 1) * NS], q[:, :, SEQ + b * NS:SEQ + (b + 1) * NS]).then_inc(S("q_masked"), 1)

            @block.tensor
            def _(pe):
                def tile_scores(u):
                    t = unit_tile(u)
                    pe.wait_ge(S(f"q_in{t * P // TC}"), 16)
                    if u:
                        pe.wait_ge(S("scored"), 2 * u)
                    for h in range(XH):
                        for d in range(2):
                            mm = pe.matmul(banks[h // 2][:, (h % 2) * NMEM:(h % 2 + 1) * NMEM], q[:, 2 * h + d, t * P:(t + 1) * P],
                                           kv[:, 2 * h + d, :], start=(d == 0), stop=(d == 1), skip_group_check=True)
                    mm.then_inc(S("scores"), 1)

                def sample_scores(b):
                    pe.wait_ge(S("q_masked"), b + 1)
                    pe.wait_ge(S(f"k_in{b % 2}"), 16 * (b // 2 + 1))
                    for h in range(XH):
                        for d in range(2):
                            first = b == 0 and d == 0
                            mm = pe.matmul(banks[6 + h // 2][:, (h % 2) * NMEM:(h % 2 + 1) * NMEM], qm[:, 2 * h + d, b % 2, :],
                                           ks[b % 2][:, 2 * h + d, :], start=(first and h % 2 == 0), stop=(b == NB - 1 and d == 1),
                                           skip_group_check=True)
                    mm.then_inc(S("k_used"), 1)

                def turn_probs(u):
                    pe.wait_ge(S("probs"), u + 1)
                    if u:
                        pe.wait_ge(S("probs_t"), 2 * u)
                    for h in range(XH):
                        for m in range(2):
                            mm = pe.transpose(banks[2 + h // 2][:, ((h % 2) * 2 + m) * P:((h % 2) * 2 + m + 1) * P],
                                              s_[u % 3][:, h, m * P:(m + 1) * P], ident)
                    mm.then_inc(S("probs_turned"), 1)

                def weigh(u):
                    t = unit_tile(u)
                    pe.wait_ge(S("probs_t"), 2 * (u + 1))
                    if t:
                        pe.wait_ge(S("out_copied"), 2 * t)
                    for f in range(KD):
                        for m in range(2):
                            mm = pe.matmul(banks[4 + f // 4][:, (f % 4) * P:(f % 4 + 1) * P], v[:, m, f * P:(f + 1) * P],
                                           pt[:, f // 2, m, :], start=(m == 0), stop=(m == 1), skip_group_check=True)
                    mm.then_inc(S("weighted"), 1)

                def weigh_sample(b):
                    if b == 0:
                        pe.wait_ge(S("scored"), 2 * SAMPLES + 2)
                        pe.wait_ge(S("probs_t"), 2 * SAMPLES + 2)
                    pe.wait_ge(S(f"v_in{b % 2}"), 16 * (b // 2 + 1))
                    for f in range(KD):
                        for m in range(2):
                            mm = pe.matmul(banks[6 + f // 4][:, (f % 4) * P + b * NS:(f % 4) * P + (b + 1) * NS],
                                           vs[b % 2][:, m, f * P:(f + 1) * P], pts[:, f // 2, m, b * NS:(b + 1) * NS],
                                           start=(m == 0), stop=(m == 1), skip_group_check=True)
                    mm.then_inc(S("v_used"), 1)

                for n in range(4):
                    if n >= 2:
                        pe.wait_ge(S("v_copied"), n - 1)
                    for j in range(4):
                        m, f = n // 2, (n % 2) * 4 + j
                        mm = pe.transpose(banks[6 + n % 2][:, j * P:(j + 1) * P], kv[:, KD + f, m * P:(m + 1) * P], ident)
                    mm.then_inc(S("v_turned"), 1)
                pe.wait_ge(S("v_copied"), 4)
                for i in range(TT + 2):
                    if i < TT and i != SAMPLES:
                        tile_scores(i)
                    if i < SAMPLES:
                        sample_scores(2 * i)
                        sample_scores(2 * i + 1)
                    u = i - 2
                    if u < 0:
                        continue
                    turn_probs(u)
                    if u != SAMPLES:
                        weigh(u)
                    if u > SAMPLES:
                        weigh_sample(2 * (u - SAMPLES - 1))
                        weigh_sample(2 * (u - SAMPLES - 1) + 1)

            @block.scalar
            def _(act):
                for n in range(4):
                    m, f = n // 2, (n % 2) * 512
                    act.wait_ge(S("v_turned"), n + 1)
                    act.copy(v[:, m, f:f + 512], banks[6 + n % 2][:]).then_inc(S("v_copied"), 1)
                def exponentials(i):
                    act.wait_ge(S("centred"), i + 1)
                    act.activation(s_[i % 3][:], s_[i % 3][:], ACT.Exp, scale=SC).then_inc(S("exp"), 1)

                for i in range(TT + 2):
                    if i < 2:
                        exponentials(i)
                        continue
                    u = i - 2
                    t = unit_tile(u)
                    act.wait_ge(S("probs_turned"), u + 1)
                    for n in range(2):
                        act.copy((pts if t is None else pt)[:, 2 * n:2 * n + 2].rearrange("p h m t -> p (h m t)"), banks[2 + n][:]).then_inc(S("probs_t"), 1)
                    if i < TT:
                        exponentials(i)
                    if t is None:
                        continue
                    act.wait_ge(S("weighted"), t + 1)
                    if t >= 2:
                        act.wait_ge(S(f"out_stored{t % 2}"), 16 * (t // 2))
                    for n in range(2):
                        act.copy(o[t % 2][:, 4 * n:4 * n + 4], dt_(4 + n)).then_inc(S("out_copied"), 1)
                    act.wait_ge(S("out_copied"), 2 * t + 2)
                    act.dma_start(io["xo"][:, :, t * P:(t + 1) * P], o[t % 2][:]).then_inc(S(f"out_stored{t % 2}"), 16)
                act.wait_ge(S("v_used"), NB)
                act.wait_ge(S("out_stored0"), 16 * (NT // 2))
                for n in range(2):
                    act.copy(o[0][:, 4 * n:4 * n + 4], dt_(6 + n)).then_inc(S("out_copied"), 1)
                act.wait_ge(S("out_copied"), 2 * TT)
                act.dma_start(io["xo"][:, :, SEQ:T], o[0][:]).then_inc(S("out_stored0"), 16)
                act.wait_ge(S("out_stored0"), 16 * 5)
                act.wait_ge(S("out_stored1"), 16 * 4)

            @block.vector
            def _(dve):
                steps = [0]

                def link(ins):
                    steps[0] += 1
                    ins.then_inc(S("dve_step"), 1)
                    dve.wait_ge(S("dve_step"), steps[0])
                up = lambda x: x.rearrange("p (h o) -> p h o", o=1).broadcast_to([P, XH, NMEM])

                def centre(t):
                    x, z = s_[t % 3], stat[t % 2]
                    if t >= 3:
                        dve.wait_ge(S("probs_turned"), t - 2)
                    bank = score_bank(t)
                    if t == SAMPLES:
                        dve.wait_ge(S("k_used"), NB)
                    else:
                        dve.wait_ge(S("scores"), unit_tile(t) + 1)
                    for n in range(2):
                        dve.tensor_reduce(z[:, 0, 2 * n:2 * n + 2], b2(bank + n), AX.X, ALU.max).then_inc(S("maxed"), 1)
                    dve.wait_ge(S("maxed"), 2 * t + 2)
                    for n in range(2):
                        m = z[:, 0, 2 * n:2 * n + 2].rearrange("p (h o) -> p h o", o=1).broadcast_to([P, 2, NMEM])
                        dve.tensor_tensor(x[:, 2 * n:2 * n + 2], b2(bank + n), m, ALU.subtract).then_inc(S("scored"), 1)
                    dve.wait_ge(S("scored"), 2 * t + 2)
                    dve.tensor_copy(z[:, 1], z[:, 0]).then_inc(S("centred"), 1)

                def normalise(t):
                    x, z = s_[t % 3], stat[t % 2]
                    dve.wait_ge(S("exp"), t + 1)
                    link(dve.tensor_reduce(z[:, 1], x[:], AX.X, ALU.add))
                    link(dve.reciprocal(z[:, 2], z[:, 1]))
                    dve.tensor_tensor(x[:], x[:], up(z[:, 2]), ALU.mult).then_inc(S("probs"), 1)

                for t in range(TT + 1):
                    if t < TT:
                        centre(t)
                    if t:
                        normalise(t - 1)


def stage_up(nc, env, io):
    with Stage(nc, "up") as st:
        banks = st.banks()
        S = st.sem
        xt, vec = env["xt"], env["vec"]
        xh, xl = st.sb("xh", [P, KD, T], F32R), st.sb("xl", [P, KD, T], F32R)
        PAD = 2 + SEQ + NB * (2 + NS)
        u = [st.sb(f"u{s}", [P, PAD]) for s in range(2)]
        y = [st.sb(f"y{s}", [P, T]) for s in range(2)]
        last = st.sb("last", [P, 2 * KF, 2 * (NB + 1)])
        state = st.sb("state", [P, 2 * KF, NB, 2])
        norm = Norm(st, "norm", xt, vec[:, VAT["norm_ffn"]:], xh, xl, env["mask"]("ones"), banks)
        norm.eps = env["eps"]
        w = io["w_up"]
        pair = lambda p, s: w[bass.ds(p + s * KF, 1)].rearrange("o p k m -> (o p) k m")
        prod = Product(st, "wup", KD, KF, pair, xh, xl, banks)
        prompt = lambda x: x[:, 0:SEQ]
        samples = lambda x: x[:, SEQ:T].rearrange("p (b s) -> p b s", b=NB)
        padded = lambda x: x[:, 2 + SEQ:PAD].rearrange("p (b s) -> p b s", b=NB)
        with nc.Block() as block:
            @block.sync
            def _(sp):
                sp.dma_start(state[:], io["ffn_state"]).then_inc(S("state_in"), 16)
                for s in range(2):
                    sp.dma_start(prod.raw[s][:], pair(0, s)).then_inc(prod.arrived[s], 16)

                def store(p):
                    sp.wait_ge(S("h"), p + 1)
                    sp.dma_start(io["h"][:, bass.ds(p, 1)].rearrange("p o t -> p (o t)"), y[0][:]).then_inc(S("h_stored"), 16)
                with sp.Fori(1, KF) as p:
                    for s in range(2):
                        sp.wait_ge(prod.rest, p * 2 + (s - 1))
                        sp.dma_start(prod.raw[s][:], pair(p, s)).then_inc(prod.arrived[s], 16)
                    store(p - 1)
                store(KF - 1)
                sp.wait_ge(S("h_stored"), 16 * KF)

            @block.gpsimd
            def _(pool):
                for s in range(2):
                    pool.memset(u[s][:, 0:2], 0.0).then_inc(S("padding_zero"), 1)
                pool.wait_ge(S("state_in"), 16)

                def put(p, s):
                    f = bass.ds(p + s * KF, 1)
                    if not (isinstance(p, int) and p == 0):
                        pool.wait_ge(S(f"conv{s}"), p * 2)
                        pool.wait_ge(S(f"last{s}"), p * 2)
                    pool.tensor_copy(padded(u[s])[:, :, 0:2], state[:, f].rearrange("p o b k -> p (o b) k")).then_inc(S(f"state_put{s}"), 1)
                    pool.wait_ge(S(f"u{s}"), p * 4 + 4)
                    pool.tensor_copy(last[:, f, 0:2].rearrange("p o k -> p (o k)"), u[s][:, SEQ:SEQ + 2]).then_inc(S(f"last{s}"), 1)
                    pool.tensor_copy(last[:, f, 2:].rearrange("p o (b k) -> p (o b) k", k=2), padded(u[s])[:, :, NS:NS + 2]).then_inc(S(f"last{s}"), 1)
                put(0, 0)
                put(0, 1)
                with pool.Fori(1, KF) as p:
                    put(p, 0)
                    put(p, 1)

            @block.scalar
            def _(act):
                norm.squares(act, weights=prod)
                norm.roots(act)

                def evac(p, s):
                    if not (isinstance(p, int) and p == 0):
                        act.wait_ge(S(f"conv{s}"), p * 2)
                        act.wait_ge(S(f"last{s}"), p * 2)
                    for c in range(NTC):
                        act.wait_ge(prod.ready, (p * 2 + s) * NTC + (c + 1))
                        n = TC if c < NTC - 1 else SEQ - c * TC
                        f = act.copy(u[s][:, 2 + c * TC:2 + c * TC + n], prod.bank[s][c][:, 0:n]).then_inc(S(f"u{s}"), 1)
                    act.copy(padded(u[s])[:, :, 2:], prod.bank[s][NTC - 1][:, TC - NB * NS:TC].rearrange("p (b s) -> p b s", b=NB)).then_inc(S(f"u{s}"), 1)
                    act.wait_ge(S(f"u{s}"), p * 4 + 4)
                    act.sem_inc(prod.used, NTC)
                    if s == 1:
                        act.wait_ge(S("conv0"), p * 2 + 2)
                        act.activation(y[0][:], y[0][:], ACT.Gelu_apprx_tanh).then_inc(S("gelu"), 1)
                prod.pipeline(act, prod.split_hi, evac)
                act.wait_ge(S("last0"), 2 * KF)
                act.wait_ge(S("last1"), 2 * KF)
                act.dma_start(io["o_ffn"], last[:]).then_inc(S("last_stored"), 16)
                act.wait_ge(S("last_stored"), 16)

            @block.vector
            def _(dve):
                prod.first_splits(dve, prod.split_lo)
                norm.vector(dve)
                dve.wait_ge(S("padding_zero"), 2)

                def evac(p, s):
                    dve.wait_ge(S(f"u{s}"), p * 4 + 4)
                    dve.wait_ge(S(f"state_put{s}"), p + 1)
                    tap = lambda k: vec[:, bass.ds(p + (VAT["ffn_conv_w"] + k * 2 * KF + s * KF), 1)]
                    if not (isinstance(p, int) and p == 0):
                        dve.wait_ge(S("h"), p)
                        dve.wait_ge(S("h_stored"), p * 16)
                    srcs = (lambda k: u[s][:, k:k + SEQ], lambda k: padded(u[s])[:, :, k:k + NS])
                    dsts = (prompt(y[s]), samples(y[s]))
                    for i, (src, dst) in enumerate(zip(srcs, dsts)):
                        dve.tensor_scalar(dst, src(0), tap(0), None, ALU.mult).then_inc(S(f"tap_a{s}"), 1)
                    dve.wait_ge(S(f"tap_a{s}"), p * 2 + 2)
                    for src, dst in zip(srcs, dsts):
                        dve.scalar_tensor_tensor(out=dst, in0=src(1), scalar=tap(1), in1=dst, op0=ALU.mult, op1=ALU.add).then_inc(S(f"tap_b{s}"), 1)
                    dve.wait_ge(S(f"tap_b{s}"), p * 2 + 2)
                    for src, dst in zip(srcs, dsts):
                        dve.scalar_tensor_tensor(out=dst, in0=src(2), scalar=tap(2), in1=dst, op0=ALU.mult, op1=ALU.add).then_inc(S(f"conv{s}"), 1)
                    if s == 1:
                        dve.wait_ge(S("gelu"), p + 1)
                        dve.wait_ge(S("conv1"), p * 2 + 2)
                        dve.tensor_tensor(y[0][:], y[0][:], y[1][:], ALU.mult).then_inc(S("h"), 1)
                prod.pipeline(dve, prod.split_lo, evac)

            @block.tensor
            def _(pe):
                norm.tensor(pe)
                prod.products(pe, norm.rest, True)


def stage_final(nc, env, io):
    with Stage(nc, "final") as st:
        banks = st.banks()
        S = st.sem
        y = st.sb("y", [P, KD, T])
        norm = Norm(st, "norm", env["xt"], env["vec"][:, VAT["norm_final"]:], None, y, env["mask"]("ones"), banks)
        norm.eps = env["eps"]
        with nc.Block() as block:
            @block.sync
            def _(sp):
                for c in range(NTC):
                    sp.wait_ge(norm.normed, KD * (c + 1))
                    cs = slice(c * TC, (c + 1) * TC)
                    sp.dma_start(io["y"][:, :, cs], y[:, :, cs]).then_inc(S("stored"), 16)
                sp.wait_ge(S("stored"), 16 * NTC)

            @block.scalar
            def _(act):
                norm.scalar(act)

            @block.vector
            def _(dve):
                norm.vector(dve)

            @block.tensor
            def _(pe):
                norm.tensor(pe)


OUTS = {"y": [P, KD, T], "o_conv_p": [KM, P, 3], "o_conv_s": [KM, P, NB, 3], "o_h": [P, KM, NB + 1],
        "o_swa_new": [2, P, P + NB * NS], "o_swa_kept": [2 * NB, (P - NS) * P], "o_shift": [P, NRW, NB + 1], "o_state_p": [P, KM, P], "o_state_s": [P, KM, NB, HD],
        "o_mem": [P, 2 * KD, NMEM], "o_ffn": [P, 2 * KF, 2 * (NB + 1)]}
SCRATCH = {"z": [Z_N, P, T], "branch": [3, P, KM, T], "merged": [P, KD, T], "q": [P, KD, T], "xo": [P, KD, T], "h": [P, KF, T]}


def hybrid_stream_step(nc, io, stages=99):
    for name, shape in SCRATCH.items():
        io[name] = nc.dram_tensor(f"scratch_{name}", shape, F32, kind="Internal").ap() if name not in io else io[name]
    with ExitStack() as ctx:
        sb = lambda n, s: ctx.enter_context(nc.sbuf_tensor(n, s, F32))
        vec, masks, eps = sb("vec", [P, NVEC]), sb("masks", [P, MW]), sb("eps", [P, 2])
        w = len(MASKS) * P
        env = {"vec": vec, "masks": masks, "eps": eps,
               "mask": lambda n: masks[:, MASKS.index(n) * P:(MASKS.index(n) + 1) * P],
               "resets": [masks[:, w + i * KM * P:w + (i + 1) * KM * P] for i in range(2)],
               "sample_rows": masks[:, w + 2 * KM * P:MW]}
        todo = [stage_in_projection, stage_lru, stage_rwkv, stage_merge]
        for stage in todo[:stages]:
            stage(nc, env, io)
        if stages < 6:
            return
        env["xt"] = sb("xt", [P, KD, T])
        stage_residual(nc, env, io, "out", io["merged"], io["w_out"], [(0, KD)], load_x=True)
        with nc.sbuf_tensor("mem_kv", [P, 2 * KD, NMEM], F32) as kv:
            env["kv"] = kv
            stage_queries(nc, env, io)
            stage_cross(nc, env, io)
        stage_residual(nc, env, io, "xo", io["xo"], io["w_xo"], [(0, KD)])
        stage_up(nc, env, io)
        stage_residual(nc, env, io, "down", io["h"], io["w_down"], [(0, KF // 2), (KF // 2, KF // 2)])
        stage_final(nc, env, io)


def lay_out(i):
    c = np.ascontiguousarray
    feat = lambda x: c(x.T.reshape(-1, P, x.shape[0]).transpose(1, 0, 2))
    tiles = lambda w: c(w.reshape(w.shape[0] // P, P, w.shape[1] // P, P).transpose(2, 1, 0, 3))
    one = {k: v[0] for k, v in i.items() if k not in ("x_prompt", "x_sample", "mem_prompt", "norm_final")}
    a = {"xt": feat(np.concatenate([i["x_prompt"].reshape(SEQ, D), i["x_sample"].reshape(NB * NS, D)])),
         "memt": feat(i["mem_prompt"].reshape(NMEM, D)), "masks": shape_masks()}
    vecs = {n: (i[n] if n == "norm_final" else one[n]).reshape(-1, P) for n, _ in VEC}
    a["vec"] = c(np.concatenate([vecs[n] for n, _ in VEC]).T)
    for n in ("w_in", "w_out", "w_xq", "w_mem_kv", "w_xo", "w_up", "w_down"):
        a[n] = tiles(one[n])
    a["w_branch"] = np.concatenate([tiles(w) for w in one["w_branch"]])
    gw = np.zeros((P, 2, KM, P), np.float32)
    for g in range(2):
        for h in range(NH):
            s = slice(64 * (h % 2), 64 * (h % 2) + 64)
            gw[s, g, h // 2, s] = one["lru_gate_w"][g, h]
    a["lru_gate_w"] = gw
    a["lru_conv"] = c(one["state_lru_conv"].reshape(NB, 3, KM, P).transpose(2, 3, 0, 1))
    a["lru_h"] = c(one["state_lru_h"].reshape(NB, KM, P).transpose(2, 1, 0))
    k = one["cache_swa_k"][:, CH:]
    two = [k.transpose(2, 3, 0, 1).reshape(P, NB, CH), k[:, :, ::-1].transpose(2, 3, 0, 1).reshape(P, NB, CH)]
    a["swa_k"] = c(np.stack(two, axis=1))
    a["swa_v"] = c(one["cache_swa_v"][:, CH:].transpose(1, 0, 2, 3).reshape(CH, NB, P))
    a["swa_cache"] = np.stack([one[n][:, NS:].reshape(NB, -1) for n in ("cache_swa_k", "cache_swa_v")]).reshape(2 * NB, -1)
    a["sink"] = one["swa_sink"].reshape(1, NH)
    a["w2a2"] = np.concatenate([one["rwkv_w2"], one["rwkv_a2"]])
    a["g2"] = one["rwkv_g2"]
    a["shift"] = c(one["state_rwkv_shift"].reshape(NB, NRW, P).transpose(2, 1, 0))
    s0 = one["state_rwkv"].reshape(NB, KM, 2, HD, HD).transpose(2, 4, 1, 0, 3)
    a["s0"] = c(s0.reshape(P, KM, NB, HD))
    diag = np.zeros((2, HD, NB, KM, 2, HD), np.float32)
    for s in range(2):
        diag[s, :, :, :, s] = s0[s].transpose(0, 2, 1, 3)
    a["s0_diag"] = diag.reshape(P, NB, KM, P)
    a["mem_k"] = c(one["cache_mem_k"].reshape(NB, NMEM, KD, P).transpose(0, 3, 2, 1))
    a["mem_v"] = c(one["cache_mem_v"].reshape(NB, 2, P, D).transpose(0, 2, 1, 3))
    a["ffn_state"] = c(one["state_ffn_conv"].reshape(NB, 2, 2 * KF, P).transpose(3, 2, 0, 1))
    return a


def hand_back(o):
    c = np.ascontiguousarray
    y = c(o["y"].transpose(2, 1, 0).reshape(T, D))
    conv_s = o["o_conv_s"].transpose(2, 3, 0, 1).reshape(1, NB, 3, MIX)
    conv_p = o["o_conv_p"].transpose(2, 0, 1).reshape(1, 1, 3, MIX)
    h = o["o_h"].transpose(2, 1, 0).reshape(NB + 1, MIX)
    new = o["o_swa_new"].transpose(0, 2, 1).reshape(2, P + NB * NS, 2, HD)
    swa_p = [c(n[:P].reshape(1, 1, P, 2, HD)) for n in new]
    kept = o["o_swa_kept"].reshape(2, 1, NB, P - NS, 2, HD)
    swa_s = [np.concatenate([old, n[P:].reshape(1, NB, NS, 2, HD)], axis=2) for old, n in zip(kept, new)]
    shift = o["o_shift"].transpose(2, 1, 0).reshape(NB + 1, 1, NRW * P)
    sp = o["o_state_p"].reshape(2, HD, KM, 2, HD)
    s_p = np.stack([sp[s, :, :, s] for s in range(2)]).transpose(2, 0, 3, 1).reshape(1, 1, NH, HD, HD)
    s_s = o["o_state_s"].reshape(2, HD, KM, NB, HD).transpose(3, 2, 0, 4, 1).reshape(1, NB, NH, HD, HD)
    ffn = o["o_ffn"].transpose(2, 1, 0).reshape(NB + 1, 2, 2 * FF)
    mem = o["o_mem"].transpose(2, 1, 0).reshape(NMEM, 2, XH, XHD)
    return (y[:SEQ].reshape(1, SEQ, D), y[SEQ:].reshape(NB, NS, D),
            c(conv_p), c(h[:1][None]), swa_p[0], swa_p[1], c(shift[:1][None]), c(s_p), c(ffn[:1][None]),
            c(mem[:, 0][None, None]), c(mem[:, 1][None, None]),
            c(conv_s), c(h[1:][None]), swa_s[0], swa_s[1], c(shift[1:][None]), c(s_s), c(ffn[1:][None]))


def kernel(**inputs):
    from concourse import bacc
    from concourse.bass_utils import run_bass_kernel_spmd

    nc = bacc.Bacc("TRN2", target_bir_lowering=False, num_devices=1)
    arrays = lay_out(inputs)
    io = {n: nc.dram_tensor(f"in_{n}", a.shape, mybir.dt.from_np(a.dtype), kind="ExternalInput").ap() for n, a in arrays.items()}
    io |= {n: nc.dram_tensor(f"out_{n}", s, F32, kind="ExternalOutput").ap() for n, s in OUTS.items()}
    hybrid_stream_step(nc, io)
    r = run_bass_kernel_spmd(nc, [{f"in_{n}": a for n, a in arrays.items()}], core_ids=[0])
    return hand_back({n: r.results[0][f"out_{n}"] for n in OUTS})
```
